# Optimizing a Trainium2 kernel written in Bass

```python
import math
import jax, jax.numpy as jnp
from jax import lax
import numpy as np
import jax
import jax.numpy as jnp

D_MODEL = 1024
BATCH = 1
SEQ = 256
DEPTH = 2

GROUP_WIDTH = D_MODEL // 4
N_GROUPS = 5
MIX_WIDTH = N_GROUPS * GROUP_WIDTH
POOL_WINDOWS = (2, 4, 8, 16)
POOL_CH = GROUP_WIDTH // len(POOL_WINDOWS)
CONV_WIDTH = 31
SHORT_CONV_WIDTH = 3
DIFF_HEADS = 4
DIFF_HEAD_DIM = GROUP_WIDTH // (2 * DIFF_HEADS)
MEM_HEADS = 4
MEM_HEAD_DIM = GROUP_WIDTH // MEM_HEADS
N_MEM = 256
Q_BLOCK = 128
PEER_HEADS = 8
PEER_N_KEYS = 128
PEER_N_EXPERTS = PEER_N_KEYS * PEER_N_KEYS
PEER_TOPK = 16
PEER_QUERY_DIM = 256
PEER_HALF = PEER_QUERY_DIM // 2
PEER_CHUNK = 128
EPS = 1e-6
IN_COLS = 10 * GROUP_WIDTH
IN_SPLITS = (GROUP_WIDTH, 3 * GROUP_WIDTH, 6 * GROUP_WIDTH, 9 * GROUP_WIDTH)


def rmsnorm(x, g):
    xf = x.astype(jnp.float32)
    xf = xf * lax.rsqrt(jnp.mean(xf * xf, axis=-1, keepdims=True) + EPS)
    return xf.astype(x.dtype) * g

def layernorm(x, g, b):
    xf = x.astype(jnp.float32)
    mu = jnp.mean(xf, axis=-1, keepdims=True)
    var = jnp.mean(jnp.square(xf - mu), axis=-1, keepdims=True)
    return ((xf - mu) * lax.rsqrt(var + EPS)).astype(x.dtype) * g + b

def depthwise_conv(x, w):
    k = w.shape[0]
    pad = k // 2
    return lax.conv_general_dilated(x, w[:, None, :].astype(x.dtype), (1,), [(pad, pad)],
                                    dimension_numbers=('NWC', 'WIO', 'NWC'),
                                    feature_group_count=x.shape[-1])

def alibi_slopes(n):
    return 2.0 ** (-8.0 * jnp.arange(1, n + 1, dtype=jnp.float32) / n)

def pool_mixer(u, w, scale):
    b, s, _ = u.shape
    cs = jnp.concatenate([jnp.zeros((b, 1, GROUP_WIDTH), jnp.float32),
                          jnp.cumsum(u.astype(jnp.float32), axis=1)], axis=1)
    t = jnp.arange(s)
    outs = []
    for gi, win in enumerate(POOL_WINDOWS):
        lo = jnp.clip(t - win // 2, 0, s)
        hi = jnp.clip(t + win // 2, 0, s)
        csg = cs[:, :, gi * POOL_CH:(gi + 1) * POOL_CH]
        outs.append((csg[:, hi] - csg[:, lo]) / (hi - lo).astype(jnp.float32)[None, :, None])
    pooled = jnp.concatenate(outs, axis=-1).astype(u.dtype) - u
    y = jnp.einsum('bsgc,gcd->bsgd', pooled.reshape(b, s, len(POOL_WINDOWS), POOL_CH), w)
    return y.reshape(b, s, GROUP_WIDTH) * scale

def conformer_conv(u, dw, ln_g, ln_b, pw):
    a, gate = jnp.split(u, 2, axis=-1)
    h = a * jax.nn.sigmoid(gate)
    h = depthwise_conv(h, dw)
    h = jax.nn.silu(layernorm(h, ln_g, ln_b))
    return h @ pw

def diff_attention(u, qk_g, lam_p, subln_g, layer_idx):
    b, s, _ = u.shape
    q, k, v = jnp.split(u, 3, axis=-1)
    q = rmsnorm(q.reshape(b, s, 2, DIFF_HEADS, DIFF_HEAD_DIM), qk_g[0])
    k = rmsnorm(k.reshape(b, s, 2, DIFF_HEADS, DIFF_HEAD_DIM), qk_g[1])
    v = v.reshape(b, s, DIFF_HEADS, 2 * DIFF_HEAD_DIM)
    lam_init = 0.8 - 0.6 * math.exp(-0.3 * layer_idx)
    lp = lam_p.astype(jnp.float32)
    lam = jnp.exp(jnp.sum(lp[0] * lp[1])) - jnp.exp(jnp.sum(lp[2] * lp[3])) + lam_init
    slopes = alibi_slopes(DIFF_HEADS)
    scale = DIFF_HEAD_DIM ** -0.5
    nb = s // Q_BLOCK
    qb = q.reshape(b, nb, Q_BLOCK, 2, DIFF_HEADS, DIFF_HEAD_DIM).transpose(1, 0, 2, 3, 4, 5)
    starts = jnp.arange(nb, dtype=jnp.int32) * Q_BLOCK
    kpos = jnp.arange(s, dtype=jnp.int32)

    def block(args):
        qblk, start = args
        sc = jnp.einsum('bqjhd,bkjhd->bjhqk', qblk, k).astype(jnp.float32) * scale
        qpos = start + jnp.arange(Q_BLOCK, dtype=jnp.int32)
        dist = jnp.abs(qpos[:, None] - kpos[None, :]).astype(jnp.float32)
        sc = sc - slopes[:, None, None] * dist
        p = jax.nn.softmax(sc, axis=-1)
        a = p[:, 0] - lam * p[:, 1]
        return jnp.einsum('bhqk,bkhe->bqhe', a.astype(v.dtype), v)

    o = lax.map(block, (qb, starts))
    o = o.transpose(1, 0, 2, 3, 4).reshape(b, s, DIFF_HEADS, 2 * DIFF_HEAD_DIM)
    o = rmsnorm(o, subln_g) * (1.0 - lam_init)
    return o.reshape(b, s, GROUP_WIDTH)

def short_conv(u, w):
    h, bg, cg = jnp.split(u, 3, axis=-1)
    return bg * depthwise_conv(cg * h, w)

def memory_attention(u, mem, mem_g, w_kv, qk_g):
    b, s, _ = u.shape
    m = mem.shape[1]
    kv = rmsnorm(mem, mem_g) @ w_kv
    k, v = jnp.split(kv, 2, axis=-1)
    q = rmsnorm(u.reshape(b, s, MEM_HEADS, MEM_HEAD_DIM), qk_g[0])
    k = rmsnorm(k.reshape(b, m, MEM_HEADS, MEM_HEAD_DIM), qk_g[1])
    v = v.reshape(b, m, MEM_HEADS, MEM_HEAD_DIM)
    sc = jnp.einsum('bshd,bmhd->bhsm', q, k).astype(jnp.float32) * (MEM_HEAD_DIM ** -0.5)
    p = jax.nn.softmax(sc, axis=-1).astype(v.dtype)
    return jnp.einsum('bhsm,bmhe->bshe', p, v).reshape(b, s, GROUP_WIDTH)

def peer_ffn(xn, wq, subkeys, u_tab, v_tab):
    b, s, d = xn.shape
    q = (xn @ wq).reshape(b, s, PEER_HEADS, 2, PEER_HALF)
    sc = jnp.einsum('bshjc,hjkc->bshjk', q, subkeys).astype(jnp.float32)
    top_s, top_i = lax.top_k(sc, PEER_TOPK)
    cand = (top_s[..., 0, :, None] + top_s[..., 1, None, :]).reshape(b, s, PEER_HEADS, PEER_TOPK * PEER_TOPK)
    best, ci = lax.top_k(cand, PEER_TOPK)
    i1 = jnp.take_along_axis(top_i[..., 0, :], ci // PEER_TOPK, axis=-1)
    i2 = jnp.take_along_axis(top_i[..., 1, :], ci % PEER_TOPK, axis=-1)
    idx = i1 * PEER_N_KEYS + i2
    g = jax.nn.softmax(best, axis=-1)
    t = b * s
    nc = t // PEER_CHUNK
    idx_c = idx.reshape(nc, PEER_CHUNK, PEER_HEADS * PEER_TOPK)
    g_c = g.reshape(nc, PEER_CHUNK, PEER_HEADS * PEER_TOPK)
    x_c = xn.reshape(nc, PEER_CHUNK, d)

    def chunk(args):
        ic, gc, xc = args
        act = jax.nn.gelu(jnp.einsum('ckd,cd->ck', u_tab[ic], xc), approximate=False)
        return jnp.einsum('ck,ckd->cd', (gc * act).astype(v_tab.dtype), v_tab[ic])

    return lax.map(chunk, (idx_c, g_c, x_c)).reshape(b, s, d)

def first_inputs(seed: int = 0) -> dict:
    key = jax.random.key(seed)
    ks = jax.random.split(key, 24)
    f32 = jnp.float32
    nrm = lambda k, shape, sc: jax.random.normal(k, shape, f32) * sc
    gain = lambda k, shape: 1.0 + 0.02 * jax.random.normal(k, shape, f32)
    L = DEPTH
    return {
        'x': nrm(ks[0], (BATCH, SEQ, D_MODEL), 1.0),
        'mem': nrm(ks[1], (BATCH, N_MEM, D_MODEL), 1.0),
        'norm_mix': gain(ks[2], (L, D_MODEL)),
        'w_in': nrm(ks[3], (L, D_MODEL, IN_COLS), D_MODEL ** -0.5),
        'pool_w': nrm(ks[4], (L, len(POOL_WINDOWS), POOL_CH, POOL_CH), POOL_CH ** -0.5),
        'pool_scale': 1.0 + 0.1 * jax.random.normal(ks[5], (L, GROUP_WIDTH), f32),
        'conv_dw': nrm(ks[6], (L, CONV_WIDTH, GROUP_WIDTH), CONV_WIDTH ** -0.5),
        'conv_ln_g': gain(ks[7], (L, GROUP_WIDTH)),
        'conv_ln_b': nrm(ks[8], (L, GROUP_WIDTH), 0.02),
        'conv_pw': nrm(ks[9], (L, GROUP_WIDTH, GROUP_WIDTH), GROUP_WIDTH ** -0.5),
        'diff_qk_norm': gain(ks[10], (L, 2, DIFF_HEAD_DIM)),
        'diff_lambda': nrm(ks[11], (L, 4, DIFF_HEAD_DIM), 0.1),
        'diff_subln': gain(ks[12], (L, 2 * DIFF_HEAD_DIM)),
        'sconv_w': nrm(ks[13], (L, SHORT_CONV_WIDTH, GROUP_WIDTH), SHORT_CONV_WIDTH ** -0.5),
        'mem_norm': gain(ks[14], (L, D_MODEL)),
        'w_mem_kv': nrm(ks[15], (L, D_MODEL, 2 * GROUP_WIDTH), D_MODEL ** -0.5),
        'mem_qk_norm': gain(ks[16], (L, 2, MEM_HEAD_DIM)),
        'group_norm': gain(ks[17], (L, MIX_WIDTH)),
        'w_out': nrm(ks[18], (L, MIX_WIDTH, D_MODEL), MIX_WIDTH ** -0.5),
        'norm_ffn': gain(ks[19], (L, D_MODEL)),
        'peer_wq': nrm(ks[20], (L, D_MODEL, PEER_HEADS * PEER_QUERY_DIM), D_MODEL ** -0.5),
        'peer_subkeys': nrm(ks[21], (L, PEER_HEADS, 2, PEER_N_KEYS, PEER_HALF), PEER_HALF ** -0.5),
        'peer_u': nrm(ks[22], (L, PEER_N_EXPERTS, D_MODEL), D_MODEL ** -0.5),
        'peer_v': nrm(ks[23], (L, PEER_N_EXPERTS, D_MODEL), 0.1),
    }

def first_block(x, mem, norm_mix, w_in, pool_w, pool_scale, conv_dw, conv_ln_g, conv_ln_b, conv_pw,
              diff_qk_norm, diff_lambda, diff_subln, sconv_w, mem_norm, w_mem_kv, mem_qk_norm,
              group_norm, w_out, norm_ffn, peer_wq, peer_subkeys, peer_u, peer_v):
    b, s, _ = x.shape
    for l in range(DEPTH):
        xn = rmsnorm(x, norm_mix[l])
        proj = xn @ w_in[l]
        u_pool, u_conv, u_diff, u_sc, u_mem = jnp.split(proj, IN_SPLITS, axis=-1)
        y_pool = pool_mixer(u_pool, pool_w[l], pool_scale[l])
        y_conv = conformer_conv(u_conv, conv_dw[l], conv_ln_g[l], conv_ln_b[l], conv_pw[l])
        y_diff = diff_attention(u_diff, diff_qk_norm[l], diff_lambda[l], diff_subln[l], l)
        y_sc = short_conv(u_sc, sconv_w[l])
        y_mem = memory_attention(u_mem, mem, mem_norm[l], w_mem_kv[l], mem_qk_norm[l])
        cat = jnp.stack([y_pool, y_conv, y_diff, y_sc, y_mem], axis=2)
        cat = rmsnorm(cat, group_norm[l].reshape(N_GROUPS, GROUP_WIDTH)).reshape(b, s, MIX_WIDTH)
        x = x + cat @ w_out[l]
        x = x + peer_ffn(rmsnorm(x, norm_ffn[l]), peer_wq[l], peer_subkeys[l], peer_u[l], peer_v[l])
    return x


CHUNK = 64
N_MIXERS = 2
CONV_WIDTH_2 = 4

D_RNN = D_MODEL
LRU_BLOCKS = 8
LRU_BLOCK_W = D_RNN // LRU_BLOCKS
RG_C = 8.0

GDN_HEAD_DIM = 128
GDN_HEADS = max(4, D_MODEL // GDN_HEAD_DIM)
GDN_DK = GDN_HEAD_DIM
GDN_DV = GDN_HEAD_DIM
GDN_HK = GDN_HEADS * GDN_DK
GDN_HV = GDN_HEADS * GDN_DV
GDN_PROJ = 2 * GDN_HK + 2 * GDN_HV + 2 * GDN_HEADS


def rmsnorm_2(x, g):
    xf = x.astype(jnp.float32)
    y = xf * lax.rsqrt(jnp.mean(xf * xf, axis=-1, keepdims=True) + EPS)
    return (y * g.astype(jnp.float32)).astype(x.dtype)

def l2norm(x):
    return x * lax.rsqrt(jnp.sum(x * x, axis=-1, keepdims=True) + EPS)

def causal_dwconv(x, w):
    k = w.shape[0]
    s = x.shape[1]
    xp = jnp.pad(x, ((0, 0), (k - 1, 0), (0, 0)))
    out = xp[:, 0:s] * w[0]
    for j in range(1, k):
        out = out + xp[:, j:j + s] * w[j]
    return out

def _lin_combine(e1, e2):
    a1, b1 = e1
    a2, b2 = e2
    return a1 * a2, a2 * b1 + b2

def rglru_block(h, in_w, conv_w, conv_b, gate_w, gate_b, lam, out_w):
    bsz, s, _ = h.shape
    proj = h @ in_w
    xb, zg = proj[..., :D_RNN], proj[..., D_RNN:]
    xb = causal_dwconv(xb, conv_w) + conv_b
    xf = xb.astype(jnp.float32)
    xg = xf.reshape(bsz, s, LRU_BLOCKS, LRU_BLOCK_W)
    pre = jnp.einsum('bsni,knij->kbsnj', xg, gate_w.astype(jnp.float32))
    pre = pre.reshape(2, bsz, s, D_RNN) + gate_b.astype(jnp.float32)[:, None, None, :]
    gates = jax.nn.sigmoid(pre)
    r_t, i_t = gates[0], gates[1]
    log_a = -RG_C * r_t * jax.nn.softplus(-lam.astype(jnp.float32))
    a_t = jnp.exp(log_a)
    mult = jnp.sqrt(-jnp.expm1(2.0 * log_a))
    b_t = mult * (i_t * xf)
    _, hseq = lax.associative_scan(_lin_combine, (a_t, b_t), axis=1)
    y = hseq.astype(h.dtype) * jax.nn.silu(zg)
    return y @ out_w

def chunk_gated_delta_rule(q, k, v, g, beta):
    bsz, s, nh, dk = q.shape
    dv = v.shape[-1]
    n = s // CHUNK

    def to_chunks(t):
        return t.reshape(bsz, n, CHUNK, nh, -1).transpose(0, 3, 1, 2, 4)

    q, k, v = to_chunks(q), to_chunks(k), to_chunks(v)
    g = g.reshape(bsz, n, CHUNK, nh).transpose(0, 3, 1, 2)
    beta = beta.reshape(bsz, n, CHUNK, nh).transpose(0, 3, 1, 2)
    g = jnp.cumsum(g, axis=-1)
    idx = jnp.arange(CHUNK)
    causal = idx[:, None] >= idx[None, :]
    strict = idx[:, None] > idx[None, :]
    diff = g[..., :, None] - g[..., None, :]
    decay_mask = jnp.exp(jnp.where(causal, diff, -jnp.inf))
    k_beta = k * beta[..., None]
    v_beta = v * beta[..., None]
    a_mat = jnp.where(strict, jnp.einsum('bhncd,bhnmd->bhncm', k_beta, k) * decay_mask, 0.0)
    eye = jnp.eye(CHUNK, dtype=jnp.float32)
    t_mat = lax.linalg.triangular_solve(a_mat + eye, jnp.broadcast_to(eye, a_mat.shape),
                                        left_side=True, lower=True)
    w = jnp.einsum('bhncm,bhnmd->bhncd', t_mat, k_beta * jnp.exp(g)[..., None])
    u = jnp.einsum('bhncm,bhnmd->bhncd', t_mat, v_beta)
    attn = jnp.where(causal, jnp.einsum('bhncd,bhnmd->bhncm', q, k) * decay_mask, 0.0)
    g_last = g[..., -1]
    q_dec = q * jnp.exp(g)[..., None]
    k_dec = k * jnp.exp(g_last[..., None] - g)[..., None]
    e_last = jnp.exp(g_last)

    def step(state, inp):
        w_c, u_c, attn_c, q_c, k_c, e_c = inp
        v_new = u_c - jnp.einsum('bhcd,bhde->bhce', w_c, state)
        o_c = jnp.einsum('bhcd,bhde->bhce', q_c, state) + jnp.einsum('bhcm,bhme->bhce', attn_c, v_new)
        state = state * e_c[..., None, None] + jnp.einsum('bhcd,bhce->bhde', k_c, v_new)
        return state, o_c

    def lead(t):
        return jnp.moveaxis(t, 2, 0)

    s0 = jnp.zeros((bsz, nh, dk, dv), jnp.float32)
    _, o = lax.scan(step, s0, (lead(w), lead(u), lead(attn), lead(q_dec), lead(k_dec), lead(e_last)))
    return o.transpose(1, 0, 3, 2, 4).reshape(bsz, s, nh, dv)

def gated_deltanet_block(h, in_w, conv_w, a_log, dt_bias, onorm_g, out_w):
    bsz, s, _ = h.shape
    proj = h @ in_w
    o1 = 2 * GDN_HK + GDN_HV
    o2 = o1 + GDN_HV
    qkv = jax.nn.silu(causal_dwconv(proj[..., :o1], conv_w))
    z = proj[..., o1:o2]
    a_in = proj[..., o2:o2 + GDN_HEADS]
    b_in = proj[..., o2 + GDN_HEADS:]
    qkv = qkv.astype(jnp.float32)
    q = qkv[..., :GDN_HK].reshape(bsz, s, GDN_HEADS, GDN_DK)
    k = qkv[..., GDN_HK:2 * GDN_HK].reshape(bsz, s, GDN_HEADS, GDN_DK)
    v = qkv[..., 2 * GDN_HK:].reshape(bsz, s, GDN_HEADS, GDN_DV)
    q = l2norm(q) * (GDN_DK ** -0.5)
    k = l2norm(k)
    beta = jax.nn.sigmoid(b_in.astype(jnp.float32))
    g = -jnp.exp(a_log.astype(jnp.float32)) * jax.nn.softplus(
        a_in.astype(jnp.float32) + dt_bias.astype(jnp.float32))
    o = chunk_gated_delta_rule(q, k, v, g, beta)
    o = o * lax.rsqrt(jnp.mean(o * o, axis=-1, keepdims=True) + EPS) * onorm_g.astype(jnp.float32)
    o = o.astype(h.dtype) * jax.nn.silu(z.reshape(bsz, s, GDN_HEADS, GDN_DV))
    return o.reshape(bsz, s, GDN_HV) @ out_w

def second_inputs(seed: int = 0) -> dict:
    key = jax.random.key(seed)
    ks = jax.random.split(key, 24)
    n_a = (DEPTH + 1) // 2
    n_b = DEPTH // 2
    f32 = jnp.float32
    nrm = lambda k, shp, sc: jax.random.normal(k, shp, f32) * sc
    x = jax.random.normal(ks[0], (BATCH, SEQ, D_MODEL), f32)
    c = jax.random.normal(ks[1], (BATCH, D_MODEL), f32)
    ada_w = nrm(ks[2], (DEPTH, D_MODEL, 3 * D_MODEL), 0.5 * D_MODEL ** -0.5)
    ada_b = nrm(ks[3], (DEPTH, 3 * D_MODEL), 0.02)
    norm_g = 1.0 + nrm(ks[4], (DEPTH, D_MODEL), 0.02)
    final_g = 1.0 + nrm(ks[5], (D_MODEL,), 0.02)
    lru_in_w = nrm(ks[6], (n_a, D_MODEL, 2 * D_RNN), D_MODEL ** -0.5)
    lru_conv_w = nrm(ks[7], (n_a, CONV_WIDTH_2, D_RNN), CONV_WIDTH_2 ** -0.5)
    lru_conv_b = nrm(ks[8], (n_a, D_RNN), 0.01)
    lru_gate_w = nrm(ks[9], (n_a, 2, LRU_BLOCKS, LRU_BLOCK_W, LRU_BLOCK_W), LRU_BLOCK_W ** -0.5)
    lru_gate_b = nrm(ks[10], (n_a, 2, D_RNN), 0.01)
    a_target = jax.random.uniform(ks[11], (n_a, D_RNN), f32, 0.9, 0.999)
    s_lam = a_target ** (1.0 / RG_C)
    lru_lambda = jnp.log(s_lam) - jnp.log1p(-s_lam)
    lru_out_w = nrm(ks[12], (n_a, D_RNN, D_MODEL), D_RNN ** -0.5)
    gdn_in_w = nrm(ks[13], (n_b, D_MODEL, GDN_PROJ), D_MODEL ** -0.5)
    gdn_conv_w = nrm(ks[14], (n_b, CONV_WIDTH_2, 2 * GDN_HK + GDN_HV), CONV_WIDTH_2 ** -0.5)
    gdn_a_log = jnp.log(jax.random.uniform(ks[15], (n_b, GDN_HEADS), f32, 1.0, 16.0))
    dt = jnp.exp(jax.random.uniform(ks[16], (n_b, GDN_HEADS), f32, math.log(1e-3), math.log(1e-1)))
    gdn_dt_bias = dt + jnp.log(-jnp.expm1(-dt))
    gdn_onorm_g = 1.0 + nrm(ks[17], (n_b, GDN_DV), 0.02)
    gdn_out_w = nrm(ks[18], (n_b, GDN_HV, D_MODEL), GDN_HV ** -0.5)
    return {"x": x, "c": c, "ada_w": ada_w, "ada_b": ada_b, "norm_g": norm_g, "final_g": final_g,
            "lru_in_w": lru_in_w, "lru_conv_w": lru_conv_w, "lru_conv_b": lru_conv_b,
            "lru_gate_w": lru_gate_w, "lru_gate_b": lru_gate_b, "lru_lambda": lru_lambda,
            "lru_out_w": lru_out_w,
            "gdn_in_w": gdn_in_w, "gdn_conv_w": gdn_conv_w, "gdn_a_log": gdn_a_log,
            "gdn_dt_bias": gdn_dt_bias, "gdn_onorm_g": gdn_onorm_g, "gdn_out_w": gdn_out_w}

def second_block(x, c, ada_w, ada_b, norm_g, final_g,
              lru_in_w, lru_conv_w, lru_conv_b, lru_gate_w, lru_gate_b, lru_lambda, lru_out_w,
              gdn_in_w, gdn_conv_w, gdn_a_log, gdn_dt_bias, gdn_onorm_g, gdn_out_w):
    c_act = jax.nn.silu(c)
    for i in range(DEPTH):
        cond = c_act @ ada_w[i] + ada_b[i]
        shift = cond[:, None, :D_MODEL]
        scale = cond[:, None, D_MODEL:2 * D_MODEL]
        gate = cond[:, None, 2 * D_MODEL:]
        h = rmsnorm_2(x, norm_g[i]) * (1.0 + scale) + shift
        j = i // N_MIXERS
        if i % N_MIXERS == 0:
            out = rglru_block(h, lru_in_w[j], lru_conv_w[j], lru_conv_b[j], lru_gate_w[j],
                              lru_gate_b[j], lru_lambda[j], lru_out_w[j])
        else:
            out = gated_deltanet_block(h, gdn_in_w[j], gdn_conv_w[j], gdn_a_log[j],
                                       gdn_dt_bias[j], gdn_onorm_g[j], gdn_out_w[j])
        x = x + gate * out
    return rmsnorm_2(x, final_g)


def setup_inputs(seed=0):
    out = dict(first_inputs(seed))
    for name, value in second_inputs(seed + 1).items():
        if name != "x":
            out[name + "_2"] = value
    return out


def reference(
    x, mem, norm_mix, w_in, pool_w, pool_scale, conv_dw, conv_ln_g, conv_ln_b, conv_pw,
    diff_qk_norm, diff_lambda, diff_subln, sconv_w, mem_norm, w_mem_kv, mem_qk_norm, group_norm,
    w_out, norm_ffn, peer_wq, peer_subkeys, peer_u, peer_v, c_2, ada_w_2, ada_b_2, norm_g_2,
    final_g_2, lru_in_w_2, lru_conv_w_2, lru_conv_b_2, lru_gate_w_2, lru_gate_b_2, lru_lambda_2,
    lru_out_w_2, gdn_in_w_2, gdn_conv_w_2, gdn_a_log_2, gdn_dt_bias_2, gdn_onorm_g_2,
    gdn_out_w_2,
):
    x = first_block(
        x, mem, norm_mix, w_in, pool_w, pool_scale, conv_dw, conv_ln_g, conv_ln_b, conv_pw,
        diff_qk_norm, diff_lambda, diff_subln, sconv_w, mem_norm, w_mem_kv, mem_qk_norm,
        group_norm, w_out, norm_ffn, peer_wq, peer_subkeys, peer_u, peer_v,
    )
    return second_block(
        x, c_2, ada_w_2, ada_b_2, norm_g_2, final_g_2, lru_in_w_2, lru_conv_w_2, lru_conv_b_2,
        lru_gate_w_2, lru_gate_b_2, lru_lambda_2, lru_out_w_2, gdn_in_w_2, gdn_conv_w_2,
        gdn_a_log_2, gdn_dt_bias_2, gdn_onorm_g_2, gdn_out_w_2,
    )


_drawn_inputs = setup_inputs


def setup_inputs(seed=0):
    import zlib

    import numpy as np

    out = dict(_drawn_inputs(seed))
    spreads = {}
    factors = {'conv_ln_g': 4.605,
     'conv_ln_b': 5.542,
     'diff_qk_norm': 3.674,
     'diff_subln': 5.76,
     'mem_norm': 3.932,
     'mem_qk_norm': 4.085,
     'norm_ffn': 7.346,
     'ada_b_2': 2.859,
     'norm_g_2': 7.913,
     'final_g_2': 8.646,
     'lru_conv_b_2': 8.0,
     'lru_gate_b_2': 24.492,
     'gdn_onorm_g_2': 32.459}
    for name, (base, spread) in spreads.items():
        noise = np.random.default_rng([zlib.crc32(name.encode()), seed]).standard_normal(out[name].shape)
        drawn = base * np.exp(spread * noise) if base else spread * noise
        out[name] = jnp.asarray(drawn.astype(out[name].dtype))
    for name, factor in factors.items():
        out[name] = (out[name] * factor).astype(out[name].dtype)
    return out
```

```python
import numpy as np
import concourse.bass as bass
from concourse import mybir
from contextlib import ExitStack

F32 = mybir.dt.float32
U32 = mybir.dt.uint32
F32R = mybir.dt.float32r
BF16 = mybir.dt.bfloat16
ALU = mybir.AluOpType
ACT = mybir.ActivationFunctionType
AX_X = mybir.AxisListType.X

P = 128
D = 1024
KD = D // P
T = 256
NT = T // P
LAYERS = 2
GW = 256
GT = GW // P
NGROUPS = 5
NIN = 20
NPROJ = 24
KMIX = NGROUPS * GT
TAPS = 31
SHORT = 3
DH = 32
MH = 64
HEADS = 4
PH = 8
NK = 128
TOPK = 16
SLOTS = PH * TOPK
EPS = 1e-6
WSLOTS = 4
WSIZE = KMIX * P
SPLITS = 3
XN_AT = NK * T - KD * T
NEG = -3.4028235e38
POOL_WINDOWS = (2, 4, 8, 16)
PADC = TAPS // 2
PADP = 8
HC = 128

C_NMIX, C_NMEM, C_NFFN, C_GROUP = 0, 8, 16, 24
C_CONV = 34
C_SCONV = C_CONV + GT * TAPS
C_LNG = C_SCONV + GT * SHORT
C_LNB = C_LNG + GT
C_QG = C_LNB + GT
C_PSCALE = C_QG + 4
C_SUBLN = C_PSCALE + GT
C_LINIT = C_SUBLN + 1
C_LAM = C_LINIT + 2
C_POOLW = C_LAM + 4 * DH
C_PW = C_POOLW + GT * P
NPAR = C_PW + GT * GW

K_ONES, K_IDENT, K_IOTA, K_BD32, K_BD64, K_EPS = 0, 128, 256, 384, 388, 390
NCONST = 392
K_COND, K_CACT = NCONST, NCONST + 2 * 24
NKEEP = K_CACT + 8
X_INV, X_DIST = 0, GT * T
NXC = X_DIST + NT * T

ORDER = [2, 3, 4, 5, 0, 1, 12, 13, 14, 15, 16, 17, 6, 7, 8, 9, 10, 11, 18, 19]
N_A, N_GATE, N_POOL, N_SH, N_SB, N_SC, N_Q, N_K, N_V, N_MQ, N_MK, N_MV = 0, 2, 4, 6, 8, 10, 12, 14, 16, 18, 20, 22
POSITION_MAJOR = (N_V, N_V + 1, N_MV, N_MV + 1)
N_CONV_MEAN, N_POOL_OUT, N_CONV_VAR = 18, 20, 22
N_OUT = NPROJ
N_WQ = N_OUT + KD
N_SUB = N_WQ + 2 * PH
N_ADA = N_SUB + 2
NCOND = 3 * KD
N_ALL = N_ADA + NCOND
NE = 2 * NK
E_HOT = 2
assert (N_ALL + E_HOT) % WSLOTS == 0


class Link:

    def __init__(self, engine, sem):
        self.engine, self.sem, self.n = engine, sem, 0

    def __call__(self, instruction):
        instruction.then_inc(self.sem, 1)
        self.n += 1
        self.engine.wait_ge(self.sem, self.n)


class Sems:

    def __init__(self, nc, ctx, prefix):
        self.nc, self.ctx, self.prefix, self.by, self.nums = nc, ctx, prefix, {}, []

    def __call__(self, name):
        if name not in self.by:
            self.by[name] = self.ctx.enter_context(self.nc.semaphore(self.prefix + name))
            self.nums.append(self.by[name].num)
        return self.by[name]

    def range(self):
        low, high = min(self.nums), max(self.nums)
        assert high - low + 1 == len(self.nums)
        return range(low, high + 1)


class Region:

    def __init__(self, tensor, size):
        self.tensor, self.size, self.at = tensor, size, 0

    def __call__(self, *shape):
        n = int(np.prod(shape))
        view = self.tensor[:, self.at:self.at + n]
        self.at += n
        assert self.at <= self.size, (self.at, self.size)
        if len(shape) == 2:
            return view.rearrange("p (a b) -> p a b", a=shape[0])
        if len(shape) == 3:
            return view.rearrange("p (a b c) -> p a b c", a=shape[0], b=shape[1])
        if len(shape) == 4:
            return view.rearrange("p (a b c d) -> p a b c d", a=shape[0], b=shape[1], c=shape[2])
        return view


def first_block(nc, ctx, mem_, ins):
    nc_ps = mem_["ps"]
    xT, xr, big, wring, split, wr, const, work = (mem_[k] for k in ("xT", "xr", "big", "wring", "split", "wr", "const", "work"))
    d_w_in, d_w_kv, d_w_out, d_wq, d_sub, d_par, d_xc, d_mem, d_e, d_ada = ins
    xn = big[:, XN_AT:].rearrange("p (k t) -> p k t", k=KD)
    s = Sems(nc, ctx, "m_")
    ones = const[:, K_ONES:K_ONES + P]
    ident = const[:, K_IDENT:K_IDENT + P]
    iota = const[:, K_IOTA:K_IOTA + P]
    ones_bf = const[:, 0:T].bitcast(BF16)
    bd32 = const[:, K_BD32:K_BD32 + HEADS]
    bd64 = const[:, K_BD64:K_BD64 + 2]
    eps = const[:, K_EPS:K_EPS + 1]
    cond = mem_["cond"]
    cact = const[:, K_CACT:K_CACT + KD]

    b = Region(big, XN_AT)
    par = b(NPAR)
    xc = b(NXC)
    memT = b(KD, T)
    memn = b(KD, T)
    sq = b(KD, T)
    proj = b(NPROJ, T)
    cat = b(KMIX, T)
    hpad = b(GT, T + 2 * PADC)
    ppad = b(3, GT, T + 2 * PADP)
    spad = b(GT, T + 2)
    conv = b(2, GT, T)
    qk = b(KD, T)
    scores = b(2, 2, T)
    probs = b(3, 2, T)
    mix = b(2, T)
    pT = b(2 * HEADS, NT, T)
    inv = xc[:, X_INV:X_INV + GT * T].rearrange("p (a t) -> p a t", a=GT)
    dist = xc[:, X_DIST:X_DIST + NT * T].rearrange("p (a t) -> p a t", a=NT)
    small = b(256)
    rexp = sq.rearrange("p k t -> p (k t)").rearrange("p (t k c) -> p t k c", t=NT, k=KD)
    r = Region(big, XN_AT)
    r.at = C_NFFN + KD
    query = r(2 * PH, T)
    score = r(NT, 2 * PH, NK)
    score2 = r(2 * PH, NK)
    cand = r(PH, TOPK * TOPK)
    cand2 = r(PH, TOPK * TOPK)
    top = r(2 * PH, TOPK)
    topi = r(2 * PH, TOPK).bitcast(U32)
    topf = r(2 * PH, TOPK)
    best = r(PH, TOPK)
    besti = r(PH, TOPK).bitcast(U32)
    pick = r(2, SLOTS).bitcast(U32)
    pickf = r(2, PH, TOPK)
    hit = r(PH, TOPK, TOPK)
    slot_t = r(NT, 3, SLOTS)
    gsum = r(2 * PH)
    w = Region(work, 4 * T)
    slot = w(3, T)
    w.at = 0
    act_e = w(2, T)
    wgt = w(2, T)
    hot = Region(mem_["wring_"], 2 * WSIZE)
    ha = hot(2, 4, P)
    hb = hot(2, 4, P)
    out_e = big[:, 0:D]
    G = big[:, :].rearrange("p (t k) -> p t k", t=T)

    def lam_slopes(h):
        return 2.0 ** (-8.0 * (h + 1) / HEADS)

    def w_source(l, n):
        if n < NIN:
            return d_w_in[l, ORDER[n]]
        if n < N_OUT:
            return d_w_kv[l, n - NIN]
        if n < N_WQ:
            return d_w_out[l, n - N_OUT]
        if n < N_SUB:
            return d_wq[l, n - N_WQ]
        if n < N_ADA:
            return d_sub[l, n - N_SUB]
        return d_ada[l, n - N_ADA]

    cat_sq = proj[:, 0:KMIX]

    def transposes(pe, u):
        pe.wait_ge(s("probs_ready"), u + 1)
        if u >= 1:
            pe.wait_ge(s("pT_ready"), u)
        for j in range(2 if u < 8 else 4):
            if u < 8:
                src, at = mix[:, u % 2, j * P:(j + 1) * P], j
            else:
                src, at = probs[:, 2, j // 2, (j % 2) * P:(j % 2 + 1) * P], j
            last = nc.tensor.transpose(nc_ps[0][:, at * P:(at + 1) * P], src, ident)
        last.then_inc(s("turned"), 1)

    def turn_evacuate(act, u):
        act.wait_ge(s("turned"), u + 1)
        if u < 8:
            h, qt = u // 2, u % 2
            nc.scalar.copy(pT[:, h, :, qt * P:(qt + 1) * P],
                           nc_ps[0][:, 0:2 * P].rearrange("p (k q) -> p k q", k=NT)).then_inc(s("pT_ready"), 1)
        else:
            h = HEADS + u - 8
            nc.scalar.copy(pT[:, h].rearrange("p k (t q) -> p t k q", t=NT),
                           nc_ps[0][:, 0:4 * P].rearrange("p (t k q) -> p t k q", t=NT, k=NT)).then_inc(s("pT_ready"), 1)

    with nc.Fori(0, LAYERS) as l:
        with nc.Block() as block:

            @block.sync
            def _(sp):
                sp.dma_start(par, d_par[l]).then_inc(s("par_loaded"), 16)
                for n in range(N_ALL):
                    if n >= WSLOTS:
                        sp.wait_ge(s("w_used"), n - WSLOTS + 1)
                    src = w_source(l, n)
                    sp.dma_start(wring[:, n % WSLOTS, 0:src.shape[1]], src).then_inc(s(f"w_loaded{n % WSLOTS}"), 16)
                    if n == 0:
                        sp.dma_start(memT, d_mem).then_inc(s("mem_loaded"), 16)
                        sp.dma_start(xc, d_xc).then_inc(s("par_loaded"), 16)
                for k in range(WSLOTS):
                    sp.wait_ge(s("w_used"), N_ALL + k - WSLOTS + 1)
                    if k == E_HOT:
                        sp.wait_ge(s("g_ready"), T // 4)
                    sp.dma_start(wring[:, (N_ALL + k) % WSLOTS, 0:D], d_e[l, k]).then_inc(s(f"w_loaded{(N_ALL + k) % WSLOTS}"), 16)
                with sp.Fori(0, NE // WSLOTS - 1) as i:
                    for e in range(WSLOTS):
                        sp.wait_ge(s("lo_done"), i * WSLOTS + (e + 1))
                        sp.dma_start(wring[:, (N_ALL + e) % WSLOTS, 0:D], d_e[l, i * WSLOTS + (e + WSLOTS)]).then_inc(s(f"w_loaded{(N_ALL + e) % WSLOTS}"), 16)

            @block.tensor
            def _(pe):
                def w_tile(n):
                    pe.wait_ge(s(f"w_loaded{n % WSLOTS}"), 16 * (n // WSLOTS + 1))
                    return wring[:, n % WSLOTS]

                def sums(out, src, tiles, columns=ones[:, 0:1]):
                    for tt in range(NT):
                        for i in range(tiles):
                            last = nc.tensor.matmul(out[:, tt], src[:, i, tt * P:(tt + 1) * P], columns,
                                                    start=(i == 0), stop=(i == tiles - 1))
                    return last

                def spread(out, col):
                    for tt in range(NT):
                        last = nc.tensor.matmul(out[:, tt * P:(tt + 1) * P], col[:, tt].broadcast_to([P, P]), ident, start=True, stop=True)
                    return last

                pe.wait_ge(s("sq_x"), 1)
                sums(nc_ps[4][:, 0:2].rearrange("p (t c) -> p t c", t=NT), sq, KD).then_inc(s("sum_x"), 1)
                pe.wait_ge(s("rstd_x"), 1)
                spread(nc_ps[4][:, T:2 * T], small[:, 0:2].rearrange("p (t c) -> p t c", t=NT)).then_inc(s("spread_x"), 1)
                pe.wait_ge(s("sq_mem"), 1)
                sums(nc_ps[5][:, 0:2].rearrange("p (t c) -> p t c", t=NT), sq, KD).then_inc(s("sum_mem"), 1)
                for n in range(NPROJ):
                    if n == 0:
                        pe.wait_ge(s("xn_ready"), 1)
                    if n == 1:
                        pe.wait_ge(s("rstd_mem"), 1)
                        spread(nc_ps[5][:, T:2 * T], small[:, 2:4].rearrange("p (t c) -> p t c", t=NT)).then_inc(s("spread_mem"), 1)
                    if n == NIN:
                        pe.wait_ge(s("memn_ready"), 1)
                    if n == N_CONV_MEAN:
                        pe.wait_ge(s("conv_done"), 1)
                        sums(nc_ps[6][:, 0:2].rearrange("p (t c) -> p t c", t=NT), conv[:, 0], GT).then_inc(s("sum_conv"), 1)
                        pe.wait_ge(s("mean_conv"), 1)
                        spread(nc_ps[6][:, T:2 * T], small[:, 4:6].rearrange("p (t c) -> p t c", t=NT)).then_inc(s("spread_mean"), 1)
                    if n == N_POOL_OUT:
                        pe.wait_ge(s("pooled"), 1)
                        for i in range(GT):
                            last = nc.tensor.matmul(nc_ps[5][:, i * T:(i + 1) * T], par[:, C_POOLW + i * P:C_POOLW + (i + 1) * P],
                                                    ppad[:, 0, i, 0:T], start=True, stop=True)
                        last.then_inc(s("pool_out"), 1)
                    if n == N_CONV_VAR:
                        pe.wait_ge(s("centred"), 1)
                        sums(nc_ps[7][:, 0:2].rearrange("p (t c) -> p t c", t=NT), conv[:, 0], GT).then_inc(s("sum_var"), 1)
                        pe.wait_ge(s("rstd_conv"), 1)
                        spread(nc_ps[7][:, T:2 * T], small[:, 6:8].rearrange("p (t c) -> p t c", t=NT)).then_inc(s("spread_var"), 1)
                    src = xn if n < NIN else memn
                    wt = w_tile(n)[:, 0:D].rearrange("p (k c) -> p k c", k=KD)
                    if n >= 4:
                        pe.wait_ge(s("proj_kept"), n - 3)
                    out = nc_ps[n % 4]
                    if n in POSITION_MAJOR:
                        for tt in range(NT):
                            for k in range(KD):
                                last = nc.tensor.matmul(out[:, tt * P:(tt + 1) * P], src[:, k, tt * P:(tt + 1) * P], wt[:, k],
                                                        start=(k == 0), stop=(k == KD - 1))
                    else:
                        for k in range(KD):
                            last = nc.tensor.matmul(out[:, 0:T], wt[:, k], src[:, k], start=(k == 0), stop=(k == KD - 1))
                    last.then_inc(s("w_used"), 1)
                pe.wait_ge(s("sq_qk"), 1)
                pe.wait_ge(s("proj_kept"), NPROJ)
                qs = nc_ps[0][:, 0:NT * 24].rearrange("p (t c) -> p t c", t=NT)
                for i in range(KD):
                    c, m, cols = (4 * i, HEADS, bd32) if i < 4 else (16 + 2 * (i - 4), 2, bd64)
                    for tt in range(NT):
                        last = nc.tensor.matmul(qs[:, tt, c:c + m], sq[:, i, tt * P:(tt + 1) * P], cols, start=True, stop=True)
                last.then_inc(s("sum_qk"), 1)
                pe.wait_ge(s("rstd_qk"), 1)
                pe.wait_ge(s("conv_normed"), 1)
                pe.wait_ge(s("pool_kept"), 1)
                for i in range(KD):
                    last = spread(nc_ps[4 + i // 2][:, (i % 2) * T:(i % 2 + 1) * T], rexp[:, :, i])
                last.then_inc(s("spread_qk"), 1)
                pe.wait_ge(s("qk_ready"), 1)
                for u in range(12):
                    if u >= 4:
                        pe.wait_ge(s("scores_used"), u - 3)
                    out = nc_ps[4 + u % 4]
                    for j in range(2):
                        if u < 8:
                            h, qt = u // 2, u % 2
                            rows = slice(DH * h, DH * (h + 1))
                            last = nc.tensor.matmul(out[:, j * T:(j + 1) * T], qk[rows, j, qt * P:(qt + 1) * P], qk[rows, 2 + j],
                                                    start=True, stop=True)
                        else:
                            h = u - 8
                            rows = slice(MH * (h % 2), MH * (h % 2 + 1))
                            last = nc.tensor.matmul(out[:, j * T:(j + 1) * T], qk[rows, 4 + h // 2, j * P:(j + 1) * P],
                                                    qk[rows, 6 + h // 2], start=True, stop=True)
                    last.then_inc(s("scores_ready"), 1)
                    if u >= 3:
                        transposes(pe, u - 3)
                for u in range(9, 12):
                    transposes(pe, u)
                pe.wait_ge(s("conv_silu"), 1)
                pe.wait_ge(s("pT_ready"), 12)
                for i in range(GT):
                    for k in range(GT):
                        last = nc.tensor.matmul(nc_ps[0][:, i * T:(i + 1) * T], par[:, C_PW + k * GW + i * P:C_PW + k * GW + (i + 1) * P],
                                                conv[:, 1, k], start=(k == 0), stop=(k == GT - 1))
                last.then_inc(s("conv_out"), 1)
                for a in range(2):
                    for h in range(HEADS):
                        rows = slice(MH * (h % 2), MH * (h % 2 + 1))
                        vt = proj[:, (N_V if a == 0 else N_MV) + h // 2]
                        for kt in range(NT):
                            last = nc.tensor.matmul(nc_ps[2 + a][rows, (h // 2) * T:(h // 2 + 1) * T],
                                                    vt[:, kt * P + MH * (h % 2):kt * P + MH * (h % 2 + 1)],
                                                    pT[:, a * HEADS + h, kt], start=(kt == 0), stop=(kt == NT - 1))
                    last.then_inc(s("attn_out"), 1)
                pe.wait_ge(s("sq_sub"), 1)
                ss = nc_ps[6][:, 0:8].rearrange("p (t c) -> p t c", t=NT)
                for tt in range(NT):
                    for i in range(GT):
                        last = nc.tensor.matmul(ss[:, tt, 2 * i:2 * i + 2], sq[:, i, tt * P:(tt + 1) * P], bd64, start=True, stop=True)
                last.then_inc(s("sum_sub"), 1)
                pe.wait_ge(s("rstd_sub"), 1)
                for i in range(GT):
                    last = spread(nc_ps[7][:, i * T:(i + 1) * T], rexp[:, :, i])
                last.then_inc(s("spread_sub"), 1)
                pe.wait_ge(s("sq_cat"), 1)
                gs = nc_ps[6][:, 16:16 + NT * NGROUPS].rearrange("p (t c) -> p t c", t=NT)
                for tt in range(NT):
                    for g in range(NGROUPS):
                        for i in range(GT):
                            last = nc.tensor.matmul(gs[:, tt, g:g + 1], cat_sq[:, GT * g + i, tt * P:(tt + 1) * P], ones[:, 0:1],
                                                    start=(i == 0), stop=(i == GT - 1))
                last.then_inc(s("sum_cat"), 1)
                pe.wait_ge(s("rstd_cat"), 1)
                for g in range(NGROUPS):
                    col = small[:, 64:64 + NT * NGROUPS].rearrange("p (t c) -> p t c", t=NT)[:, :, g:g + 1]
                    last = spread(nc_ps[1 + g // 2][:, (g % 2) * T:(g % 2 + 1) * T], col)
                last.then_inc(s("spread_cat"), 1)
                pe.wait_ge(s("cat_ready"), 1)
                for m in range(KD):
                    wt = w_tile(N_OUT + m)[:, 0:WSIZE].rearrange("p (k c) -> p k c", k=KMIX)
                    if m >= 4:
                        pe.wait_ge(s("out_added"), m - 3)
                    for k in range(KMIX):
                        last = nc.tensor.matmul(nc_ps[4 + m % 4][:, 0:T], wt[:, k], cat[:, k], start=(k == 0), stop=(k == KMIX - 1))
                    last.then_inc(s("w_used"), 1)

                pe.wait_ge(s("sq_ffn"), 1)
                sums(nc_ps[0][:, 0:2].rearrange("p (t c) -> p t c", t=NT), sq, KD).then_inc(s("sum_ffn"), 1)
                pe.wait_ge(s("rstd_ffn"), 1)
                spread(nc_ps[0][:, T:2 * T], small[:, 80:82].rearrange("p (t c) -> p t c", t=NT)).then_inc(s("spread_ffn"), 1)
                pe.wait_ge(s("ffn_ready"), 1)
                for m in range(2 * PH):
                    wt = w_tile(N_WQ + m)[:, 0:D].rearrange("p (k c) -> p k c", k=KD)
                    if m >= 4:
                        pe.wait_ge(s("query_kept"), m - 3)
                    for k in range(KD):
                        last = nc.tensor.matmul(nc_ps[m % 4][:, 0:T], wt[:, k], xn[:, k], start=(k == 0), stop=(k == KD - 1))
                    last.then_inc(s("w_used"), 1)
                pe.wait_ge(s("query_kept"), 2 * PH)
                w_tile(N_SUB), w_tile(N_SUB + 1)
                for tt in range(NT):
                    for q in range(4):
                        if tt > 0:
                            pe.wait_ge(s("score_kept"), q + 1)
                        for j in range(4):
                            m = 4 * q + j
                            sub = wring[:, (N_SUB + m // 8) % WSLOTS, 0:D].rearrange("p (k c) -> p k c", k=KD)[:, m % 8]
                            last = nc.tensor.matmul(nc_ps[4 + q][:, j * P:(j + 1) * P], query[:, m, tt * P:(tt + 1) * P], sub,
                                                    start=True, stop=True)
                        last.then_inc(s("score_ready"), 1)
                pe.wait_ge(s("score_kept"), 4 * NT)
                pe.sem_inc(s("w_used"), 2)
                for n in range(NCOND):
                    wt = w_tile(N_ADA + n)[:, 0:D].rearrange("p (k c) -> p k c", k=KD)
                    for k in range(KD):
                        last = nc.tensor.matmul(nc_ps[3][:, n:n + 1], wt[:, k], cact[:, k:k + 1], start=(k == 0), stop=(k == KD - 1))
                    last.then_inc(s("w_used"), 1)
                for tt in range(NT):
                    pe.wait_ge(s("slots_ready"), tt + 1)
                    for j in range(3):
                        last = nc.tensor.transpose(nc_ps[j][:, tt * P:(tt + 1) * P], slot_t[:, tt, j], ident)
                    last.then_inc(s("slots_turned"), 1)

                with pe.Fori(0, T // 8) as i:
                    for g in range(2):
                        pe.wait_ge(s("hot_ready"), i * 2 + (g + 1))
                        pe.wait_ge(s("g_kept"), i * 2 + (g + 1))
                        for j in range(4):
                            last = nc.tensor.matmul(nc_ps[g][:, j * P:(j + 1) * P], ha[:, g, j], hb[:, g, j], start=True, stop=True)
                        last.then_inc(s("g_ready"), 1)

                pe.wait_ge(s("g_kept"), 2 + T // 4)
                pe.wait_ge(s("zeros"), 1)
                pe.wait_ge(s("cond_kept"), 1)
                for tt in range(NT):
                    for c in range(2):
                        nc.tensor.matmul(nc_ps[4 + 2 * tt + c][:, 0:512], mem_["zeros"][:, 0:P], ones_bf,
                                         start=True, stop=False, skip_group_check=True)

                def up(n, k, ready, wait_free):
                    pe.wait_ge(s("lo_done"), ready)
                    if wait_free is not None:
                        pe.wait_ge(s("act_used"), wait_free)
                    hi, lo = split[:, k % SPLITS, 0], split[:, k % SPLITS, 1]
                    for j in range(KD):
                        for a, x in ((hi, 0), (hi, 1), (lo, 0)):
                            last = nc.tensor.matmul(nc_ps[2 + n % 2][:, 0:T], a[:, j * P:(j + 1) * P], xr[:, x, j],
                                                    start=(j == 0 and a is hi and x == 0), stop=(j == KD - 1 and a is lo))
                    last.then_inc(s("split_used"), 1)

                def down(n, k, ready, wgt_, stop=False):
                    pe.wait_ge(s("lo_done"), ready)
                    pe.wait_ge(s("wgt_ready"), wgt_)
                    hi, lo = split[:, k % SPLITS, 0], split[:, k % SPLITS, 1]
                    for tt in range(NT):
                        for x, v in ((0, hi), (0, lo), (1, hi)):
                            for c in range(2):
                                last = nc.tensor.matmul(nc_ps[4 + 2 * tt + c][:, 0:512], wr[:, x, n % 2, tt * P:(tt + 1) * P],
                                                        v[:, c * 512:(c + 1) * 512], start=False, stop=stop and x == 1, skip_group_check=True)
                    last.then_inc(s("split_used"), 1)

                up(0, 0, 1, None)
                with pe.Fori(0, NK // 6) as i:
                    for e in range(6):
                        up(e + 1, 2 * e + 1, i * 12 + (2 * e + 2), i * 6 + (e + 2))
                        down(e, 2 * e + 2, i * 12 + (2 * e + 3), i * 6 + (e + 1))
                for n in range(NK // 6 * 6, NK):
                    if n + 1 < NK:
                        up(n + 1, 2 * n + 1, 2 * n + 2, n + 2)
                    k = min(2 * n + 2, NE - 1)
                    down(n, k, k + 1, n + 1, n == NK - 1)
                for tt in range(NT):
                    for k in range(KD):
                        if k % 4 == 0:
                            pe.wait_ge(s("peer_kept"), tt + 1)
                            if tt > 0:
                                pe.wait_ge(s("peer_added"), k // 4 + 1)
                        last = nc.tensor.transpose(nc_ps[k // 4][:, (k % 4) * P:(k % 4 + 1) * P], out_e[:, k * P:(k + 1) * P], ident)
                        if k % 4 == 3:
                            last.then_inc(s("peer_turned"), 1)

            @block.scalar
            def _(act):
                link = Link(act, s("act_link"))

                def root(src, dst, n, width, ready, done):
                    act.wait_ge(s(ready), 1)
                    nc.scalar.activation(dst, src, ACT.Sqrt, scale=1.0 / width, bias=eps).then_inc(s(done), 1)

                nc.scalar.activation(sq[:, :, :], xT[:, :, :], ACT.Square).then_inc(s("sq_x"), 1)
                root(nc_ps[4][:, 0:2], small[:, 0:2], 2, D, "sum_x", "root_x")
                act.wait_ge(s("mem_loaded"), 16)
                nc.scalar.activation(sq[:, :, :], memT, ACT.Square).then_inc(s("sq_mem"), 1)
                root(nc_ps[5][:, 0:2], small[:, 2:4], 2, D, "sum_mem", "root_mem")
                for n in range(NPROJ):
                    if n == N_CONV_MEAN:
                        act.wait_ge(s("sum_conv"), 1)
                        nc.scalar.mul(small[:, 4:6], nc_ps[6][:, 0:2], 1.0 / GW).then_inc(s("mean_conv"), 1)
                    if n == N_CONV_VAR:
                        act.wait_ge(s("pool_out"), 1)
                        for i in range(GT):
                            last = nc.scalar.activation(cat[:, i], nc_ps[5][:, i * T:(i + 1) * T], ACT.Copy,
                                                        scale=par[:, C_PSCALE + i:C_PSCALE + i + 1])
                        last.then_inc(s("pool_kept"), 1)
                        root(nc_ps[7][:, 0:2], small[:, 6:8], 2, GW, "sum_var", "root_conv")
                    act.wait_ge(s("w_used"), n + 1)
                    nc.scalar.copy(proj[:, n], nc_ps[n % 4][:, 0:T]).then_inc(s("proj_kept"), 1)
                    if n == N_GATE + 1:
                        act.wait_ge(s("proj_kept"), N_GATE + 2)
                        nc.scalar.activation(proj[:, N_GATE:N_GATE + 2], proj[:, N_GATE:N_GATE + 2], ACT.Sigmoid).then_inc(s("gate_ready"), 1)
                act.wait_ge(s("proj_kept"), NPROJ)
                act.wait_ge(s("spread_mem"), 1)
                nc.scalar.activation(sq[:, 0:4], proj[:, N_Q:N_Q + 4], ACT.Square)
                nc.scalar.activation(sq[:, 4:8], proj[:, N_MQ:N_MQ + 4], ACT.Square).then_inc(s("sq_qk"), 1)
                act.wait_ge(s("sum_qk"), 1)
                qs = nc_ps[0][:, 0:NT * 24].rearrange("p (t c) -> p t c", t=NT)
                rq = small[:, 16:16 + NT * 24].rearrange("p (t c) -> p t c", t=NT)
                nc.scalar.activation(rq[:, :, 0:16], qs[:, :, 0:16], ACT.Sqrt, scale=1.0 / DH, bias=eps)
                nc.scalar.activation(rq[:, :, 16:24], qs[:, :, 16:24], ACT.Sqrt, scale=1.0 / MH, bias=eps).then_inc(s("root_qk"), 1)
                act.wait_ge(s("conv_normed"), 1)
                for i in range(GT):
                    last = nc.scalar.activation(conv[:, 1, i], conv[:, 0, i], ACT.Silu, scale=par[:, C_LNG + i:C_LNG + i + 1],
                                                bias=par[:, C_LNB + i:C_LNB + i + 1])
                last.then_inc(s("conv_silu"), 1)
                act.wait_ge(s("lam_sums"), 1)
                nc.scalar.activation(small[:, 100:102], small[:, 102:104], ACT.Exp).then_inc(s("lam_exp"), 1)
                for u in range(12):
                    act.wait_ge(s("max_ready"), u + 1)
                    slot_ = u % 2 if u < 8 else 2
                    if u >= 2 and u < 8:
                        act.wait_ge(s("probs_ready"), u - 1)
                    if u >= 9:
                        act.wait_ge(s("turned"), u)
                    for j in range(2):
                        src = scores[:, u % 2, j] if u < 8 else nc_ps[4 + u % 4][:, j * T:(j + 1) * T]
                        c = 112 + 2 * (u % 4) + j
                        last = nc.scalar.activation(probs[:, slot_, j], src, ACT.Exp, bias=small[:, c:c + 1],
                                                    scale=(DH if u < 8 else MH) ** -0.5, accum_out=small[:, 128 + 2 * u + j:129 + 2 * u + j])
                    last.then_inc(s("exp_ready"), 1)
                    if u >= 1:
                        turn_evacuate(act, u - 1)
                turn_evacuate(act, 11)
                act.wait_ge(s("conv_out"), 1)
                nc.scalar.copy(cat[:, GT:2 * GT], nc_ps[0][:, 0:GT * T].rearrange("p (a t) -> p a t", a=GT)).then_inc(s("conv_kept"), 1)
                act.wait_ge(s("attn_out"), 1)
                nc.scalar.copy(cat[:, 2 * GT:3 * GT], nc_ps[2][:, 0:GT * T].rearrange("p (a t) -> p a t", a=GT))
                nc.scalar.activation(sq[:, 0:GT], nc_ps[2][:, 0:GT * T].rearrange("p (a t) -> p a t", a=GT), ACT.Square).then_inc(s("sq_sub"), 1)
                act.wait_ge(s("attn_out"), 2)
                nc.scalar.copy(cat[:, 4 * GT:5 * GT], nc_ps[3][:, 0:GT * T].rearrange("p (a t) -> p a t", a=GT)).then_inc(s("mem_kept"), 1)
                act.wait_ge(s("sum_sub"), 1)
                nc.scalar.activation(small[:, 8:16], nc_ps[6][:, 0:8], ACT.Sqrt, scale=1.0 / MH, bias=eps).then_inc(s("root_sub"), 1)
                act.wait_ge(s("cat_full"), 1)
                nc.scalar.activation(cat_sq, cat, ACT.Square).then_inc(s("sq_cat"), 1)
                act.wait_ge(s("sum_cat"), 1)
                nc.scalar.activation(small[:, 64:64 + NT * NGROUPS], nc_ps[6][:, 16:16 + NT * NGROUPS], ACT.Sqrt,
                                     scale=1.0 / GW, bias=eps).then_inc(s("root_cat"), 1)

                act.wait_ge(s("out_added"), KD)
                nc.scalar.activation(sq[:, :, :], xT[:, :, :], ACT.Square).then_inc(s("sq_ffn"), 1)
                act.wait_ge(s("sum_ffn"), 1)
                nc.scalar.activation(small[:, 80:82], nc_ps[0][:, 0:2], ACT.Sqrt, scale=1.0 / D, bias=eps).then_inc(s("root_ffn"), 1)
                act.wait_ge(s("ffn_ready"), 1)
                for m in range(2 * PH):
                    act.wait_ge(s("w_used"), N_WQ + m + 1)
                    nc.scalar.copy(query[:, m], nc_ps[m % 4][:, 0:T]).then_inc(s("query_kept"), 1)
                for tt in range(NT):
                    for q in range(4):
                        act.wait_ge(s("score_ready"), 4 * tt + q + 1)
                        nc.scalar.copy(score[:, tt, 4 * q:4 * q + 4], nc_ps[4 + q][:, :].rearrange("p (a c) -> p a c", a=4)).then_inc(s("score_kept"), 1)
                for tt in range(NT):
                    act.wait_ge(s("best_shifted"), tt + 1)
                    nc.scalar.activation(cand[:, :, 0:TOPK], cand2[:, :, 0:TOPK], ACT.Exp).then_inc(s("best_exp"), 1)
                act.wait_ge(s("w_used"), N_ALL)
                nc.scalar.copy(cond[:, bass.ds(l, 1)].squeeze(1), nc_ps[3][:, 0:NCOND]).then_inc(s("cond_kept"), 1)
                act.wait_ge(s("slots_turned"), NT)
                for j in range(3):
                    last = nc.scalar.copy(slot[:, j], nc_ps[j][:, 0:T])
                last.then_inc(s("slots_kept"), 1)
                act.wait_ge(s("slots_kept"), 1)
                act.sem_inc(s("g_kept"), 2)
                with act.Fori(0, T // 8) as i:
                    for g in range(2):
                        act.wait_ge(s("g_ready"), i * 2 + (g + 1))
                        nc.scalar.copy(G[:, bass.ds(i * 8 + 4 * g, 4)], nc_ps[g][:, :].rearrange("p (a c) -> p a c", a=4)).then_inc(s("g_kept"), 1)

                def high(k, slot_, loaded, free):
                    act.wait_ge(s(f"w_loaded{slot_}"), loaded)
                    if free is not None:
                        act.wait_ge(s("split_used"), free)
                    nc.scalar.copy(split[:, k % SPLITS, 0], wring[:, slot_, 0:D]).then_inc(s("hi_done"), 1)

                def gelu(n, used):
                    act.wait_ge(s("split_used"), used)
                    nc.scalar.activation(act_e[:, n % 2], nc_ps[2 + n % 2][:, 0:T], ACT.Gelu).then_inc(s("act_used"), 1)

                act.sem_inc(s("act_used"), 2)
                for n in range(2):
                    if n == 1:
                        gelu(0, 1)
                    for k in (2 * n, 2 * n + 1):
                        high(k, (N_ALL + k) % WSLOTS, 16 * ((N_ALL + k) // WSLOTS + 1), k - 2 if k > 2 else None)
                with act.Fori(0, NK // 6) as i:
                    for e in range(6):
                        gelu(e + 1, i * 12 + (2 * e + 2))
                        for k in (2 * e + 4, 2 * e + 5):
                            high(k, (N_ALL + k) % WSLOTS, (i * 3 + ((N_ALL + k) // WSLOTS + 1)) * 16, i * 12 + (k - 2))
                gelu(NK - 1, 2 * (NK - 1))
                for tt in range(NT):
                    act.wait_ge(s("split_used"), NE)
                    if tt > 0:
                        act.wait_ge(s("peer_turned"), 2 * tt)
                    for c in range(2):
                        last = nc.scalar.copy(out_e[:, c * 512:(c + 1) * 512], nc_ps[4 + 2 * tt + c][:, :])
                    last.then_inc(s("peer_kept"), 1)

            @block.gpsimd
            def _(pool):
                link = Link(pool, s("pool_link"))
                nc.gpsimd.memset(hpad, 0.0)
                nc.gpsimd.memset(spad, 0.0)
                nc.gpsimd.memset(ppad, 0.0).then_inc(s("pads"), 1)
                nc.gpsimd.memset(mem_["zeros"][:, :], 0.0).then_inc(s("zeros"), 1)
                pool.wait_ge(s("pads"), 1)
                pool.wait_ge(s("proj_kept"), N_POOL + 2)
                link(nc.gpsimd.tensor_copy(ppad[:, 0, :, PADP:PADP + T], proj[:, N_POOL:N_POOL + 2]))
                W_ = T + 2 * PADP
                link(nc.gpsimd.tensor_tensor(ppad[:, 1, :, 1:W_], ppad[:, 0, :, 0:W_ - 1], ppad[:, 0, :, 1:W_], ALU.add))
                link(nc.gpsimd.tensor_tensor(ppad[:, 2, :, 1:W_ - 1], ppad[:, 1, :, 0:W_ - 2], ppad[:, 1, :, 2:W_], ALU.add))
                nc.gpsimd.tensor_copy(ppad[0:64, 0, 0, 0:T], ppad[0:64, 1, 0, PADP:PADP + T])
                link(nc.gpsimd.tensor_copy(ppad[64:128, 0, 0, 0:T], ppad[64:128, 2, 0, PADP:PADP + T]))
                link(nc.gpsimd.tensor_tensor(ppad[:, 1, 1, 3:W_ - 3], ppad[:, 2, 1, 1:W_ - 5], ppad[:, 2, 1, 5:W_ - 1], ALU.add))
                nc.gpsimd.tensor_copy(ppad[0:64, 0, 1, 0:T], ppad[0:64, 1, 1, PADP:PADP + T])
                link(nc.gpsimd.tensor_tensor(ppad[64:128, 0, 1, 0:T], ppad[64:128, 1, 1, PADP - 4:PADP - 4 + T],
                                             ppad[64:128, 1, 1, PADP + 4:PADP + 4 + T], ALU.add))
                link(nc.gpsimd.tensor_tensor(ppad[:, 0, :, 0:T], ppad[:, 0, :, 0:T], inv, ALU.mult))
                nc.gpsimd.tensor_tensor(ppad[:, 0, :, 0:T], ppad[:, 0, :, 0:T], proj[:, N_POOL:N_POOL + 2], ALU.subtract).then_inc(s("pooled"), 1)
                pool.wait_ge(s("proj_kept"), N_SC + 2)
                nc.gpsimd.tensor_tensor(spad[:, :, 1:1 + T], proj[:, N_SC:N_SC + 2], proj[:, N_SH:N_SH + 2], ALU.mult).then_inc(s("short_in"), 1)

            @block.vector
            def _(dve):
                link = Link(dve, s("dve_link"))

                def recip(n0, n1, ready, done):
                    dve.wait_ge(s(ready), 1)
                    nc.vector.reciprocal(small[:, n0:n1], small[:, n0:n1]).then_inc(s(done), 1)

                def normed(dst, src, gain, spread_, ready, done):
                    dve.wait_ge(s(ready), 1)
                    for k in range(KD):
                        last = nc.vector.scalar_tensor_tensor(dst[:, k], src[:, k], gain[:, k:k + 1], spread_, ALU.mult, ALU.mult)
                    last.then_inc(s(done), 1)

                recip(0, 2, "root_x", "rstd_x")
                dve.wait_ge(s("par_loaded"), 32)
                normed(xn, xT, par[:, C_NMIX:C_NMIX + KD], nc_ps[4][:, T:2 * T], "spread_x", "xn_ready")
                recip(2, 4, "root_mem", "rstd_mem")
                normed(memn, memT, par[:, C_NMEM:C_NMEM + KD], nc_ps[5][:, T:2 * T], "spread_mem", "memn_ready")
                for j in range(2):
                    a = C_LAM + 2 * DH * j
                    link(nc.vector.tensor_tensor(small[:, 192:192 + DH], par[:, a:a + DH], par[:, a + DH:a + 2 * DH], ALU.mult))
                    link(nc.vector.reduce_sum(small[:, 102 + j:103 + j], small[:, 192:192 + DH], AX_X))
                dve.sem_inc(s("lam_sums"), 1)
                dve.wait_ge(s("gate_ready"), 1)
                dve.wait_ge(s("pads"), 1)
                link(nc.vector.tensor_tensor(hpad[:, :, PADC:PADC + T], proj[:, N_A:N_A + 2], proj[:, N_GATE:N_GATE + 2], ALU.mult))
                for k in range(TAPS):
                    for i in range(GT):
                        tap = par[:, C_CONV + i * TAPS + k:C_CONV + i * TAPS + k + 1]
                        src = hpad[:, i, k:k + T]
                        if k == 0:
                            nc.vector.tensor_scalar(conv[:, 0, i], src, tap, None, ALU.mult).then_inc(s("conv_tap"), 1)
                        else:
                            dve.wait_ge(s("conv_tap"), GT * (k - 1) + i + 1)
                            nc.vector.scalar_tensor_tensor(conv[:, 0, i], src, tap, conv[:, 0, i], ALU.mult, ALU.add).then_inc(s("conv_tap"), 1)
                dve.wait_ge(s("conv_tap"), GT * TAPS)
                dve.sem_inc(s("conv_done"), 1)
                dve.wait_ge(s("short_in"), 1)
                for k in range(SHORT):
                    for i in range(GT):
                        tap = par[:, C_SCONV + i * SHORT + k:C_SCONV + i * SHORT + k + 1]
                        src = spad[:, i, k:k + T]
                        if k == 0:
                            last = nc.vector.tensor_scalar(cat[:, 3 * GT + i], src, tap, None, ALU.mult)
                        else:
                            last = nc.vector.scalar_tensor_tensor(cat[:, 3 * GT + i], src, tap, cat[:, 3 * GT + i], ALU.mult, ALU.add)
                    link(last)
                dve.wait_ge(s("proj_kept"), N_SB + 2)
                nc.vector.tensor_tensor(cat[:, 3 * GT:4 * GT], cat[:, 3 * GT:4 * GT], proj[:, N_SB:N_SB + 2], ALU.mult).then_inc(s("short_out"), 1)
                dve.wait_ge(s("spread_mean"), 1)
                for i in range(GT):
                    link(nc.vector.tensor_tensor(conv[:, 1, i], conv[:, 0, i], nc_ps[6][:, T:2 * T], ALU.subtract))
                nc.vector.tensor_tensor(conv[:, 0], conv[:, 1], conv[:, 1], ALU.mult).then_inc(s("centred"), 1)
                recip(6, 8, "root_conv", "rstd_conv")
                dve.wait_ge(s("spread_var"), 1)
                for i in range(GT):
                    last = nc.vector.tensor_tensor(conv[:, 0, i], conv[:, 1, i], nc_ps[7][:, T:2 * T], ALU.mult)
                last.then_inc(s("conv_normed"), 1)
                dve.wait_ge(s("root_qk"), 1)
                link(nc.vector.reciprocal(small[:, 16:16 + NT * 24], small[:, 16:16 + NT * 24]))
                rq = small[:, 16:16 + NT * 24].rearrange("p (t c) -> p t c", t=NT)
                for tt in range(NT):
                    nc.vector.tensor_copy(rexp[:, tt, 0:4].rearrange("p k (h c) -> p (k h) c", h=HEADS),
                                          rq[:, tt, 0:16].unsqueeze(2).broadcast_to([P, 16, DH]))
                    last = nc.vector.tensor_copy(rexp[:, tt, 4:8].rearrange("p k (h c) -> p (k h) c", h=2),
                                                 rq[:, tt, 16:24].unsqueeze(2).broadcast_to([P, 8, MH]))
                last.then_inc(s("rstd_qk"), 1)
                dve.wait_ge(s("spread_qk"), 1)
                for i in range(KD):
                    src = proj[:, N_Q + i] if i < 4 else proj[:, N_MQ + i - 4]
                    gain = par[:, C_QG + i // 2:C_QG + i // 2 + 1]
                    last = nc.vector.scalar_tensor_tensor(qk[:, i], src, gain, nc_ps[4 + i // 2][:, (i % 2) * T:(i % 2 + 1) * T],
                                                          ALU.mult, ALU.mult)
                last.then_inc(s("qk_ready"), 1)
                dve.wait_ge(s("lam_exp"), 1)
                link(nc.vector.tensor_tensor(small[:, 104:105], small[:, 101:102], small[:, 100:101], ALU.subtract))
                link(nc.vector.tensor_tensor(small[:, 104:105], small[:, 104:105], par[:, C_LINIT:C_LINIT + 1], ALU.subtract))

                def maxima(u):
                    dve.wait_ge(s("scores_ready"), u + 1)
                    scale = (DH if u < 8 else MH) ** -0.5
                    bank = nc_ps[4 + u % 4][:, :].rearrange("p (j k) -> p j k", j=2)
                    src = bank
                    if u < 8:
                        h, qt = u // 2, u % 2
                        if u >= 2:
                            dve.wait_ge(s("exp_ready"), u - 1)
                        link(nc.vector.scalar_tensor_tensor(scores[:, u % 2], dist[:, qt].unsqueeze(1).broadcast_to([P, 2, T]),
                                                            -lam_slopes(h) / scale, bank, ALU.mult, ALU.add))
                        src = scores[:, u % 2]
                    if u >= 4:
                        dve.wait_ge(s("exp_ready"), u - 3)
                    m = small[:, 112 + 2 * (u % 4):114 + 2 * (u % 4)]
                    link(nc.vector.tensor_reduce(m, src, AX_X, ALU.max))
                    if u < 8:
                        nc.vector.tensor_scalar(m, m, -scale, None, ALU.mult).then_inc(s("max_ready"), 1)
                        dve.sem_inc(s("scores_used"), 1)
                    else:
                        nc.vector.tensor_scalar(m, m, -scale, None, ALU.mult).then_inc(s("max_ready"), 1)

                def combine(u):
                    dve.wait_ge(s("exp_ready"), u + 1)
                    z = small[:, 128 + 2 * u:130 + 2 * u]
                    link(nc.vector.reciprocal(z, z))
                    if u < 8:
                        if u >= 2:
                            dve.wait_ge(s("turned"), u - 1)
                        link(nc.vector.tensor_tensor(z[:, 1:2], z[:, 1:2], small[:, 104:105], ALU.mult))
                        link(nc.vector.tensor_scalar(mix[:, u % 2], probs[:, u % 2, 1], z[:, 1:2], None, ALU.mult))
                        nc.vector.scalar_tensor_tensor(mix[:, u % 2], probs[:, u % 2, 0], z[:, 0:1], mix[:, u % 2],
                                                       ALU.mult, ALU.add).then_inc(s("probs_ready"), 1)
                    else:
                        for j in range(2):
                            last = nc.vector.tensor_scalar(probs[:, 2, j], probs[:, 2, j], z[:, j:j + 1], None, ALU.mult)
                        last.then_inc(s("probs_ready"), 1)

                for u in range(12):
                    maxima(u)
                    if u >= 1:
                        combine(u - 1)
                combine(11)
                dve.wait_ge(s("root_sub"), 1)
                link(nc.vector.reciprocal(small[:, 8:16], small[:, 8:16]))
                for tt in range(NT):
                    last = nc.vector.tensor_copy(rexp[:, tt, 0:2].rearrange("p k (h c) -> p (k h) c", h=2),
                                                 small[:, 8 + 4 * tt:12 + 4 * tt].unsqueeze(2).broadcast_to([P, 4, MH]))
                last.then_inc(s("rstd_sub"), 1)
                link(nc.vector.tensor_tensor(small[:, 105:106], par[:, C_SUBLN:C_SUBLN + 1], par[:, C_LINIT + 1:C_LINIT + 2], ALU.mult))
                dve.wait_ge(s("spread_sub"), 1)
                for i in range(GT):
                    link(nc.vector.scalar_tensor_tensor(cat[:, 2 * GT + i], cat[:, 2 * GT + i], small[:, 105:106],
                                                        nc_ps[7][:, i * T:(i + 1) * T], ALU.mult, ALU.mult))
                dve.wait_ge(s("pool_kept"), 1)
                dve.wait_ge(s("conv_kept"), 1)
                dve.wait_ge(s("mem_kept"), 1)
                dve.wait_ge(s("short_out"), 1)
                dve.sem_inc(s("cat_full"), 1)
                recip(64, 64 + NT * NGROUPS, "root_cat", "rstd_cat")
                dve.wait_ge(s("spread_cat"), 1)
                for k in range(KMIX):
                    g = k // GT
                    last = nc.vector.scalar_tensor_tensor(cat[:, k], cat[:, k], par[:, C_GROUP + k:C_GROUP + k + 1],
                                                          nc_ps[1 + g // 2][:, (g % 2) * T:(g % 2 + 1) * T], ALU.mult, ALU.mult)
                last.then_inc(s("cat_ready"), 1)
                for m in range(KD):
                    dve.wait_ge(s("w_used"), N_OUT + m + 1)
                    nc.vector.tensor_tensor(xT[:, m], xT[:, m], nc_ps[4 + m % 4][:, 0:T], ALU.add).then_inc(s("out_added"), 1)

                recip(80, 82, "root_ffn", "rstd_ffn")
                normed(xn, xT, par[:, C_NFFN:C_NFFN + KD], nc_ps[0][:, T:2 * T], "spread_ffn", "ffn_ready")
                dve.wait_ge(s("ffn_ready"), 1)
                link(nc.vector.tensor_copy(xr[:, 0], xn))
                link(nc.vector.tensor_tensor(xr[:, 1], xn, xr[:, 0].bitcast(F32), ALU.subtract))
                R = range(2 * PH)
                for tt in range(NT):
                    dve.wait_ge(s("score_kept"), 4 * (tt + 1))
                    sc = score[:, tt]

                    def sixteen(rows, src, spare, vals, idx):
                        for q in rows:
                            last = nc.vector.max(vals[:, q, 0:8], src[:, q])
                        link(last)
                        for q in rows:
                            nc.vector.max_index(idx[:, q, 0:8], vals[:, q, 0:8], src[:, q])
                            last = nc.vector.match_replace(spare[:, q], vals[:, q, 0:8], src[:, q], NEG)
                        link(last)
                        for q in rows:
                            last = nc.vector.max(vals[:, q, 8:16], spare[:, q])
                        link(last)
                        for q in rows:
                            last = nc.vector.max_index(idx[:, q, 8:16], vals[:, q, 8:16], spare[:, q])
                        link(last)

                    sixteen(R, sc, score2, top, topi)
                    link(nc.vector.tensor_copy(topf, topi))
                    tv = top.rearrange("p (h j) a -> p h j a", j=2)
                    link(nc.vector.tensor_tensor(cand.rearrange("p h (a b) -> p h a b", a=TOPK),
                                                 tv[:, :, 0].unsqueeze(3).broadcast_to([P, PH, TOPK, TOPK]),
                                                 tv[:, :, 1].unsqueeze(2).broadcast_to([P, PH, TOPK, TOPK]), ALU.add))
                    sixteen(range(PH), cand, cand2, best, besti)
                    link(nc.vector.tensor_tensor(cand2[:, :, 0:TOPK], best, best[:, :, 0:1].broadcast_to([P, PH, TOPK]), ALU.subtract))
                    dve.sem_inc(s("best_shifted"), 1)
                    bi = besti.rearrange("p h a -> p (h a)")
                    link(nc.vector.tensor_scalar(pick[:, 0], bi, 4, None, ALU.logical_shift_right))
                    link(nc.vector.tensor_scalar(pick[:, 1], bi, TOPK - 1, None, ALU.bitwise_and))
                    link(nc.vector.tensor_copy(pickf.rearrange("p j h a -> p j (h a)"), pick))
                    tf = topf.rearrange("p (h j) a -> p h j a", j=2)
                    for j in range(2):
                        link(nc.vector.tensor_tensor(hit, pickf[:, j].unsqueeze(3).broadcast_to([P, PH, TOPK, TOPK]),
                                                     iota[:, 0:TOPK].unsqueeze(1).unsqueeze(1).broadcast_to([P, PH, TOPK, TOPK]), ALU.is_equal))
                        link(nc.vector.tensor_tensor(hit, hit, tf[:, :, j].unsqueeze(2).broadcast_to([P, PH, TOPK, TOPK]), ALU.mult))
                        link(nc.vector.tensor_reduce(slot_t[:, tt, j].rearrange("p (h a) -> p h a", h=PH), hit, AX_X, ALU.add))
                    dve.wait_ge(s("best_exp"), tt + 1)
                    link(nc.vector.reduce_sum(gsum[:, 0:PH], cand[:, :, 0:TOPK], AX_X))
                    link(nc.vector.reciprocal(gsum[:, 0:PH], gsum[:, 0:PH]))
                    link(nc.vector.tensor_tensor(slot_t[:, tt, 2].rearrange("p (h a) -> p h a", h=PH), cand[:, :, 0:TOPK],
                                                 gsum[:, 0:PH].unsqueeze(2).broadcast_to([P, PH, TOPK]), ALU.mult))
                    dve.sem_inc(s("slots_ready"), 1)
                dve.wait_ge(s("slots_kept"), 1)
                dve.wait_ge(s("w_used"), N_ALL)

                def one_hot(g, position, free):
                    if free is not None:
                        dve.wait_ge(s("g_ready"), free)
                    for j in range(4):
                        last = nc.vector.tensor_scalar(ha[:, g, j], iota, slot[:, 0, bass.ds(position + j, 1)],
                                                       slot[:, 2, bass.ds(position + j, 1)], ALU.is_equal, ALU.mult)
                    nc.vector.tensor_tensor(hb[:, g], iota.unsqueeze(1).broadcast_to([P, 4, P]),
                                            slot[:, 1, bass.ds(position, 4)].unsqueeze(2).broadcast_to([P, 4, P]),
                                            ALU.is_equal).then_inc(s("hot_ready"), 1)

                one_hot(0, 0, None)
                one_hot(1, 4, None)
                with dve.Fori(1, T // 8) as i:
                    for g in range(2):
                        one_hot(g, i * 8 + 4 * g, i * 2 + (g - 1))
                dve.wait_ge(s("g_kept"), 2 + T // 4)


                def gated(n, tile, ready, links):
                    dve.wait_ge(s("act_used"), ready)
                    nc.vector.tensor_tensor(wgt[:, n % 2], act_e[:, n % 2], G[:, :, bass.ds(tile, 1)].squeeze(2), ALU.mult).then_inc(s("w_full"), 1)
                    dve.wait_ge(s("w_full"), links)
                    nc.vector.tensor_copy(wr[:, 0, n % 2], wgt[:, n % 2]).then_inc(s("w_high"), 1)
                    dve.wait_ge(s("w_high"), links)
                    nc.vector.tensor_tensor(wr[:, 1, n % 2], wgt[:, n % 2], wr[:, 0, n % 2].bitcast(F32), ALU.subtract).then_inc(s("wgt_ready"), 1)

                def low(k, ready):
                    dve.wait_ge(s("hi_done"), ready)
                    nc.vector.tensor_tensor(split[:, k % SPLITS, 1], wring[:, (N_ALL + k) % WSLOTS, 0:D],
                                            split[:, k % SPLITS, 0].bitcast(F32), ALU.subtract).then_inc(s("lo_done"), 1)

                low(0, 1)
                low(1, 2)
                gated(0, 0, 3, 1)
                low(2, 3)
                low(3, 4)
                with dve.Fori(0, NK // 6) as i:
                    for e in range(6):
                        gated(e + 1, i * 6 + (e + 1), i * 6 + (e + 4), i * 6 + (e + 2))
                        for k in (2 * e + 4, 2 * e + 5):
                            low(k, i * 12 + (k + 1))
                gated(NK - 1, NK - 1, NK + 2, NK)
                for tt in range(NT):
                    for c in range(2):
                        dve.wait_ge(s("peer_turned"), 2 * tt + c + 1)
                        at = xT[:, 4 * c:4 * c + 4, tt * P:(tt + 1) * P]
                        link(nc.vector.tensor_tensor(at, at, nc_ps[c][:, :].rearrange("p (a t) -> p a t", a=4), ALU.add))
                        dve.sem_inc(s("peer_added"), 1)

        nc.all_engine_barrier(sems_to_clear=s.range())


LH = 8
CTAPS = 4
RG_C = 8.0
R2 = 5
NPAIR = LH * NT
GRP = 4
LEVELS = (1, 2, 4, 8, 16, 32, 64)

Q_NORM = 0
Q_FINAL = Q_NORM + 2 * KD
Q_ADAB = Q_FINAL + KD
Q_LCW = Q_ADAB + 2 * 3 * KD
Q_LCB = Q_LCW + LH * CTAPS
Q_LGB = Q_LCB + LH
Q_LAM = Q_LGB + 2 * LH
Q_GCW = Q_LAM + LH
Q_ONORM = Q_GCW + 3 * LH * CTAPS
Q_ALOG = Q_ONORM + 1
Q_DT = Q_ALOG + LH
NPAR2 = Q_DT + LH
M_TRI, M_LEVEL = 0, P
NMASK = P + len(LEVELS) * P


def softplus(nc, dve, link, s, out, z, w):
    link(nc.vector.tensor_scalar(w[0], z, -1.0, None, ALU.mult))
    link(nc.vector.tensor_tensor(w[0], w[0], z, ALU.min))
    dve.sem_inc(s("sp_in"), 1)
    dve.wait_ge(s("sp_exp"), 1)
    link(nc.vector.tensor_scalar(w[1], w[0], 2.0, None, ALU.add))
    link(nc.vector.reciprocal(w[1], w[1]))
    link(nc.vector.tensor_tensor(w[1], w[1], w[0], ALU.mult))
    link(nc.vector.tensor_tensor(w[2], w[1], w[1], ALU.mult))
    link(nc.vector.tensor_scalar(w[3], w[2], 1.0 / 19, 1.0 / 17, ALU.mult, ALU.add))
    for n in (15, 13, 11, 9, 7, 5, 3, 1):
        link(nc.vector.tensor_tensor(w[3], w[3], w[2], ALU.mult))
        link(nc.vector.tensor_scalar(w[3], w[3], 1.0 / n, None, ALU.add))
    link(nc.vector.tensor_tensor(w[3], w[3], w[1], ALU.mult))
    link(nc.vector.tensor_scalar(w[1], z, 0.0, None, ALU.max))
    link(nc.vector.scalar_tensor_tensor(out, w[3], 2.0, w[1], ALU.mult, ALU.add))


def lru_layer(nc, ctx, m, d_in, d_gate, d_out, d_par):
    ps, xT, big, const, par, cond, ring = (m[k] for k in ("ps", "xT", "big", "const", "par2", "cond", "ring2"))
    s = Sems(nc, ctx, "r_")
    ones, ident, eps = const[:, K_ONES:K_ONES + P], const[:, K_IDENT:K_IDENT + P], const[:, K_EPS:K_EPS + 1]
    b = Region(big, NK * T)
    sq = b(KD, T)
    xn = b(KD, T)
    xpad = b(LH, T + CTAPS - 1)
    xc = b(LH, T)
    zs = b(LH, T)
    rt = b(LH, T)
    it = b(LH, T)
    at = b(LH, T)
    th = b(LH, T)
    hs = b(LH, T)
    small = b(128)
    sp = small[:, 8:16]
    w4 = [small[:, 32 + 8 * j:40 + 8 * j] for j in range(4)]
    gain = small[:, 64:72]
    NIN2 = 2 * LH
    N_G, N_O = NIN2, NIN2 + 2
    N_END = N_O + KD
    cd = cond[:, 0]

    with nc.Block() as block:
        @block.sync
        def _(sy):
            sy.dma_start(par, d_par).then_inc(s("par_loaded"), 16)
            for n in range(N_END):
                if n >= R2:
                    sy.wait_ge(s("used"), n - R2 + 1)
                src = d_in[n] if n < N_G else d_gate[n - N_G] if n < N_O else d_out[n - N_O]
                sy.dma_start(ring[n % R2], src).then_inc(s(f"loaded{n % R2}"), 16)

        @block.tensor
        def _(pe):
            def tile_of(n):
                pe.wait_ge(s(f"loaded{n % R2}"), 16 * (n // R2 + 1))
                return ring[n % R2].rearrange("p (k c) -> p k c", k=KD)

            norm_pe(nc, pe, s, ps[4], sq, small, ones, ident)
            pe.wait_ge(s("xn_ready"), KD)
            for n in range(NIN2):
                wt = tile_of(n)
                if n >= 4:
                    pe.wait_ge(s("kept"), n - 3)
                for k in range(KD):
                    last = nc.tensor.matmul(ps[n % 4][:, 0:T], wt[:, k], xn[:, k], start=(k == 0), stop=(k == KD - 1))
                last.then_inc(s("used"), 1)
            pe.wait_ge(s("kept"), NIN2)
            for n in range(LH):
                pe.wait_ge(s("convolved"), n + 1)
                for g in range(2):
                    wt = tile_of(N_G + g)
                    i = 2 * n + g
                    if i >= 8:
                        pe.wait_ge(s("gates_kept"), i - 7)
                    last = nc.tensor.matmul(ps[i % 8][:, 0:T], wt[:, n], xc[:, n], start=True, stop=True)
                    last.then_inc(s("gates"), 1)
            pe.wait_ge(s("gates_kept"), 2 * LH)
            pe.wait_ge(s("y_ready"), 1)
            pe.sem_inc(s("used"), 2)
            for mm in range(KD):
                wt = tile_of(N_O + mm)
                if mm >= 4:
                    pe.wait_ge(s("x_added"), mm - 3)
                for k in range(KD):
                    last = nc.tensor.matmul(ps[mm % 4][:, 0:T], wt[:, k], hs[:, k], start=(k == 0), stop=(k == KD - 1))
                last.then_inc(s("used"), 1)

        @block.scalar
        def _(act):
            norm_act(nc, act, s, ps[4], sq, xT, small, eps)
            modulate_act(nc, act, s, xn, cd)
            act.wait_ge(s("sp_in"), 1)
            nc.scalar.activation(w4[0], w4[0], ACT.Exp).then_inc(s("sp_exp"), 1)
            act.wait_ge(s("pads"), 1)
            for n in range(NIN2):
                act.wait_ge(s("used"), n + 1)
                if n < LH:
                    nc.scalar.copy(xpad[:, n, CTAPS - 1:], ps[n % 4][:, 0:T]).then_inc(s("kept"), 1)
                else:
                    nc.scalar.activation(zs[:, n - LH], ps[n % 4][:, 0:T], ACT.Silu).then_inc(s("kept"), 1)
            for i in range(2 * LH):
                act.wait_ge(s("gates"), i + 1)
                n, g = i // 2, i % 2
                nc.scalar.activation((rt, it)[g][:, n], ps[i % 8][:, 0:T], ACT.Sigmoid,
                                     bias=par[:, Q_LGB + g * LH + n:Q_LGB + g * LH + n + 1]).then_inc(s("gates_kept"), 1)
            act.wait_ge(s("sp_ready"), 1)
            act.wait_ge(s("gates_kept"), 2 * LH)
            for n in range(LH):
                nc.scalar.activation(at[:, n], rt[:, n], ACT.Exp, scale=small[:, 8 + n:9 + n])
                nc.scalar.activation(th[:, n], rt[:, n], ACT.Tanh, scale=small[:, 16 + n:17 + n]).then_inc(s("a_ready"), 1)
            act.wait_ge(s("m2_ready"), 1)
            nc.scalar.activation(th, th, ACT.Sqrt).then_inc(s("mult_ready"), 1)

        @block.gpsimd
        def _(pool):
            nc.gpsimd.memset(xpad, 0.0).then_inc(s("pads"), 1)
            pool.wait_ge(s("gates_kept"), 2 * LH)
            pool.wait_ge(s("convolved"), LH)
            nc.gpsimd.tensor_tensor(it, it, xc, ALU.mult).then_inc(s("ix_ready"), 1)

        @block.vector
        def _(dve):
            link = Link(dve, s("dve_link"))
            dve.wait_ge(s("par_loaded"), 16)
            link(nc.vector.tensor_tensor(cond[:, :, :], cond[:, :, :], par[:, Q_ADAB:Q_ADAB + 6 * KD].rearrange("p (l c) -> p l c", l=2), ALU.add))
            dve.sem_inc(s("cond_ready"), 1)
            norm_dve(nc, dve, link, s, ps[4], xT, xn, small, gain, par[:, Q_NORM:Q_NORM + KD], cd)
            link(nc.vector.tensor_scalar(small[:, 24:32], par[:, Q_LAM:Q_LAM + LH], -1.0, None, ALU.mult))
            softplus(nc, dve, link, s, sp, small[:, 24:32], w4)
            link(nc.vector.tensor_scalar(small[:, 16:24], sp, RG_C, None, ALU.mult))
            link(nc.vector.tensor_scalar(sp, sp, -RG_C, None, ALU.mult))
            dve.sem_inc(s("sp_ready"), 1)
            causal_conv(nc, dve, s, "kept", "convolved", LH, xpad, xc, par, Q_LCW, par[:, Q_LCB:Q_LCB + LH])
            dve.wait_ge(s("a_ready"), LH)
            link(nc.vector.tensor_tensor(hs, at, at, ALU.mult))
            link(nc.vector.scalar_tensor_tensor(flat(th), flat(hs), 1.0, flat(th), ALU.add, ALU.mult))
            dve.sem_inc(s("m2_ready"), 1)
            dve.wait_ge(s("mult_ready"), 1)
            dve.wait_ge(s("ix_ready"), 1)
            link(nc.vector.tensor_tensor(th, th, it, ALU.mult))
            for n in range(LH):
                last = nc.vector.tensor_tensor_scan(hs[:, n], at[:, n], th[:, n], 0.0, ALU.mult, ALU.add)
            link(last)
            nc.vector.tensor_tensor(hs, hs, zs, ALU.mult).then_inc(s("y_ready"), 1)
            for mm in range(KD):
                dve.wait_ge(s("used"), N_O + mm + 1)
                nc.vector.scalar_tensor_tensor(xT[:, mm], ps[mm % 4][:, 0:T], cd[:, 2 * KD + mm:2 * KD + mm + 1], xT[:, mm],
                                               ALU.mult, ALU.add).then_inc(s("x_added"), 1)
    nc.all_engine_barrier(sems_to_clear=s.range())


def flat(v):
    return v.rearrange("p a b -> p (a b)")


def causal_conv(nc, dve, s, ready, done, tiles, src, dst, par, at, bias):
    for n0 in range(0, tiles, 2):
        dve.wait_ge(s(ready), n0 + 2)
        for j in range(CTAPS):
            for n in (n0, n0 + 1):
                tap = par[:, at + n * CTAPS + j:at + n * CTAPS + j + 1]
                x = src[:, n, j:j + T]
                count = (n0 * CTAPS) + 2 * j + (n - n0) + 1
                if j == 0:
                    ins = nc.vector.tensor_scalar(dst[:, n], x, tap, 0.0 if bias is None else bias[:, n:n + 1], ALU.mult, ALU.add)
                else:
                    dve.wait_ge(s(done + "_tap"), count - 2)
                    ins = nc.vector.scalar_tensor_tensor(dst[:, n], x, tap, dst[:, n], ALU.mult, ALU.add)
                ins.then_inc(s(done + "_tap"), 1)
        for i in range(2):
            dve.wait_ge(s(done + "_tap"), (n0 + 2) * CTAPS - 1 + i)
            dve.sem_inc(s(done), 1)


def norm_pe(nc, pe, s, bank, sq, small, ones, ident):
    pe.wait_ge(s("sq_x"), 1)
    for tt in range(NT):
        for k in range(KD):
            last = nc.tensor.matmul(bank[:, tt:tt + 1], sq[:, k, tt * P:(tt + 1) * P], ones[:, 0:1], start=(k == 0), stop=(k == KD - 1))
    last.then_inc(s("sum_x"), 1)
    pe.wait_ge(s("rstd_x"), 1)
    for tt in range(NT):
        last = nc.tensor.matmul(bank[:, T + tt * P:T + (tt + 1) * P], small[:, tt:tt + 1].broadcast_to([P, P]), ident, start=True, stop=True)
    last.then_inc(s("spread_x"), 1)


def norm_act(nc, act, s, bank, sq, xT, small, eps):
    nc.scalar.activation(sq, xT, ACT.Square).then_inc(s("sq_x"), 1)
    act.wait_ge(s("sum_x"), 1)
    nc.scalar.activation(small[:, 0:NT], bank[:, 0:NT], ACT.Sqrt, scale=1.0 / D, bias=eps).then_inc(s("root_x"), 1)


def modulate_act(nc, act, s, xn, cd):
    act.wait_ge(s("cond_ready"), 1)
    for k in range(KD):
        act.wait_ge(s("scaled"), k + 1)
        nc.scalar.activation(xn[:, k], xn[:, k], ACT.Identity, bias=cd[:, k:k + 1]).then_inc(s("xn_ready"), 1)


def norm_dve(nc, dve, link, s, bank, xT, dst, small, gain, g, cd):
    if cd is not None:
        link(nc.vector.scalar_tensor_tensor(gain, cd[:, KD:2 * KD], 1.0, g, ALU.add, ALU.mult))
    else:
        gain = g
    dve.wait_ge(s("root_x"), 1)
    nc.vector.reciprocal(small[:, 0:NT], small[:, 0:NT]).then_inc(s("rstd_x"), 1)
    dve.wait_ge(s("spread_x"), 1)
    for k in range(KD):
        nc.vector.scalar_tensor_tensor(dst[:, k], xT[:, k], gain[:, k:k + 1], bank[:, T:2 * T], ALU.mult, ALU.mult).then_inc(s("scaled"), 1)


def gdn_layer(nc, ctx, m, d_in, d_ab, d_out, d_mask, out):
    ps, xT, big, const, par, cond, ring = (m[k] for k in ("ps", "xT", "big", "const", "par2", "cond", "ring2"))
    s = Sems(nc, ctx, "g_")
    ones, ident, eps = const[:, K_ONES:K_ONES + P], const[:, K_IDENT:K_IDENT + P], const[:, K_EPS:K_EPS + 1]
    b = Region(big, NK * T)
    qkv = b(3 * LH, T)
    zs = b(LH, T)
    at_pad = b.at
    pad = b(3 * LH, T + CTAPS - 1)
    end_pad = b.at
    mask = b(NMASK)
    sq = b(2 * LH, T)
    b2 = Region(big, end_pad)
    b2.at = at_pad
    kbg = b2(LH, P)
    kdec = b2(LH, P)
    eg = b2(LH, P)
    qdec = b2(LH, P)
    vb = b2(LH, NT, P)
    dec = b(LH, NT, P)
    aT = b(LH, NT, P)
    attn = b(LH, NT, P)
    xn = attn.rearrange("p h t c -> p h (t c)")
    Tm = b(LH, NT, P)
    Um = b(LH, NT, P)
    X = sq.rearrange("p (a h) t -> p a h t", a=2)[:, 0].rearrange("p h (t c) -> p h t c", t=NT)
    BT = sq.rearrange("p (a h) t -> p a h t", a=2)[:, 1].rearrange("p h (t c) -> p h t c", t=NT)
    u_ = b(LH, NT, P)
    small = m["small2"]
    wT = dec[:, :, 0]
    state = aT[:, :, 1]
    oT = Tm.rearrange("p h t c -> p h (t c)")
    osq = X.rearrange("p h t c -> p h (t c)")

    def cols(i):
        return small[:, 16 * i:16 * (i + 1)].rearrange("p (t h) -> p t h", t=NT)

    ab, bb, gg, gc, rk, rq, rb, gl, kb_s, kd_s = (cols(i) for i in range(1, 11))
    w4 = [small[:, 176 + 16 * j:192 + 16 * j].rearrange("p (t h) -> p t h", t=NT) for j in range(4)]
    gain = small[:, 240:248]
    ms = cols(16)
    beta = bb
    cd = cond[:, 1]
    tri = mask[:, M_TRI:M_TRI + P]
    wab = m["wab"]
    NQ = 4 * LH
    N_END = NQ + KD
    NG = NPAIR // GRP

    def grp(v, q):
        return v[:, 2 * q:2 * q + 2].rearrange("p h t c -> p (h t) c")

    with nc.Block() as block:
        @block.sync
        def _(sy):
            sy.dma_start(wab, d_ab.rearrange("p (k c) -> p k c", k=KD)).then_inc(s("ab_loaded"), 16)
            for n in range(N_END):
                if n >= R2:
                    sy.wait_ge(s("used"), n - R2 + 1)
                src = d_in[n] if n < NQ else d_out[n - NQ]
                sy.dma_start(ring[n % R2], src).then_inc(s(f"loaded{n % R2}"), 16)
                if n == R2 - 1:
                    sy.dma_start(mask, d_mask).then_inc(s("mask_loaded"), 16)
            for k in range(KD):
                sy.wait_ge(s("scaled"), KD + k + 1)
                sy.dma_start(out[:, k], xn[:, k]).then_inc(s("stored"), 16)
            sy.wait_ge(s("stored"), 16 * KD)

        @block.tensor
        def _(pe):
            def tile_of(n):
                pe.wait_ge(s(f"loaded{n % R2}"), 16 * (n // R2 + 1))
                return ring[n % R2].rearrange("p (k c) -> p k c", k=KD)

            norm_pe(nc, pe, s, ps[4], sq, small, ones, ident)
            pe.wait_ge(s("xn_ready"), KD)
            pe.wait_ge(s("ab_loaded"), 16)
            for tt in range(NT):
                for k in range(KD):
                    last = nc.tensor.matmul(ps[5][:, 16 * tt:16 * (tt + 1)], xn[:, k, tt * P:(tt + 1) * P], wab[:, k],
                                            start=(k == 0), stop=(k == KD - 1))
            last.then_inc(s("ab_done"), 1)
            for n in range(NQ):
                wt = tile_of(n)
                if n >= 4:
                    pe.wait_ge(s("kept"), n - 3)
                for k in range(KD):
                    last = nc.tensor.matmul(ps[n % 4][:, 0:T], wt[:, k], xn[:, k], start=(k == 0), stop=(k == KD - 1))
                last.then_inc(s("used"), 1)
                if n == LH:
                    pe.wait_ge(s("g_ready"), 1)
                    pe.wait_ge(s("mask_loaded"), 16)
                    for tt in range(NT):
                        last = nc.tensor.matmul(ps[6][:, 8 * tt:8 * (tt + 1)], tri, gg[:, tt], start=True, stop=True)
                    last.then_inc(s("gc_done"), 1)
            pe.wait_ge(s("sq_qk"), 1)
            for tt in range(NT):
                for i in range(2 * LH):
                    last = nc.tensor.matmul(ps[5][:, 32 + 16 * tt + i:33 + 16 * tt + i], sq[:, i, tt * P:(tt + 1) * P], ones[:, 0:1],
                                            start=True, stop=True)
            last.then_inc(s("sum_qk"), 1)
            pe.wait_ge(s("gc_kept"), 1)
            pe.wait_ge(s("kept"), NQ)
            for q in range(NG):
                for j in range(GRP):
                    h, tt = 2 * q + j // 2, j % 2
                    last = nc.tensor.matmul(ps[q][:, j * P:(j + 1) * P], gc[:, tt, h:h + 1].broadcast_to([P, P]), ident, start=True, stop=True)
                last.then_inc(s("g_spread"), 1)
            pe.wait_ge(s("rb_ready"), 1)
            for q in range(NG):
                if q >= 1:
                    pe.wait_ge(s("kk_used"), q)
                    pe.wait_ge(s("kq_used"), q)
                for j in range(GRP):
                    h, tt = 2 * q + j // 2, j % 2
                    kT = qkv[:, LH + h, tt * P:(tt + 1) * P]
                    nc.tensor.matmul(ps[4][:, j * P:(j + 1) * P], kT, kT, start=True, stop=True)
                    last = nc.tensor.matmul(ps[5][:, j * P:(j + 1) * P], rb[:, tt, h:h + 1].broadcast_to([P, P]), ident, start=True, stop=True)
                last.then_inc(s("kk_done"), 1)
                for j in range(GRP):
                    h, tt = 2 * q + j // 2, j % 2
                    last = nc.tensor.matmul(ps[6][:, j * P:(j + 1) * P], qkv[:, LH + h, tt * P:(tt + 1) * P],
                                            qkv[:, h, tt * P:(tt + 1) * P], start=True, stop=True)
                last.then_inc(s("kq_done"), 1)
            for q in range(NG):
                pe.wait_ge(s("g_used"), q + 1)
                if q >= 2:
                    pe.wait_ge(s("kv_kept"), q - 1)
                for c in range(2):
                    bank = ps[2 * (q % 2) + c]
                    if q == 0:
                        pe.wait_ge(s("g_used"), NG)
                    for j in range(GRP):
                        h, tt = 2 * q + j // 2, j % 2
                        last = nc.tensor.transpose(bank[:, j * P:(j + 1) * P], qkv[:, (1 + c) * LH + h, tt * P:(tt + 1) * P], ident)
                last.then_inc(s("kv_turned"), 1)
            pe.wait_ge(s("kv_kept"), NG)
            pe.wait_ge(s("kq_used"), NG)
            for v, lv in enumerate(LEVELS):
                for q in range(NG):
                    pe.wait_ge(s("bt_ready"), v * NG + q + 1)
                    if v > 0:
                        pe.wait_ge(s("inv_ready"), v * NG - NG + q + 1)
                    for j in range(GRP):
                        rhs = ident if v == 0 else grp(Tm, q)[:, j]
                        last = nc.tensor.matmul(ps[q][:, j * P:(j + 1) * P], grp(BT, q)[:, j], rhs, start=True, stop=True)
                    last.then_inc(s("x_done"), 1)
                if v == 0:
                    continue
                for q in range(NG):
                    pe.wait_ge(s("x_kept"), (v - 1) * NG + q + 1)
                    i = (v - 1) * NG + q
                    if i >= 2:
                        pe.wait_ge(s("inv_ready"), NG + i - 1)
                    for j in range(GRP):
                        last = nc.tensor.matmul(ps[4 + 2 * (q % 2)][:, j * P:(j + 1) * P], grp(X, q)[:, j], grp(Um, q)[:, j], start=True, stop=True)
                    if v < len(LEVELS) - 1:
                        for j in range(GRP):
                            last = nc.tensor.matmul(ps[5 + 2 * (q % 2)][:, j * P:(j + 1) * P], grp(Um, q)[:, j], grp(X, q)[:, j], start=True, stop=True)
                    last.then_inc(s("y_done"), 1)
            for q in range(NG):
                pe.wait_ge(s("inv_ready"), NG * len(LEVELS) - NG + q + 1)
                for j in range(GRP):
                    h, tt = 2 * q + j // 2, j % 2
                    last = nc.tensor.matmul(ps[q][:, j * P:(j + 1) * P], Um[:, h, tt], vb[:, h, tt], start=True, stop=True)
                last.then_inc(s("u_done"), 1)
            for hh in range(2):
                pe.wait_ge(s("inv_ready"), NG * len(LEVELS))
                for j in range(4):
                    h = 4 * hh + j
                    last = nc.tensor.matmul(ps[4 + hh][:, j * P:(j + 1) * P], kbg[:, h], Um[:, h, 1], start=True, stop=True)
                last.then_inc(s("wT_done"), 1)
            for hh in range(2):
                pe.wait_ge(s("u_kept"), 2 * hh + 2)
                for j in range(4):
                    h = 4 * hh + j
                    last = nc.tensor.matmul(ps[6 + hh][:, j * P:(j + 1) * P], kdec[:, h], u_[:, h, 0], start=True, stop=True)
                last.then_inc(s("state_done"), 1)
            for hh in range(2):
                pe.wait_ge(s("state_kept"), hh + 1)
                pe.wait_ge(s("wT_kept"), hh + 1)
                for j in range(4):
                    h = 4 * hh + j
                    last = nc.tensor.matmul(ps[4 + hh][:, j * P:(j + 1) * P], wT[:, h], state[:, h], start=True, stop=True)
                last.then_inc(s("wS_done"), 1)
            pe.wait_ge(s("qdec_ready"), 1)
            for q in range(NG):
                pe.wait_ge(s("vnew"), q // 2 + 1)
                for j in range(GRP):
                    h, tt = 2 * q + j // 2, j % 2
                    o = ps[q][:, j * P:(j + 1) * P]
                    if tt == 1:
                        nc.tensor.matmul(o, state[:, h], qdec[:, h], start=True, stop=False)
                    last = nc.tensor.matmul(o, u_[:, h, tt], attn[:, h, tt], start=(tt == 0), stop=True)
                last.then_inc(s("o_done"), 1)
            pe.wait_ge(s("o_sq"), 1)
            for tt in range(NT):
                for h in range(LH):
                    last = nc.tensor.matmul(ps[4][:, 8 * tt + h:8 * tt + h + 1], osq[:, h, tt * P:(tt + 1) * P], ones[:, 0:1], start=True, stop=True)
            last.then_inc(s("sum_o"), 1)
            pe.wait_ge(s("o_rstd"), 1)
            for q in range(NG):
                for j in range(GRP):
                    h, tt = 2 * q + j // 2, j % 2
                    last = nc.tensor.matmul(ps[q][:, j * P:(j + 1) * P], ms[:, tt, h:h + 1].broadcast_to([P, P]), ident, start=True, stop=True)
                last.then_inc(s("o_spread"), 1)
            pe.wait_ge(s("y_ready"), 1)
            for mm in range(KD):
                wt = tile_of(NQ + mm)
                if mm >= 4:
                    pe.wait_ge(s("x_added"), mm - 3)
                for k in range(KD):
                    last = nc.tensor.matmul(ps[4 + mm % 4][:, 0:T], wt[:, k], oT[:, k], start=(k == 0), stop=(k == KD - 1))
                last.then_inc(s("used"), 1)
            pe.wait_ge(s("sq_f"), 1)
            for tt in range(NT):
                for k in range(KD):
                    last = nc.tensor.matmul(ps[0][:, tt:tt + 1], sq[:, k, tt * P:(tt + 1) * P], ones[:, 0:1], start=(k == 0), stop=(k == KD - 1))
            last.then_inc(s("sum_f"), 1)
            pe.wait_ge(s("rstd_f"), 1)
            for tt in range(NT):
                last = nc.tensor.matmul(ps[0][:, T + tt * P:T + (tt + 1) * P], small[:, tt:tt + 1].broadcast_to([P, P]), ident, start=True, stop=True)
            last.then_inc(s("spread_f"), 1)

        @block.scalar
        def _(act):
            norm_act(nc, act, s, ps[4], sq[:, 0:KD], xT, small, eps)
            modulate_act(nc, act, s, xn, cd)
            act.wait_ge(s("sp_in"), 1)
            nc.scalar.activation(w4[0], w4[0], ACT.Exp).then_inc(s("sp_exp"), 1)
            nc.scalar.activation(small[:, 248:256], par[:, Q_ALOG:Q_ALOG + LH], ACT.Exp).then_inc(s("alog_exp"), 1)
            act.wait_ge(s("ab_kept"), 1)
            nc.scalar.activation(beta, bb, ACT.Sigmoid).then_inc(s("beta_ready"), 1)
            act.wait_ge(s("pads"), 1)
            done = 0
            for n in range(NQ):
                act.wait_ge(s("used"), n + 1)
                if n < 3 * LH:
                    nc.scalar.copy(pad[:, n, CTAPS - 1:], ps[n % 4][:, 0:T]).then_inc(s("kept"), 1)
                else:
                    nc.scalar.activation(zs[:, n - 3 * LH], ps[n % 4][:, 0:T], ACT.Silu).then_inc(s("kept"), 1)
                if n >= 4 and n % 2 == 1 and done < 3 * LH:
                    act.wait_ge(s("convolved"), done + 2)
                    nc.scalar.activation(qkv[:, done:done + 2], qkv[:, done:done + 2], ACT.Silu).then_inc(s("silu"), 2)
                    done += 2
                    if done == 2 * LH:
                        act.wait_ge(s("silu"), 2 * LH)
                        nc.scalar.activation(sq, qkv[:, 0:2 * LH], ACT.Square).then_inc(s("sq_qk"), 1)
            assert done == 3 * LH
            act.wait_ge(s("sum_qk"), 1)
            for tt in range(NT):
                nc.scalar.activation(rq[:, tt], ps[5][:, 32 + 16 * tt:40 + 16 * tt], ACT.Sqrt, bias=eps)
                last = nc.scalar.activation(rk[:, tt], ps[5][:, 40 + 16 * tt:48 + 16 * tt], ACT.Sqrt, bias=eps)
            last.then_inc(s("rqk_root"), 1)
            act.wait_ge(s("gl_in"), 1)
            nc.scalar.activation(gl, gl, ACT.Exp)
            nc.scalar.activation(kb_s, gc, ACT.Exp).then_inc(s("gl_exp"), 1)
            for q in range(NG):
                act.wait_ge(s("dec_in"), q + 1)
                nc.scalar.activation(grp(dec, q), grp(dec, q), ACT.Exp)
                for j in range(2):
                    h = 2 * q + j
                    last = nc.scalar.activation(eg[:, h], ps[q][:, (2 * j + 1) * P:(2 * j + 2) * P], ACT.Exp)
                last.then_inc(s("dec_ready"), 1)
            for q in range(NG):
                act.wait_ge(s("kv_turned"), q + 1)
                for j in range(GRP):
                    h, tt = 2 * q + j // 2, j % 2
                    if q == 0 and j == 0:
                        act.wait_ge(s("kb_ready"), 1)
                        act.wait_ge(s("beta_ready"), 1)
                    kk, scale = (kdec, kd_s) if tt == 0 else (kbg, kb_s)
                    nc.scalar.activation(kk[:, h], ps[2 * (q % 2)][:, j * P:(j + 1) * P], ACT.Copy, scale=scale[:, tt, h:h + 1])
                    last = nc.scalar.activation(vb[:, h, tt], ps[2 * (q % 2) + 1][:, j * P:(j + 1) * P], ACT.Copy, scale=beta[:, tt, h:h + 1])
                last.then_inc(s("kv_kept"), 1)
            for v in range(1, len(LEVELS)):
                for q in range(NG):
                    act.wait_ge(s("x_done"), v * NG + q + 1)
                    nc.scalar.copy(grp(X, q), ps[q][:, :].rearrange("p (a c) -> p a c", a=GRP)).then_inc(s("x_kept"), 1)
            for q in range(NG):
                act.wait_ge(s("u_done"), q + 1)
                nc.scalar.copy(grp(u_, q), ps[q][:, :].rearrange("p (a c) -> p a c", a=GRP)).then_inc(s("u_kept"), 1)
                if q >= 2:
                    hh = q - 2
                    act.wait_ge(s("wT_done"), hh + 1)
                    nc.scalar.copy(wT[:, 4 * hh:4 * hh + 4], ps[4 + hh][:, :].rearrange("p (a c) -> p a c", a=4)).then_inc(s("wT_kept"), 1)
            for hh in range(2):
                act.wait_ge(s("state_done"), hh + 1)
                nc.scalar.copy(state[:, 4 * hh:4 * hh + 4], ps[6 + hh][:, :].rearrange("p (a c) -> p a c", a=4)).then_inc(s("state_kept"), 1)
            for q in range(NG):
                act.wait_ge(s("o_done"), q + 1)
                src = ps[q][:, :].rearrange("p (h t) -> p h t", h=2)
                nc.scalar.copy(oT[:, 2 * q:2 * q + 2], src)
                last = nc.scalar.activation(osq[:, 2 * q:2 * q + 2], src, ACT.Square)
            last.then_inc(s("o_sq"), 1)
            act.wait_ge(s("ms_in"), 1)
            nc.scalar.activation(ms, ms, ACT.Sqrt, bias=eps).then_inc(s("o_root"), 1)
            act.wait_ge(s("x_added"), KD)
            nc.scalar.activation(sq[:, 0:KD], xT, ACT.Square).then_inc(s("sq_f"), 1)
            act.wait_ge(s("sum_f"), 1)
            nc.scalar.activation(small[:, 0:NT], ps[0][:, 0:NT], ACT.Sqrt, scale=1.0 / D, bias=eps).then_inc(s("root_f"), 1)

        @block.gpsimd
        def _(pool):
            nc.gpsimd.memset(pad, 0.0).then_inc(s("pads"), 1)
            pool.wait_ge(s("mask_loaded"), 16)
            for v in range(len(LEVELS)):
                mk = mask[:, M_LEVEL + v * P:M_LEVEL + (v + 1) * P]
                for q in range(NG):
                    if v == 0:
                        pool.wait_ge(s("aT_ready"), q + 1)
                    else:
                        pool.wait_ge(s("x_done"), (v - 1) * NG + q + 1)
                        if v == 1:
                            pool.wait_ge(s("inv_ready"), q + 1)
                    nc.gpsimd.tensor_tensor(grp(BT, q), grp(aT, q), mk.unsqueeze(1).broadcast_to([P, GRP, P]), ALU.mult).then_inc(s("bt_ready"), 1)

        @block.vector
        def _(dve):
            link = Link(dve, s("dve_link"))
            dve.sem_inc(s("cond_ready"), 1)
            norm_dve(nc, dve, link, s, ps[4], xT, xn, small, gain, par[:, Q_NORM + KD:Q_NORM + 2 * KD], cd)
            dve.wait_ge(s("ab_done"), 1)
            for tt in range(NT):
                nc.vector.tensor_tensor(ab[:, tt], ps[5][:, 16 * tt:16 * tt + 8], par[:, Q_DT:Q_DT + LH], ALU.add)
                last = nc.vector.tensor_copy(bb[:, tt], ps[5][:, 16 * tt + 8:16 * tt + 16])
            link(last)
            dve.sem_inc(s("ab_kept"), 1)
            softplus(nc, dve, link, s, gg, ab, w4)
            dve.wait_ge(s("alog_exp"), 1)
            for tt in range(NT):
                last = nc.vector.scalar_tensor_tensor(gg[:, tt], gg[:, tt], -1.0, small[:, 248:256], ALU.mult, ALU.mult)
            last.then_inc(s("g_ready"), 1)
            causal_conv(nc, dve, s, "kept", "convolved", 3 * LH, pad, qkv, par, Q_GCW, None)
            dve.wait_ge(s("gc_done"), 1)
            nc.vector.tensor_copy(gc, ps[6][:, 0:16].rearrange("p (t h) -> p t h", t=NT)).then_inc(s("gc_kept"), 1)
            dve.wait_ge(s("rqk_root"), 1)
            nc.vector.reciprocal(rq, rq)
            link(nc.vector.reciprocal(rk, rk))
            dve.wait_ge(s("beta_ready"), 1)
            link(nc.vector.tensor_scalar(rq, rq, float(P) ** -0.5, None, ALU.mult))
            nc.vector.tensor_tensor(rb, rk, beta, ALU.mult).then_inc(s("rb_ready"), 1)
            dve.wait_ge(s("rb_ready"), 1)
            dve.wait_ge(s("g_spread"), NG)
            for q in range(NG):
                for j in range(GRP):
                    h, tt = 2 * q + j // 2, j % 2
                    last = nc.vector.tensor_tensor(gl[:, tt, h:h + 1], ps[q][:, (j + 1) * P - 1:(j + 1) * P], gc[:, tt, h:h + 1], ALU.subtract)
            link(last)
            dve.sem_inc(s("gl_in"), 1)
            for q in range(NG):
                for j in range(GRP):
                    h, tt = 2 * q + j // 2, j % 2
                    last = nc.vector.tensor_scalar(dec[:, h, tt], ps[q][:, j * P:(j + 1) * P], gc[:, tt, h:h + 1], 0.0, ALU.subtract, ALU.min)
                last.then_inc(s("dec_in"), 1)
            dve.wait_ge(s("gl_exp"), 1)
            nc.vector.tensor_tensor(kb_s, kb_s, rb, ALU.mult)
            link(nc.vector.tensor_tensor(kd_s, gl, rk, ALU.mult))
            dve.sem_inc(s("kb_ready"), 1)
            for q in range(NG):
                dve.wait_ge(s("dec_ready"), q + 1)
                dve.sem_inc(s("g_used"), 1)
                dve.wait_ge(s("kk_done"), q + 1)
                for j in range(GRP):
                    h, tt = 2 * q + j // 2, j % 2
                    last = nc.vector.scalar_tensor_tensor(aT[:, h, tt], ps[4][:, j * P:(j + 1) * P], rk[:, tt, h:h + 1], dec[:, h, tt], ALU.mult, ALU.mult)
                link(last)
                link(nc.vector.tensor_tensor(grp(aT, q), grp(aT, q), ps[5][:, :].rearrange("p (a c) -> p a c", a=GRP), ALU.mult))
                dve.sem_inc(s("aT_ready"), 1)
                dve.sem_inc(s("kk_used"), 1)
                dve.wait_ge(s("kq_done"), q + 1)
                for j in range(GRP):
                    h, tt = 2 * q + j // 2, j % 2
                    last = nc.vector.scalar_tensor_tensor(attn[:, h, tt], ps[6][:, j * P:(j + 1) * P], rk[:, tt, h:h + 1], dec[:, h, tt], ALU.mult, ALU.mult)
                link(last)
                dve.sem_inc(s("kq_used"), 1)
                last = nc.vector.tensor_tensor(grp(attn, q), grp(attn, q), tri.unsqueeze(1).broadcast_to([P, GRP, P]), ALU.mult)
            link(last)
            for v in range(len(LEVELS)):
                for q in range(NG):
                    idb = ident.unsqueeze(1).broadcast_to([P, GRP, P])
                    if v == 0:
                        dve.wait_ge(s("x_done"), q + 1)
                        nc.vector.tensor_tensor(grp(Um, q), idb, grp(BT, q), ALU.subtract)
                        nc.vector.tensor_tensor(grp(Tm, q), idb, ps[q][:, :].rearrange("p (a c) -> p a c", a=GRP), ALU.subtract).then_inc(s("inv_ready"), 1)
                    else:
                        dve.wait_ge(s("y_done"), (v - 1) * NG + q + 1)
                        if v < len(LEVELS) - 1:
                            nc.vector.tensor_tensor(grp(Tm, q), grp(Tm, q), ps[5 + 2 * (q % 2)][:, :].rearrange("p (a c) -> p a c", a=GRP), ALU.subtract)
                        nc.vector.tensor_tensor(grp(Um, q), grp(Um, q), ps[4 + 2 * (q % 2)][:, :].rearrange("p (a c) -> p a c", a=GRP), ALU.subtract).then_inc(s("inv_ready"), 1)
                if v == 0:
                    nc.vector.tensor_tensor(qdec, qkv[:, 0:LH, P:2 * P], eg, ALU.mult).then_inc(s("qdec_ready"), 1)
            dve.wait_ge(s("u_kept"), NG)
            for hh in range(2):
                dve.wait_ge(s("wS_done"), hh + 1)
                sl = u_[:, 4 * hh:4 * hh + 4, 1]
                nc.vector.tensor_tensor(sl, sl, ps[4 + hh][:, :].rearrange("p (a c) -> p a c", a=4), ALU.subtract).then_inc(s("vnew"), 1)
            dve.wait_ge(s("sum_o"), 1)
            link(nc.vector.tensor_tensor(ms, ps[4][:, 0:16].rearrange("p (t h) -> p t h", t=NT), rq, ALU.mult))
            link(nc.vector.scalar_tensor_tensor(ms, ms, 1.0 / P, rq, ALU.mult, ALU.mult))
            dve.sem_inc(s("ms_in"), 1)
            dve.wait_ge(s("o_root"), 1)
            link(nc.vector.reciprocal(ms, ms))
            nc.vector.tensor_tensor(ms, ms, rq, ALU.mult).then_inc(s("o_rstd"), 1)
            link(nc.vector.tensor_tensor(zs, zs, oT, ALU.mult))
            for q in range(NG):
                dve.wait_ge(s("o_spread"), q + 1)
                last = nc.vector.scalar_tensor_tensor(flat(oT[:, 2 * q:2 * q + 2]), flat(zs[:, 2 * q:2 * q + 2]), par[:, Q_ONORM:Q_ONORM + 1],
                                                      ps[q][:, :], ALU.mult, ALU.mult)
            last.then_inc(s("y_ready"), 1)
            for mm in range(KD):
                dve.wait_ge(s("used"), NQ + mm + 1)
                nc.vector.scalar_tensor_tensor(xT[:, mm], ps[4 + mm % 4][:, 0:T], cd[:, 2 * KD + mm:2 * KD + mm + 1], xT[:, mm],
                                               ALU.mult, ALU.add).then_inc(s("x_added"), 1)
            dve.wait_ge(s("root_f"), 1)
            nc.vector.reciprocal(small[:, 0:NT], small[:, 0:NT]).then_inc(s("rstd_f"), 1)
            dve.wait_ge(s("spread_f"), 1)
            for k in range(KD):
                nc.vector.scalar_tensor_tensor(xn[:, k], xT[:, k], par[:, Q_FINAL + k:Q_FINAL + k + 1], ps[0][:, T:2 * T],
                                               ALU.mult, ALU.mult).then_inc(s("scaled"), 1)


def build(nc, a, out):
    ctx = ExitStack()
    with ctx:
        def sb(name, size, dt=F32):
            return ctx.enter_context(nc.sbuf_tensor(name, [P, size], dt))

        m = {"big": sb("big", NK * T), "wring_": sb("weight_ring", WSLOTS * WSIZE), "const": sb("constants", NKEEP),
             "work": sb("work", 4 * T), "xT_": sb("x_t", KD * T), "zeros": sb("zeros", P, BF16)}
        m["wring"] = m["wring_"][:, :].rearrange("p (s c) -> p s c", s=WSLOTS)
        m["xr"] = sb("x_parts", 2 * KD * T, F32R)[:, :].rearrange("p (a k t) -> p a k t", a=2, k=KD)
        m["wr"] = sb("weight_parts", 2 * 2 * T, F32R)[:, :].rearrange("p (a n t) -> p a n t", a=2, n=2)
        m["split"] = sb("chunk_parts", SPLITS * 2 * D, F32R)[:, :].rearrange("p (s a c) -> p s a c", s=SPLITS, a=2)
        m["xT"] = m["xT_"][:, :].rearrange("p (k t) -> p k t", k=KD)
        m["cond"] = m["const"][:, K_COND:K_COND + 2 * NCOND].rearrange("p (l c) -> p l c", l=2)
        m["ring2"] = [m["wring_"][:, i * D:(i + 1) * D] for i in range(R2)]
        m["par2"] = m["work"][:, 0:NPAR2]
        m["small2"] = m["work"][:, 256:256 + 272]
        m["wab"] = m["work"][:, 640:640 + KD * 2 * LH].rearrange("p (k c) -> p k c", k=KD)
        m["ps"] = [ctx.enter_context(nc.psum_tensor(f"bank{i}", [P, 512], F32)) for i in range(8)]
        loaded = ctx.enter_context(nc.semaphore("start_loaded"))
        stored = ctx.enter_context(nc.semaphore("stored"))
        with nc.Block() as block:
            @block.sync
            def _(sp):
                sp.dma_start(m["xT"], a["x"]).then_inc(loaded, 16)
                sp.dma_start(m["const"][:, 0:NCONST], a["const"]).then_inc(loaded, 16)
                sp.dma_start(m["const"][:, K_CACT:NKEEP], a["c"]).then_inc(loaded, 16)

            @block.scalar
            def _(act):
                act.wait_ge(loaded, 48)
                cact = m["const"][:, K_CACT:NKEEP]
                nc.scalar.activation(cact, cact, ACT.Silu).then_inc(stored, 1)
                act.wait_ge(stored, 1)
        with ExitStack() as part:
            first_block(nc, part, m, [a[k] for k in ("w_in", "w_kv", "w_out", "wq", "sub", "par", "xc", "mem", "experts", "ada")])
        with ExitStack() as part:
            lru_layer(nc, part, m, a["lru_in"], a["lru_gate"], a["lru_out"], a["par2"])
        with ExitStack() as part:
            gdn_layer(nc, part, m, a["gdn_in"], a["gdn_ab"], a["gdn_out"], a["mask"], out)


def columns(w):
    *lead, k, n = w.shape
    v = w.reshape(*lead, k // P, P, n // P, P)
    v = np.moveaxis(v, -2, -4)
    v = np.swapaxes(v, -3, -2)
    return np.ascontiguousarray(v).reshape(*lead, n // P, P, k // P * P)


def per_channel(v):
    return np.swapaxes(v.reshape(v.shape[0], -1, P), 1, 2)


def constants():
    c = np.zeros((P, NCONST), np.float32)
    c[:, K_ONES:K_ONES + P] = 1.0
    c[:, K_IDENT:K_IDENT + P] = np.eye(P)
    c[:, K_IOTA:K_IOTA + P] = np.arange(P)
    c[np.arange(P), K_BD32 + np.arange(P) // DH] = 1.0
    c[np.arange(P), K_BD64 + np.arange(P) // MH] = 1.0
    c[:, K_EPS] = EPS
    x = np.zeros((P, NXC), np.float32)
    t = np.arange(T)
    for g, w in enumerate(POOL_WINDOWS):
        n = np.clip(t + w // 2, 0, T) - np.clip(t - w // 2, 0, T)
        rows = slice(64 * (g % 2), 64 * (g % 2 + 1))
        x[rows, X_INV + (g // 2) * T:X_INV + (g // 2 + 1) * T] = 1.0 / n
    for q in range(NT):
        x[:, X_DIST + q * T:X_DIST + (q + 1) * T] = np.abs((q * P + np.arange(P))[:, None] - t[None])
    return c, x


def layout(i):
    L = LAYERS
    f = {k: np.asarray(v) for k, v in i.items()}
    a = {}
    a["x"] = np.ascontiguousarray(f["x"][0].T.reshape(KD, P, T).transpose(1, 0, 2))
    a["mem"] = np.ascontiguousarray(f["mem"][0].T.reshape(KD, P, T).transpose(1, 0, 2))
    a["const"], a["xc"] = constants()
    a["w_in"] = columns(f["w_in"])
    a["w_kv"] = columns(f["w_mem_kv"])
    a["w_out"] = columns(f["w_out"])
    a["wq"] = columns(f["peer_wq"])
    sub = f["peer_subkeys"].reshape(L, 2, 8, NK, P).transpose(0, 1, 4, 2, 3)
    a["sub"] = np.ascontiguousarray(sub).reshape(L, 2, P, 8 * NK)
    u = f["peer_u"].reshape(L, NK, NK, KD, P).transpose(0, 2, 4, 3, 1).reshape(L, NK, P, D)
    v = f["peer_v"].reshape(L, NK, NK, D).transpose(0, 2, 1, 3)
    e = np.empty((L, NE, P, D), np.float32)
    e[:, 0], e[:, 1:NE - 1:2] = u[:, 0], u[:, 1:]
    e[:, 2:NE:2], e[:, NE - 1] = v[:, 0:NK - 1], v[:, NK - 1]
    a["experts"] = e
    p = np.zeros((L, P, NPAR), np.float32)
    p[:, :, C_NMIX:C_NMIX + KD] = per_channel(f["norm_mix"])
    p[:, :, C_NMEM:C_NMEM + KD] = per_channel(f["mem_norm"])
    p[:, :, C_NFFN:C_NFFN + KD] = per_channel(f["norm_ffn"])
    p[:, :, C_GROUP:C_GROUP + KMIX] = per_channel(f["group_norm"])
    for name, at, taps in (("conv_dw", C_CONV, TAPS), ("sconv_w", C_SCONV, SHORT)):
        w = f[name].transpose(0, 2, 1).reshape(L, GT, P, taps).transpose(0, 2, 1, 3)
        p[:, :, at:at + GT * taps] = w.reshape(L, P, GT * taps)
    p[:, :, C_LNG:C_LNG + GT] = per_channel(f["conv_ln_g"])
    p[:, :, C_LNB:C_LNB + GT] = per_channel(f["conv_ln_b"])
    for j in range(2):
        p[:, :, C_QG + j] = np.tile(f["diff_qk_norm"][:, j], (1, P // DH))
        p[:, :, C_QG + 2 + j] = np.tile(f["mem_qk_norm"][:, j], (1, P // MH))
    p[:, :, C_PSCALE:C_PSCALE + GT] = per_channel(f["pool_scale"])
    p[:, :, C_SUBLN] = np.tile(f["diff_subln"], (1, P // MH))
    for l in range(L):
        start = 0.8 - 0.6 * np.exp(-0.3 * l)
        p[l, :, C_LINIT] = start
        p[l, :, C_LINIT + 1] = 1.0 - start
    p[:, :, C_LAM:C_LAM + 4 * DH] = f["diff_lambda"].reshape(L, 1, 4 * DH)
    for g in range(4):
        rows = slice(64 * (g % 2), 64 * (g % 2 + 1))
        at = C_POOLW + (g // 2) * P + 64 * (g % 2)
        p[:, rows, at:at + 64] = f["pool_w"][:, g]
    p[:, :, C_PW:C_PW + GT * GW] = f["conv_pw"].reshape(L, GT, P, GW).transpose(0, 2, 1, 3).reshape(L, P, GT * GW)
    a["par"] = p
    a["c"] = np.ascontiguousarray(f["c_2"].reshape(KD, P).T)
    a["ada"] = columns(f["ada_w_2"])
    a["lru_in"] = columns(f["lru_in_w_2"][0])
    a["lru_out"] = columns(f["lru_out_w_2"][0])
    a["lru_gate"] = np.ascontiguousarray(f["lru_gate_w_2"][0].transpose(0, 2, 1, 3)).reshape(2, P, LH * P)
    gin = f["gdn_in_w_2"][0]
    a["gdn_in"] = columns(np.ascontiguousarray(gin[:, 0:4 * D]))
    a["gdn_ab"] = np.ascontiguousarray(gin[:, 4 * D:].reshape(KD, P, 2 * LH).transpose(1, 0, 2)).reshape(P, KD * 2 * LH)
    a["gdn_out"] = columns(f["gdn_out_w_2"][0])
    q = np.zeros((P, NPAR2), np.float32)
    for l in range(2):
        q[:, Q_NORM + l * KD:Q_NORM + (l + 1) * KD] = f["norm_g_2"][l].reshape(KD, P).T
        q[:, Q_ADAB + l * 3 * KD:Q_ADAB + (l + 1) * 3 * KD] = f["ada_b_2"][l].reshape(3 * KD, P).T
    q[:, Q_FINAL:Q_FINAL + KD] = f["final_g_2"].reshape(KD, P).T
    q[:, Q_LCW:Q_LCW + LH * CTAPS] = f["lru_conv_w_2"][0].reshape(CTAPS, LH, P).transpose(2, 1, 0).reshape(P, LH * CTAPS)
    q[:, Q_LCB:Q_LCB + LH] = f["lru_conv_b_2"][0].reshape(LH, P).T
    q[:, Q_LGB:Q_LGB + 2 * LH] = f["lru_gate_b_2"][0].reshape(2 * LH, P).T
    q[:, Q_LAM:Q_LAM + LH] = f["lru_lambda_2"][0].reshape(LH, P).T
    q[:, Q_GCW:Q_GCW + 3 * LH * CTAPS] = f["gdn_conv_w_2"][0].reshape(CTAPS, 3 * LH, P).transpose(2, 1, 0).reshape(P, 3 * LH * CTAPS)
    q[:, Q_ONORM] = f["gdn_onorm_g_2"][0]
    q[:, Q_ALOG:Q_ALOG + LH] = f["gdn_a_log_2"][0]
    q[:, Q_DT:Q_DT + LH] = f["gdn_dt_bias_2"][0]
    a["par2"] = q
    mask = np.zeros((P, NMASK), np.float32)
    j, i = np.arange(P)[:, None], np.arange(P)[None]
    mask[:, M_TRI:M_TRI + P] = j <= i
    for v, lv in enumerate(LEVELS):
        block = (i // (2 * lv) == j // (2 * lv)) & ((i // lv) % 2 == 1) & ((j // lv) % 2 == 0)
        mask[:, M_LEVEL + v * P:M_LEVEL + (v + 1) * P] = block
    a["mask"] = mask
    return a


def kernel(**inputs):
    import concourse.bacc as bacc
    from concourse.bass_utils import run_bass_kernel_spmd

    arrays = layout(inputs)
    nc = bacc.Bacc("TRN2", target_bir_lowering=False, num_devices=1)
    dram = {k: nc.dram_tensor(f"in_{k}", v.shape, mybir.dt.from_np(v.dtype), kind="ExternalInput").ap() for k, v in arrays.items()}
    out = nc.dram_tensor("out", (P, KD, T), F32, kind="ExternalOutput").ap()
    build(nc, dram, out)
    r = run_bass_kernel_spmd(nc, [{f"in_{k}": v for k, v in arrays.items()}], core_ids=[0])
    y = np.asarray(r.results[0]["out"])
    return np.ascontiguousarray(y.transpose(2, 1, 0)).reshape(1, T, D)
```

```python
import numpy as np
import concourse.bass as bass
from concourse import mybir
from contextlib import ExitStack

F32 = mybir.dt.float32
U32 = mybir.dt.uint32
F32R = mybir.dt.float32r
BF16 = mybir.dt.bfloat16
ALU = mybir.AluOpType
ACT = mybir.ActivationFunctionType
AX_X = mybir.AxisListType.X

P = 128
D = 1024
KD = D // P
T = 256
NT = T // P
LAYERS = 2
GW = 256
GT = GW // P
NGROUPS = 5
NIN = 20
NPROJ = 24
KMIX = NGROUPS * GT
TAPS = 31
SHORT = 3
DH = 32
MH = 64
HEADS = 4
PH = 8
NK = 128
TOPK = 16
SLOTS = PH * TOPK
EPS = 1e-6
WSLOTS = 4
WSIZE = KMIX * P
SPLITS = 3
XN_AT = NK * T - KD * T
NEG = -3.4028235e38
POOL_WINDOWS = (2, 4, 8, 16)
PADC = TAPS // 2
PADP = 8
HC = 128

C_NMIX, C_NMEM, C_NFFN, C_GROUP = 0, 8, 16, 24
C_CONV = 34
C_SCONV = C_CONV + GT * TAPS
C_LNG = C_SCONV + GT * SHORT
C_LNB = C_LNG + GT
C_QG = C_LNB + GT
C_PSCALE = C_QG + 4
C_SUBLN = C_PSCALE + GT
C_LINIT = C_SUBLN + 1
C_LAM = C_LINIT + 2
C_POOLW = C_LAM + 4 * DH
C_PW = C_POOLW + GT * P
NPAR = C_PW + GT * GW

K_ONES, K_IDENT, K_IOTA, K_BD32, K_BD64, K_EPS = 0, 128, 256, 384, 388, 390
NCONST = 392
K_COND = NCONST
NKEEP = K_COND + 2 * 24
X_INV, X_DIST = 0, GT * T
NXC = X_DIST + NT * T

ORDER = [2, 3, 4, 5, 0, 1, 12, 13, 14, 15, 16, 17, 6, 7, 8, 9, 10, 11, 18, 19]
N_A, N_GATE, N_POOL, N_SH, N_SB, N_SC, N_Q, N_K, N_V, N_MQ, N_MK, N_MV = 0, 2, 4, 6, 8, 10, 12, 14, 16, 18, 20, 22
POSITION_MAJOR = (N_V, N_V + 1, N_MV, N_MV + 1)
N_CONV_MEAN, N_POOL_OUT, N_CONV_VAR = 18, 20, 22
N_OUT = NPROJ
N_WQ = N_OUT + KD
N_ALL = N_WQ + 2 * PH
NCOND = 3 * KD
NPART = 16
ADA_PLACE = [0] * 4 + [n % 3 for n in range(NCOND - 4)]
ADA_EARLY = {8: 0, 18: 1, 20: 2, 22: 3}
ADA_LATE = {N_OUT + WSLOTS + i: NCOND - 5 + i for i in range(5)}
NE = 2 * NK
E_HOT = 2
assert (N_ALL + E_HOT) % WSLOTS == 2


class Link:

    def __init__(self, engine, sem):
        self.engine, self.sem, self.n = engine, sem, 0

    def __call__(self, instruction):
        instruction.then_inc(self.sem, 1)
        self.n += 1
        self.engine.wait_ge(self.sem, self.n)


class Sems:

    def __init__(self, nc, ctx, prefix):
        self.nc, self.ctx, self.prefix, self.by, self.nums = nc, ctx, prefix, {}, []

    def __call__(self, name):
        if name not in self.by:
            self.by[name] = self.ctx.enter_context(self.nc.semaphore(self.prefix + name))
            self.nums.append(self.by[name].num)
        return self.by[name]

    def range(self):
        low, high = min(self.nums), max(self.nums)
        assert high - low + 1 == len(self.nums)
        return range(low, high + 1)


class Region:

    def __init__(self, tensor, size):
        self.tensor, self.size, self.at = tensor, size, 0

    def __call__(self, *shape):
        n = int(np.prod(shape))
        view = self.tensor[:, self.at:self.at + n]
        self.at += n
        assert self.at <= self.size, (self.at, self.size)
        if len(shape) == 2:
            return view.rearrange("p (a b) -> p a b", a=shape[0])
        if len(shape) == 3:
            return view.rearrange("p (a b c) -> p a b c", a=shape[0], b=shape[1])
        if len(shape) == 4:
            return view.rearrange("p (a b c d) -> p a b c d", a=shape[0], b=shape[1], c=shape[2])
        return view


def first_block(nc, ctx, mem_, ins):
    nc_ps = mem_["ps"]
    xT, xr, big, wring, split, wr, const, work = (mem_[k] for k in ("xT", "xr", "big", "wring", "split", "wr", "const", "work"))
    d_w_in, d_w_kv, d_w_out, d_wq, d_sub, d_par, d_xc, d_mem, d_e, d_ada, d_c = ins
    xn = big[:, XN_AT:].rearrange("p (k t) -> p k t", k=KD)
    s = Sems(nc, ctx, "m_")
    ones = const[:, K_ONES:K_ONES + P]
    ident = const[:, K_IDENT:K_IDENT + P]
    iota = const[:, K_IOTA:K_IOTA + P]
    ones_bf = const[:, 0:T].bitcast(BF16)
    bd32 = const[:, K_BD32:K_BD32 + HEADS]
    bd64 = const[:, K_BD64:K_BD64 + 2]
    eps = const[:, K_EPS:K_EPS + 1]
    cond = mem_["cond"]

    b = Region(big, XN_AT)
    par = b(NPAR)
    xc = b(NXC)
    memT = b(KD, T)
    memn = b(KD, T)
    sq = b(KD, T)
    proj = b(NPROJ, T)
    cat = b(KMIX, T)
    hpad = b(GT, T + 2 * PADC)
    ppad = b(3, GT, T + 2 * PADP)
    spad = b(GT, T + 2)
    conv = b(2, GT, T)
    qk = b(KD, T)
    scores = b(2, 2, T)
    probs = b(3, 2, T)
    mix = b(2, T)
    pT = b(2 * HEADS, NT, T)
    rms = mix
    rms_g = [proj[:, i] for i in (10, 12, 14, 11, 13)]
    inv = xc[:, X_INV:X_INV + GT * T].rearrange("p (a t) -> p a t", a=GT)
    dist = xc[:, X_DIST:X_DIST + NT * T].rearrange("p (a t) -> p a t", a=NT)
    small = b(256)
    adap = b(NCOND, NPART)
    cact = memT.rearrange("p k t -> p (k t)")[:, 0:D]
    ada = [memT.rearrange("p k t -> p (k t)")[:, D:]] + [memn.rearrange("p k t -> p (k t)")[:, i * D:(i + 1) * D] for i in range(2)]
    rexp = sq.rearrange("p k t -> p (k t)").rearrange("p (t k c) -> p t k c", t=NT, k=KD)
    r = Region(big, XN_AT)
    r.at = C_NFFN + KD
    query = r(2 * PH, T)
    score = r(4, NT * 2, NK)
    spare = r(NT * 2, NK)
    topf = r(NT, PH, 2, TOPK)
    ex = r(NT * PH, TOPK)
    gsum = r(NT * PH)
    assert r.at <= KD * KD * P
    r.at = KD * KD * P
    sub = r(2 * PH, NK)
    cand = r(2, NT, TOPK * TOPK)
    cand2 = r(NT, TOPK * TOPK)
    top = r(NT, PH, 2, TOPK)
    topi = r(NT, PH, 2, TOPK).bitcast(U32)
    best = r(NT, PH, TOPK)
    besti = r(NT, PH, TOPK).bitcast(U32)
    pick = r(2, NT * SLOTS).bitcast(U32)
    pickf = r(2, NT, PH, TOPK)
    hit = [r(PH, TOPK, TOPK) for i in range(2 * NT)]
    slot_t = r(NT, 3, SLOTS)
    w = Region(work, 4 * T)
    slot = w(3, T)
    w.at = 0
    act_e = w(2, T)
    wgt = w(2, T)
    hot = Region(mem_["wring_"], WSLOTS * WSIZE + P * 2)
    hot.at = WSIZE + D
    ha = hot(4, 4, P)
    hb = hot(2, 4, P)
    GROUPS = T // 4
    ROUND = 4
    out_e = big[:, 0:D]
    G = big[:, :].rearrange("p (t k) -> p t k", t=T)

    def lam_slopes(h):
        return 2.0 ** (-8.0 * (h + 1) / HEADS)

    def w_source(l, n):
        if n < NIN:
            return d_w_in[l, ORDER[n]]
        if n < N_OUT:
            return d_w_kv[l, n - NIN]
        if n < N_WQ:
            return d_w_out[l, n - N_OUT]
        return d_wq[l, n - N_WQ]

    cat_sq = proj[:, 0:KMIX]

    def transposes(pe, u):
        pe.wait_ge(s("probs_ready"), u + 1)
        if u >= 1:
            pe.wait_ge(s("pT_ready"), u)
        for j in range(2 if u < 8 else 4):
            if u < 8:
                src, at = mix[:, u % 2, j * P:(j + 1) * P], j
            else:
                src, at = probs[:, 2, j // 2, (j % 2) * P:(j % 2 + 1) * P], j
            last = nc.tensor.transpose(nc_ps[0][:, at * P:(at + 1) * P], src, ident)
        last.then_inc(s("turned"), 1)

    def turn_evacuate(act, u):
        act.wait_ge(s("turned"), u + 1)
        if u < 8:
            h, qt = u // 2, u % 2
            nc.scalar.copy(pT[:, h, :, qt * P:(qt + 1) * P],
                           nc_ps[0][:, 0:2 * P].rearrange("p (k q) -> p k q", k=NT)).then_inc(s("pT_ready"), 1)
        else:
            h = HEADS + u - 8
            nc.scalar.copy(pT[:, h].rearrange("p k (t q) -> p t k q", t=NT),
                           nc_ps[0][:, 0:4 * P].rearrange("p (t k q) -> p t k q", t=NT, k=NT)).then_inc(s("pT_ready"), 1)

    with nc.Fori(0, LAYERS) as l:
        with nc.Block() as block:

            @block.sync
            def _(sp):
                def load_ada(n):
                    if ADA_PLACE[n] in ADA_PLACE[:n]:
                        sp.wait_ge(s("ada_used"), n - ADA_PLACE[n - 1::-1].index(ADA_PLACE[n]))
                    sp.dma_start(ada[ADA_PLACE[n]], d_ada[l, n]).then_inc(s(f"ada_loaded{ADA_PLACE[n]}"), 16)

                sp.dma_start(par, d_par[l]).then_inc(s("par_loaded"), 16)
                for n in range(N_ALL):
                    if n >= WSLOTS:
                        sp.wait_ge(s("w_used"), n - WSLOTS + 1)
                    src = w_source(l, n)
                    sp.dma_start(wring[:, n % WSLOTS, 0:src.shape[1]], src).then_inc(s(f"w_loaded{n % WSLOTS}"), 16)
                    if n == 0:
                        sp.dma_start(memT, d_mem).then_inc(s("mem_loaded"), 16)
                        sp.dma_start(xc, d_xc).then_inc(s("par_loaded"), 16)
                    if n == 8:
                        sp.wait_ge(s("memn_ready"), KD)
                        sp.dma_start(cact, d_c).then_inc(s("c_loaded"), 16)
                    if n in ADA_EARLY:
                        load_ada(ADA_EARLY[n])
                    if n in ADA_LATE:
                        load_ada(ADA_LATE[n])
                    if n == N_OUT + WSLOTS - 1:
                        for j in range(len(ADA_EARLY), NCOND - len(ADA_LATE)):
                            load_ada(j)
                        sp.wait_ge(s("sum_diff"), 1)
                        sp.dma_start(sub[:, 0:PH], d_sub[l, 0].rearrange("p (m c) -> p m c", m=PH)).then_inc(s("sub_loaded"), 16)
                        sp.dma_start(sub[:, PH:], d_sub[l, 1].rearrange("p (m c) -> p m c", m=PH)).then_inc(s("sub_loaded"), 16)
                for k in range(WSLOTS):
                    sp.wait_ge(s("w_used"), N_ALL + k - WSLOTS + 1)
                    if k == E_HOT:
                        sp.wait_ge(s("g_ready"), 4 + GROUPS)
                    sp.dma_start(wring[:, (N_ALL + k) % WSLOTS, 0:D], d_e[l, k]).then_inc(s(f"w_loaded{(N_ALL + k) % WSLOTS}"), 16)
                with sp.Fori(0, NE // WSLOTS - 1) as i:
                    for e in range(WSLOTS):
                        sp.wait_ge(s("lo_done"), i * WSLOTS + (e + 1))
                        sp.dma_start(wring[:, (N_ALL + e) % WSLOTS, 0:D], d_e[l, i * WSLOTS + (e + WSLOTS)]).then_inc(s(f"w_loaded{(N_ALL + e) % WSLOTS}"), 16)

            @block.tensor
            def _(pe):
                def w_tile(n):
                    pe.wait_ge(s(f"w_loaded{n % WSLOTS}"), 16 * (n // WSLOTS + 1))
                    return wring[:, n % WSLOTS]

                def sums(out, src, tiles, columns=ones[:, 0:1]):
                    for tt in range(NT):
                        for i in range(tiles):
                            last = nc.tensor.matmul(out[:, tt], src[:, i, tt * P:(tt + 1) * P], columns,
                                                    start=(i == 0), stop=(i == tiles - 1))
                    return last

                def spread(out, col):
                    for tt in range(NT):
                        last = nc.tensor.matmul(out[:, tt * P:(tt + 1) * P], col[:, tt].broadcast_to([P, P]), ident, start=True, stop=True)
                    return last

                def total(out, src, ready, first=0, tiles=KD, opened=True, closed=True):
                    for i in range(first, first + tiles):
                        if ready is not None:
                            pe.wait_ge(s(ready), i + 1)
                        last = nc.tensor.matmul(out, ones, src[:, i], start=(opened and i == first), stop=(closed and i == first + tiles - 1))
                    return last

                total(nc_ps[4][:, 0:T], sq, "sq_x").then_inc(s("sum_x"), 1)
                total(nc_ps[5][:, 0:T], sq, "sq_mem").then_inc(s("sum_mem"), 1)
                for n in range(NPROJ):
                    if n == NIN:
                        pe.wait_ge(s("memn_ready"), KD)
                    if n == N_CONV_MEAN:
                        pe.wait_ge(s("conv_done"), 1)
                        sums(nc_ps[6][:, 0:2].rearrange("p (t c) -> p t c", t=NT), conv[:, 0], GT).then_inc(s("sum_conv"), 1)
                        pe.wait_ge(s("mean_conv"), 1)
                        spread(nc_ps[6][:, T:2 * T], small[:, 4:6].rearrange("p (t c) -> p t c", t=NT)).then_inc(s("spread_mean"), 1)
                    if n == N_POOL_OUT:
                        pe.wait_ge(s("pooled"), 1)
                        for i in range(GT):
                            last = nc.tensor.matmul(nc_ps[5][:, i * T:(i + 1) * T], par[:, C_POOLW + i * P:C_POOLW + (i + 1) * P],
                                                    ppad[:, 0, i, 0:T], start=True, stop=True)
                        last.then_inc(s("pool_out"), 1)
                    if n == N_CONV_VAR:
                        pe.wait_ge(s("centred"), 1)
                        sums(nc_ps[7][:, 0:2].rearrange("p (t c) -> p t c", t=NT), conv[:, 0], GT).then_inc(s("sum_var"), 1)
                        pe.wait_ge(s("rstd_conv"), 1)
                        spread(nc_ps[7][:, T:2 * T], small[:, 6:8].rearrange("p (t c) -> p t c", t=NT)).then_inc(s("spread_var"), 1)
                    src = xn if n < NIN else memn
                    wt = w_tile(n)[:, 0:D].rearrange("p (k c) -> p k c", k=KD)
                    if n >= 4:
                        pe.wait_ge(s("proj_kept"), n - 3)
                    out = nc_ps[n % 4]
                    if n in POSITION_MAJOR:
                        for tt in range(NT):
                            for k in range(KD):
                                last = nc.tensor.matmul(out[:, tt * P:(tt + 1) * P], src[:, k, tt * P:(tt + 1) * P], wt[:, k],
                                                        start=(k == 0), stop=(k == KD - 1))
                    else:
                        for k in range(KD):
                            if n == 0:
                                pe.wait_ge(s("xn_ready"), k + 1)
                            last = nc.tensor.matmul(out[:, 0:T], wt[:, k], src[:, k], start=(k == 0), stop=(k == KD - 1))
                    last.then_inc(s("w_used"), 1)
                pe.wait_ge(s("sq_qk"), 1)
                pe.wait_ge(s("proj_kept"), NPROJ)
                qs = nc_ps[0][:, 0:NT * 24].rearrange("p (t c) -> p t c", t=NT)
                for i in range(KD):
                    c, m, cols = (4 * i, HEADS, bd32) if i < 4 else (16 + 2 * (i - 4), 2, bd64)
                    for tt in range(NT):
                        last = nc.tensor.matmul(qs[:, tt, c:c + m], sq[:, i, tt * P:(tt + 1) * P], cols, start=True, stop=True)
                last.then_inc(s("sum_qk"), 1)
                pe.wait_ge(s("sq_early"), 1)
                for i, g in enumerate((0, 3)):
                    last = total(nc_ps[1][:, i * T:(i + 1) * T], cat_sq, None, GT * g, GT)
                last.then_inc(s("sum_early"), 1)
                pe.wait_ge(s("rstd_qk"), 1)
                pe.wait_ge(s("conv_normed"), 1)
                pe.wait_ge(s("pool_kept"), 1)
                for i in range(KD):
                    last = spread(nc_ps[4 + i // 2][:, (i % 2) * T:(i % 2 + 1) * T], rexp[:, :, i])
                last.then_inc(s("spread_qk"), 1)
                pe.wait_ge(s("qk_ready"), 1)
                for u in range(12):
                    if u >= 4:
                        pe.wait_ge(s("scores_used"), u - 3)
                    out = nc_ps[4 + u % 4]
                    for j in range(2):
                        if u < 8:
                            h, qt = u // 2, u % 2
                            rows = slice(DH * h, DH * (h + 1))
                            last = nc.tensor.matmul(out[:, j * T:(j + 1) * T], qk[rows, j, qt * P:(qt + 1) * P], qk[rows, 2 + j],
                                                    start=True, stop=True)
                        else:
                            h = u - 8
                            rows = slice(MH * (h % 2), MH * (h % 2 + 1))
                            last = nc.tensor.matmul(out[:, j * T:(j + 1) * T], qk[rows, 4 + h // 2, j * P:(j + 1) * P],
                                                    qk[rows, 6 + h // 2], start=True, stop=True)
                    last.then_inc(s("scores_ready"), 1)
                    if u >= 3:
                        transposes(pe, u - 3)
                for u in range(9, 12):
                    transposes(pe, u)
                pe.wait_ge(s("conv_silu"), 1)
                pe.wait_ge(s("pT_ready"), 12)
                for i in range(GT):
                    for k in range(GT):
                        last = nc.tensor.matmul(nc_ps[0][:, i * T:(i + 1) * T], par[:, C_PW + k * GW + i * P:C_PW + k * GW + (i + 1) * P],
                                                conv[:, 1, k], start=(k == 0), stop=(k == GT - 1))
                last.then_inc(s("conv_out"), 1)
                for a in range(2):
                    for h in range(HEADS):
                        rows = slice(MH * (h % 2), MH * (h % 2 + 1))
                        vt = proj[:, (N_V if a == 0 else N_MV) + h // 2]
                        for kt in range(NT):
                            last = nc.tensor.matmul(nc_ps[2 + a][rows, (h // 2) * T:(h // 2 + 1) * T],
                                                    vt[:, kt * P + MH * (h % 2):kt * P + MH * (h % 2 + 1)],
                                                    pT[:, a * HEADS + h, kt], start=(kt == 0), stop=(kt == NT - 1))
                    last.then_inc(s("attn_out"), 1)
                pe.wait_ge(s("sq_sub"), 1)
                ss = nc_ps[6][:, 0:8].rearrange("p (t c) -> p t c", t=NT)
                for tt in range(NT):
                    for i in range(GT):
                        last = nc.tensor.matmul(ss[:, tt, 2 * i:2 * i + 2], sq[:, i, tt * P:(tt + 1) * P], bd64, start=True, stop=True)
                last.then_inc(s("sum_sub"), 1)
                pe.wait_ge(s("sq_late"), 1)
                pe.wait_ge(s("root_early"), 1)
                for i, g in enumerate((1, 4)):
                    last = total(nc_ps[1][:, i * T:(i + 1) * T], cat_sq, None, GT * g, GT)
                last.then_inc(s("sum_late"), 1)
                pe.wait_ge(s("rstd_sub"), 1)
                for i in range(GT):
                    last = spread(nc_ps[7][:, i * T:(i + 1) * T], rexp[:, :, i])
                last.then_inc(s("spread_sub"), 1)
                pe.wait_ge(s("sq_diff"), 1)
                total(nc_ps[6][:, T:2 * T], cat_sq, None, GT * 2, GT).then_inc(s("sum_diff"), 1)
                order = [GT * g + i for g in (0, 3, 1, 4, 2) for i in range(GT)]
                for m in range(KD):
                    wt = w_tile(N_OUT + m)[:, 0:WSIZE].rearrange("p (k c) -> p k c", k=KMIX)
                    if m >= 4:
                        pe.wait_ge(s("out_added"), m - 3)
                    for i, k in enumerate(order):
                        if m == 0 and i % GT == 0:
                            pe.wait_ge(s("cat_ready"), i // (2 * GT) + 1)
                        last = nc.tensor.matmul(nc_ps[4 + m % 4][:, 0:T], wt[:, k], cat[:, k], start=(i == 0), stop=(i == KMIX - 1))
                    last.then_inc(s("w_used"), 1)
                    if m >= 1:
                        total(nc_ps[0][:, 0:T], sq, "sq_ffn", m - 1, 1, m == 1, False)

                total(nc_ps[0][:, 0:T], sq, "sq_ffn", KD - 1, 1, False, True).then_inc(s("sum_ffn"), 1)

                def key_scores(h):
                    pe.wait_ge(s("query_kept"), 2 * h + 2)
                    if h >= 4:
                        pe.wait_ge(s("score_kept"), h - 3)
                    for tt in range(NT):
                        for j in range(2):
                            last = nc.tensor.matmul(nc_ps[4 + h % 4][:, (2 * tt + j) * P:(2 * tt + j + 1) * P],
                                                    query[:, 2 * h + j, tt * P:(tt + 1) * P], sub[:, 2 * h + j], start=True, stop=True)
                    last.then_inc(s("score_ready"), 1)

                for m in range(2 * PH):
                    wt = w_tile(N_WQ + m)[:, 0:D].rearrange("p (k c) -> p k c", k=KD)
                    if m >= 4:
                        pe.wait_ge(s("query_kept"), m - 3)
                    for k in range(KD):
                        if m == 0:
                            pe.wait_ge(s("ffn_ready"), k + 1)
                        last = nc.tensor.matmul(nc_ps[m % 4][:, 0:T], wt[:, k], xn[:, k], start=(k == 0), stop=(k == KD - 1))
                    last.then_inc(s("w_used"), 1)
                    if m == 2:
                        pe.wait_ge(s("sub_loaded"), 32)
                    if m >= 2 and m % 2 == 0:
                        key_scores(m // 2 - 1)
                key_scores(PH - 1)
                for tt in range(NT):
                    pe.wait_ge(s("slots_ready"), tt + 1)
                    for j in range(3):
                        last = nc.tensor.transpose(nc_ps[j][:, tt * P:(tt + 1) * P], slot_t[:, tt, j], ident)
                    last.then_inc(s("slots_turned"), 1)

                def gate_products(g, count):
                    pe.wait_ge(s("first_gated"), count)
                    pe.wait_ge(s("second_hot"), count)
                    pe.wait_ge(s("g_kept"), count)
                    for j in range(4):
                        last = nc.tensor.matmul(nc_ps[g % 2][:, j * P:(j + 1) * P], ha[:, g % 4, j], hb[:, g % 2, j], start=True, stop=True)
                    last.then_inc(s("g_ready"), 1)

                with pe.Fori(0, GROUPS // ROUND) as i:
                    for g in range(ROUND):
                        gate_products(g, i * ROUND + (g + 1))

                pe.wait_ge(s("g_kept"), 2 + T // 4)
                pe.wait_ge(s("zeros"), 1)
                for tt in range(NT):
                    for c in range(2):
                        nc.tensor.matmul(nc_ps[4 + 2 * tt + c][:, 0:512], mem_["zeros"][:, 0:P], ones_bf,
                                         start=True, stop=False, skip_group_check=True)

                def up(n, k, ready, wait_free):
                    pe.wait_ge(s("lo_done"), ready)
                    if wait_free is not None:
                        pe.wait_ge(s("act_used"), wait_free)
                    hi, lo = split[:, k % SPLITS, 0], split[:, k % SPLITS, 1]
                    for j in range(KD):
                        for a, x in ((hi, 0), (hi, 1), (lo, 0)):
                            last = nc.tensor.matmul(nc_ps[2 + n % 2][:, 0:T], a[:, j * P:(j + 1) * P], xr[:, x, j],
                                                    start=(j == 0 and a is hi and x == 0), stop=(j == KD - 1 and a is lo))
                    last.then_inc(s("split_used"), 1)

                def down(n, k, ready, wgt_, stop=False):
                    pe.wait_ge(s("lo_done"), ready)
                    pe.wait_ge(s("wgt_ready"), wgt_)
                    hi, lo = split[:, k % SPLITS, 0], split[:, k % SPLITS, 1]
                    for tt in range(NT):
                        for x, v in ((0, hi), (0, lo), (1, hi)):
                            for c in range(2):
                                last = nc.tensor.matmul(nc_ps[4 + 2 * tt + c][:, 0:512], wr[:, x, n % 2, tt * P:(tt + 1) * P],
                                                        v[:, c * 512:(c + 1) * 512], start=False, stop=stop and x == 1, skip_group_check=True)
                    last.then_inc(s("split_used"), 1)

                up(0, 0, 1, None)
                with pe.Fori(0, NK // 6) as i:
                    for e in range(6):
                        up(e + 1, 2 * e + 1, i * 12 + (2 * e + 2), i * 6 + (e + 2))
                        down(e, 2 * e + 2, i * 12 + (2 * e + 3), i * 6 + (e + 1))
                for n in range(NK // 6 * 6, NK):
                    if n + 1 < NK:
                        up(n + 1, 2 * n + 1, 2 * n + 2, n + 2)
                    k = min(2 * n + 2, NE - 1)
                    down(n, k, k + 1, n + 1, n == NK - 1)
                for tt in range(NT):
                    for k in range(KD):
                        if k % 4 == 0:
                            pe.wait_ge(s("peer_kept"), tt + 1)
                            if tt > 0:
                                pe.wait_ge(s("peer_added"), k // 4 + 1)
                        last = nc.tensor.transpose(nc_ps[k // 4][:, (k % 4) * P:(k % 4 + 1) * P], out_e[:, k * P:(k + 1) * P], ident)
                        if k % 4 == 3:
                            last.then_inc(s("peer_turned"), 1)

            @block.scalar
            def _(act):

                def root(src, dst, n, width, ready, done):
                    act.wait_ge(s(ready), 1)
                    nc.scalar.activation(dst, src, ACT.Sqrt, scale=1.0 / width, bias=eps).then_inc(s(done), 1)

                def squares(src, done, ready=None):
                    for k in range(KD):
                        if ready is not None:
                            act.wait_ge(s(ready), k + 1)
                        nc.scalar.activation(sq[:, k], src[:, k], ACT.Square).then_inc(s(done), 1)

                squares(xT, "sq_x")
                root(nc_ps[4][:, 0:T], rms[:, 0], T, D, "sum_x", "root_x")
                act.wait_ge(s("mem_loaded"), 16)
                squares(memT, "sq_mem")
                root(nc_ps[5][:, 0:T], rms[:, 1], T, D, "sum_mem", "root_mem")
                for n in range(NPROJ):
                    if n == N_CONV_MEAN:
                        act.wait_ge(s("sum_conv"), 1)
                        nc.scalar.mul(small[:, 4:6], nc_ps[6][:, 0:2], 1.0 / GW).then_inc(s("mean_conv"), 1)
                    if n == N_CONV_VAR:
                        act.wait_ge(s("pool_out"), 1)
                        for i in range(GT):
                            last = nc.scalar.activation(cat[:, i], nc_ps[5][:, i * T:(i + 1) * T], ACT.Copy,
                                                        scale=par[:, C_PSCALE + i:C_PSCALE + i + 1])
                        last.then_inc(s("pool_kept"), 1)
                        root(nc_ps[7][:, 0:2], small[:, 6:8], 2, GW, "sum_var", "root_conv")
                    act.wait_ge(s("w_used"), n + 1)
                    nc.scalar.copy(proj[:, n], nc_ps[n % 4][:, 0:T]).then_inc(s("proj_kept"), 1)
                    if n == NIN // 2:
                        act.wait_ge(s("c_loaded"), 16)
                        nc.scalar.activation(cact, cact, ACT.Silu).then_inc(s("cact_ready"), 1)
                    if n == N_GATE + 1:
                        act.wait_ge(s("proj_kept"), N_GATE + 2)
                        nc.scalar.activation(proj[:, N_GATE:N_GATE + 2], proj[:, N_GATE:N_GATE + 2], ACT.Sigmoid).then_inc(s("gate_ready"), 1)
                act.wait_ge(s("proj_kept"), NPROJ)
                nc.scalar.activation(sq[:, 0:4], proj[:, N_Q:N_Q + 4], ACT.Square)
                nc.scalar.activation(sq[:, 4:8], proj[:, N_MQ:N_MQ + 4], ACT.Square).then_inc(s("sq_qk"), 1)
                act.wait_ge(s("pool_kept"), 1)
                act.wait_ge(s("short_out"), 1)
                nc.scalar.activation(cat_sq[:, 0:GT], cat[:, 0:GT], ACT.Square)
                nc.scalar.activation(cat_sq[:, 3 * GT:4 * GT], cat[:, 3 * GT:4 * GT], ACT.Square).then_inc(s("sq_early"), 1)
                act.wait_ge(s("sum_qk"), 1)
                qs = nc_ps[0][:, 0:NT * 24].rearrange("p (t c) -> p t c", t=NT)
                rq = small[:, 16:16 + NT * 24].rearrange("p (t c) -> p t c", t=NT)
                nc.scalar.activation(rq[:, :, 0:16], qs[:, :, 0:16], ACT.Sqrt, scale=1.0 / DH, bias=eps)
                nc.scalar.activation(rq[:, :, 16:24], qs[:, :, 16:24], ACT.Sqrt, scale=1.0 / MH, bias=eps).then_inc(s("root_qk"), 1)
                act.wait_ge(s("sum_early"), 1)
                for i, g in enumerate((0, 3)):
                    last = nc.scalar.activation(rms_g[g], nc_ps[1][:, i * T:(i + 1) * T], ACT.Sqrt, scale=1.0 / GW, bias=eps)
                last.then_inc(s("root_early"), 1)
                act.wait_ge(s("conv_normed"), 1)
                for i in range(GT):
                    last = nc.scalar.activation(conv[:, 1, i], conv[:, 0, i], ACT.Silu, scale=par[:, C_LNG + i:C_LNG + i + 1],
                                                bias=par[:, C_LNB + i:C_LNB + i + 1])
                last.then_inc(s("conv_silu"), 1)
                act.wait_ge(s("lam_sums"), 1)
                nc.scalar.activation(small[:, 100:102], small[:, 102:104], ACT.Exp).then_inc(s("lam_exp"), 1)
                for u in range(12):
                    act.wait_ge(s("max_ready"), u + 1)
                    slot_ = u % 2 if u < 8 else 2
                    if u >= 2 and u < 8:
                        act.wait_ge(s("probs_ready"), u - 1)
                    if u >= 9:
                        act.wait_ge(s("turned"), u)
                    for j in range(2):
                        src = scores[:, u % 2, j] if u < 8 else nc_ps[4 + u % 4][:, j * T:(j + 1) * T]
                        c = 112 + 2 * (u % 4) + j
                        last = nc.scalar.activation(probs[:, slot_, j], src, ACT.Exp, bias=small[:, c:c + 1],
                                                    scale=(DH if u < 8 else MH) ** -0.5, accum_out=small[:, 128 + 2 * u + j:129 + 2 * u + j])
                    last.then_inc(s("exp_ready"), 1)
                    if u >= 1:
                        turn_evacuate(act, u - 1)
                turn_evacuate(act, 11)
                act.wait_ge(s("conv_out"), 1)
                nc.scalar.copy(cat[:, GT:2 * GT], nc_ps[0][:, 0:GT * T].rearrange("p (a t) -> p a t", a=GT)).then_inc(s("conv_kept"), 1)
                act.wait_ge(s("attn_out"), 1)
                nc.scalar.copy(cat[:, 2 * GT:3 * GT], nc_ps[2][:, 0:GT * T].rearrange("p (a t) -> p a t", a=GT))
                nc.scalar.activation(sq[:, 0:GT], nc_ps[2][:, 0:GT * T].rearrange("p (a t) -> p a t", a=GT), ACT.Square).then_inc(s("sq_sub"), 1)
                act.wait_ge(s("attn_out"), 2)
                nc.scalar.copy(cat[:, 4 * GT:5 * GT], nc_ps[3][:, 0:GT * T].rearrange("p (a t) -> p a t", a=GT)).then_inc(s("mem_kept"), 1)
                act.wait_ge(s("conv_kept"), 1)
                nc.scalar.activation(cat_sq[:, GT:2 * GT], cat[:, GT:2 * GT], ACT.Square)
                act.wait_ge(s("mem_kept"), 1)
                nc.scalar.activation(cat_sq[:, 4 * GT:5 * GT], cat[:, 4 * GT:5 * GT], ACT.Square).then_inc(s("sq_late"), 1)
                act.wait_ge(s("sum_sub"), 1)
                nc.scalar.activation(small[:, 8:16], nc_ps[6][:, 0:8], ACT.Sqrt, scale=1.0 / MH, bias=eps).then_inc(s("root_sub"), 1)
                act.wait_ge(s("sum_late"), 1)
                for i, g in enumerate((1, 4)):
                    last = nc.scalar.activation(rms_g[g], nc_ps[1][:, i * T:(i + 1) * T], ACT.Sqrt, scale=1.0 / GW, bias=eps)
                last.then_inc(s("root_late"), 1)
                act.wait_ge(s("diff_scaled"), 1)
                nc.scalar.activation(cat_sq[:, 2 * GT:3 * GT], cat[:, 2 * GT:3 * GT], ACT.Square).then_inc(s("sq_diff"), 1)
                root(nc_ps[6][:, T:2 * T], rms_g[2], T, GW, "sum_diff", "root_diff")

                squares(xT, "sq_ffn", "out_added")
                root(nc_ps[0][:, 0:T], rms[:, 0], T, D, "sum_ffn", "root_ffn")
                act.wait_ge(s("ffn_ready"), KD)
                act.wait_ge(s("ada_summed"), 1)
                nc.scalar.copy(cond[:, bass.ds(l, 1)].squeeze(1), adap[:, :, 0])
                for m in range(2 * PH):
                    act.wait_ge(s("w_used"), N_WQ + m + 1)
                    nc.scalar.copy(query[:, m], nc_ps[m % 4][:, 0:T]).then_inc(s("query_kept"), 1)
                    if (m >= 2 and m % 2 == 0) or m == 2 * PH - 1:
                        h = m // 2 - 1 if m % 2 == 0 else PH - 1
                        act.wait_ge(s("score_ready"), h + 1)
                        if h >= 4:
                            act.wait_ge(s("score_used"), h - 3)
                        nc.scalar.copy(score[:, h % 4], nc_ps[4 + h % 4][:, :].rearrange("p (a c) -> p a c", a=2 * NT)).then_inc(s("score_kept"), 1)
                act.wait_ge(s("best_shifted"), 1)
                nc.scalar.activation(ex, ex, ACT.Exp).then_inc(s("best_exp"), 1)
                act.wait_ge(s("slots_turned"), NT)
                for j in range(3):
                    last = nc.scalar.copy(slot[:, j], nc_ps[j][:, 0:T])
                last.then_inc(s("slots_kept"), 1)
                act.wait_ge(s("slots_kept"), 1)
                act.sem_inc(s("g_kept"), 2)
                with act.Fori(0, T // 8) as i:
                    for g in range(2):
                        act.wait_ge(s("g_ready"), i * 2 + (g + 5))
                        nc.scalar.copy(G[:, bass.ds(i * 8 + 4 * g, 4)], nc_ps[g][:, :].rearrange("p (a c) -> p a c", a=4)).then_inc(s("g_kept"), 1)

                def high(k, slot_, loaded, free):
                    act.wait_ge(s(f"w_loaded{slot_}"), loaded)
                    if free is not None:
                        act.wait_ge(s("split_used"), free)
                    nc.scalar.copy(split[:, k % SPLITS, 0], wring[:, slot_, 0:D]).then_inc(s("hi_done"), 1)

                def gelu(n, used):
                    act.wait_ge(s("split_used"), used)
                    nc.scalar.activation(act_e[:, n % 2], nc_ps[2 + n % 2][:, 0:T], ACT.Gelu).then_inc(s("act_used"), 1)

                act.sem_inc(s("act_used"), 2)
                for n in range(2):
                    if n == 1:
                        gelu(0, 1)
                    for k in (2 * n, 2 * n + 1):
                        high(k, (N_ALL + k) % WSLOTS, 16 * ((N_ALL + k) // WSLOTS + 1), k - 2 if k > 2 else None)
                with act.Fori(0, NK // 6) as i:
                    for e in range(6):
                        gelu(e + 1, i * 12 + (2 * e + 2))
                        for k in (2 * e + 4, 2 * e + 5):
                            high(k, (N_ALL + k) % WSLOTS, (i * 3 + ((N_ALL + k) // WSLOTS + 1)) * 16, i * 12 + (k - 2))
                gelu(NK - 1, 2 * (NK - 1))
                for tt in range(NT):
                    act.wait_ge(s("split_used"), NE)
                    if tt > 0:
                        act.wait_ge(s("peer_turned"), 2 * tt)
                    for c in range(2):
                        last = nc.scalar.copy(out_e[:, c * 512:(c + 1) * 512], nc_ps[4 + 2 * tt + c][:, :])
                    last.then_inc(s("peer_kept"), 1)

            @block.gpsimd
            def _(pool):
                link = Link(pool, s("pool_link"))
                nc.gpsimd.memset(hpad, 0.0)
                nc.gpsimd.memset(spad, 0.0)
                nc.gpsimd.memset(ppad, 0.0).then_inc(s("pads"), 1)
                nc.gpsimd.memset(mem_["zeros"][:, :], 0.0).then_inc(s("zeros"), 1)
                pool.wait_ge(s("pads"), 1)
                pool.wait_ge(s("proj_kept"), N_POOL + 2)
                link(nc.gpsimd.tensor_copy(ppad[:, 0, :, PADP:PADP + T], proj[:, N_POOL:N_POOL + 2]))
                W_ = T + 2 * PADP
                link(nc.gpsimd.tensor_tensor(ppad[:, 1, :, 1:W_], ppad[:, 0, :, 0:W_ - 1], ppad[:, 0, :, 1:W_], ALU.add))
                link(nc.gpsimd.tensor_tensor(ppad[:, 2, :, 1:W_ - 1], ppad[:, 1, :, 0:W_ - 2], ppad[:, 1, :, 2:W_], ALU.add))
                nc.gpsimd.tensor_copy(ppad[0:64, 0, 0, 0:T], ppad[0:64, 1, 0, PADP:PADP + T])
                link(nc.gpsimd.tensor_copy(ppad[64:128, 0, 0, 0:T], ppad[64:128, 2, 0, PADP:PADP + T]))
                link(nc.gpsimd.tensor_tensor(ppad[:, 1, 1, 3:W_ - 3], ppad[:, 2, 1, 1:W_ - 5], ppad[:, 2, 1, 5:W_ - 1], ALU.add))
                nc.gpsimd.tensor_copy(ppad[0:64, 0, 1, 0:T], ppad[0:64, 1, 1, PADP:PADP + T])
                link(nc.gpsimd.tensor_tensor(ppad[64:128, 0, 1, 0:T], ppad[64:128, 1, 1, PADP - 4:PADP - 4 + T],
                                             ppad[64:128, 1, 1, PADP + 4:PADP + 4 + T], ALU.add))
                link(nc.gpsimd.tensor_tensor(ppad[:, 0, :, 0:T], ppad[:, 0, :, 0:T], inv, ALU.mult))
                nc.gpsimd.tensor_tensor(ppad[:, 0, :, 0:T], ppad[:, 0, :, 0:T], proj[:, N_POOL:N_POOL + 2], ALU.subtract).then_inc(s("pooled"), 1)
                pool.wait_ge(s("proj_kept"), N_SC + 2)
                nc.gpsimd.tensor_tensor(spad[:, :, 1:1 + T], proj[:, N_SC:N_SC + 2], proj[:, N_SH:N_SH + 2], ALU.mult).then_inc(s("short_in"), 1)
                pool.wait_ge(s("cact_ready"), 1)
                for n in range(NCOND):
                    w_, at = ada[ADA_PLACE[n]], ADA_PLACE[n]
                    pool.wait_ge(s(f"ada_loaded{at}"), 16 * ADA_PLACE[:n + 1].count(at))
                    link(nc.gpsimd.tensor_tensor(w_, w_, cact, ALU.mult))
                    width = D // 2
                    while width > NPART:
                        link(nc.gpsimd.tensor_tensor(w_[:, 0:width], w_[:, 0:width], w_[:, width:2 * width], ALU.add))
                        width //= 2
                    nc.gpsimd.tensor_tensor(adap[:, n], w_[:, 0:NPART], w_[:, NPART:2 * NPART], ALU.add).then_inc(s("ada_used"), 1)
                pool.wait_ge(s("ada_used"), NCOND)
                width = NPART // 2
                while width > 1:
                    link(nc.gpsimd.tensor_tensor(adap[:, :, 0:width], adap[:, :, 0:width], adap[:, :, width:2 * width], ALU.add))
                    width //= 2
                nc.gpsimd.tensor_tensor(adap[:, :, 0], adap[:, :, 0], adap[:, :, 1], ALU.add).then_inc(s("ada_summed"), 1)

                for h in range(PH):
                    pool.wait_ge(s("halves_done"), h + 1)
                    if h >= 2:
                        pool.wait_ge(s("cand_used"), h - 1)
                    nc.gpsimd.tensor_tensor(cand[:, h % 2].rearrange("p t (a b) -> p t a b", a=TOPK),
                                            top[:, :, h, 0].unsqueeze(3).broadcast_to([P, NT, TOPK, TOPK]),
                                            top[:, :, h, 1].unsqueeze(2).broadcast_to([P, NT, TOPK, TOPK]), ALU.add).then_inc(s("cand_ready"), 1)
                for i in range(2 * NT - 1):
                    pool.wait_ge(s("hit_ready"), i + 1)
                    nc.gpsimd.tensor_tensor(hit[i], hit[i], topf[:, i // 2, :, i % 2].unsqueeze(2).broadcast_to([P, PH, TOPK, TOPK]),
                                            ALU.mult).then_inc(s("hit_keyed"), 1)

                def gate_rows(g, position, count):
                    pool.wait_ge(s("first_hot"), count)
                    nc.gpsimd.tensor_tensor(ha[:, g % 4], ha[:, g % 4], slot[:, 2, bass.ds(position, 4)].unsqueeze(2).broadcast_to([P, 4, P]),
                                            ALU.mult).then_inc(s("first_gated"), 1)

                with pool.Fori(0, GROUPS // ROUND) as i:
                    for g in range(ROUND):
                        gate_rows(g, i * (4 * ROUND) + 4 * g, i * ROUND + (g + 1))

            @block.vector
            def _(dve):
                link = Link(dve, s("dve_link"))

                def recip(v, ready, done):
                    dve.wait_ge(s(ready), 1)
                    nc.vector.reciprocal(v, v).then_inc(s(done), 1)

                def normed(dst, src, gain, rms_, ready, done):
                    dve.wait_ge(s(ready), 1)
                    for k in range(KD):
                        nc.vector.scalar_tensor_tensor(dst[:, k], src[:, k], gain[:, k:k + 1], rms_, ALU.mult, ALU.mult).then_inc(s(done), 1)

                def grouped(groups, done):
                    for g in groups:
                        for k in (GT * g, GT * g + 1):
                            last = nc.vector.scalar_tensor_tensor(cat[:, k], cat[:, k], par[:, C_GROUP + k:C_GROUP + k + 1], rms_g[g],
                                                                  ALU.mult, ALU.mult)
                    last.then_inc(s(done), 1)

                recip(rms[:, 0], "root_x", "rstd_x")
                dve.wait_ge(s("par_loaded"), 32)
                normed(xn, xT, par[:, C_NMIX:C_NMIX + KD], rms[:, 0], "rstd_x", "xn_ready")
                recip(rms[:, 1], "root_mem", "rstd_mem")
                normed(memn, memT, par[:, C_NMEM:C_NMEM + KD], rms[:, 1], "rstd_mem", "memn_ready")
                for j in range(2):
                    a = C_LAM + 2 * DH * j
                    link(nc.vector.tensor_tensor(small[:, 192:192 + DH], par[:, a:a + DH], par[:, a + DH:a + 2 * DH], ALU.mult))
                    link(nc.vector.reduce_sum(small[:, 102 + j:103 + j], small[:, 192:192 + DH], AX_X))
                dve.sem_inc(s("lam_sums"), 1)
                dve.wait_ge(s("gate_ready"), 1)
                dve.wait_ge(s("pads"), 1)
                link(nc.vector.tensor_tensor(hpad[:, :, PADC:PADC + T], proj[:, N_A:N_A + 2], proj[:, N_GATE:N_GATE + 2], ALU.mult))
                for k in range(TAPS):
                    for i in range(GT):
                        tap = par[:, C_CONV + i * TAPS + k:C_CONV + i * TAPS + k + 1]
                        src = hpad[:, i, k:k + T]
                        if k == 0:
                            nc.vector.tensor_scalar(conv[:, 0, i], src, tap, None, ALU.mult).then_inc(s("conv_tap"), 1)
                        else:
                            dve.wait_ge(s("conv_tap"), GT * (k - 1) + i + 1)
                            nc.vector.scalar_tensor_tensor(conv[:, 0, i], src, tap, conv[:, 0, i], ALU.mult, ALU.add).then_inc(s("conv_tap"), 1)
                dve.wait_ge(s("conv_tap"), GT * TAPS)
                dve.sem_inc(s("conv_done"), 1)
                dve.wait_ge(s("short_in"), 1)
                for k in range(SHORT):
                    for i in range(GT):
                        tap = par[:, C_SCONV + i * SHORT + k:C_SCONV + i * SHORT + k + 1]
                        src = spad[:, i, k:k + T]
                        if k == 0:
                            last = nc.vector.tensor_scalar(cat[:, 3 * GT + i], src, tap, None, ALU.mult)
                        else:
                            last = nc.vector.scalar_tensor_tensor(cat[:, 3 * GT + i], src, tap, cat[:, 3 * GT + i], ALU.mult, ALU.add)
                    link(last)
                dve.wait_ge(s("proj_kept"), N_SB + 2)
                nc.vector.tensor_tensor(cat[:, 3 * GT:4 * GT], cat[:, 3 * GT:4 * GT], proj[:, N_SB:N_SB + 2], ALU.mult).then_inc(s("short_out"), 1)
                dve.wait_ge(s("spread_mean"), 1)
                for i in range(GT):
                    link(nc.vector.tensor_tensor(conv[:, 1, i], conv[:, 0, i], nc_ps[6][:, T:2 * T], ALU.subtract))
                nc.vector.tensor_tensor(conv[:, 0], conv[:, 1], conv[:, 1], ALU.mult).then_inc(s("centred"), 1)
                recip(small[:, 6:8], "root_conv", "rstd_conv")
                dve.wait_ge(s("spread_var"), 1)
                for i in range(GT):
                    last = nc.vector.tensor_tensor(conv[:, 0, i], conv[:, 1, i], nc_ps[7][:, T:2 * T], ALU.mult)
                last.then_inc(s("conv_normed"), 1)
                dve.wait_ge(s("root_qk"), 1)
                link(nc.vector.reciprocal(small[:, 16:16 + NT * 24], small[:, 16:16 + NT * 24]))
                rq = small[:, 16:16 + NT * 24].rearrange("p (t c) -> p t c", t=NT)
                for tt in range(NT):
                    nc.vector.tensor_copy(rexp[:, tt, 0:4].rearrange("p k (h c) -> p (k h) c", h=HEADS),
                                          rq[:, tt, 0:16].unsqueeze(2).broadcast_to([P, 16, DH]))
                    last = nc.vector.tensor_copy(rexp[:, tt, 4:8].rearrange("p k (h c) -> p (k h) c", h=2),
                                                 rq[:, tt, 16:24].unsqueeze(2).broadcast_to([P, 8, MH]))
                last.then_inc(s("rstd_qk"), 1)
                dve.wait_ge(s("root_early"), 1)
                nc.vector.reciprocal(rms_g[0], rms_g[0])
                link(nc.vector.reciprocal(rms_g[3], rms_g[3]))
                dve.wait_ge(s("spread_qk"), 1)
                for i in range(KD):
                    src = proj[:, N_Q + i] if i < 4 else proj[:, N_MQ + i - 4]
                    gain = par[:, C_QG + i // 2:C_QG + i // 2 + 1]
                    last = nc.vector.scalar_tensor_tensor(qk[:, i], src, gain, nc_ps[4 + i // 2][:, (i % 2) * T:(i % 2 + 1) * T],
                                                          ALU.mult, ALU.mult)
                last.then_inc(s("qk_ready"), 1)
                grouped((0, 3), "cat_ready")
                dve.wait_ge(s("lam_exp"), 1)
                link(nc.vector.tensor_tensor(small[:, 104:105], small[:, 101:102], small[:, 100:101], ALU.subtract))
                link(nc.vector.tensor_tensor(small[:, 104:105], small[:, 104:105], par[:, C_LINIT:C_LINIT + 1], ALU.subtract))

                def maxima(u):
                    dve.wait_ge(s("scores_ready"), u + 1)
                    scale = (DH if u < 8 else MH) ** -0.5
                    bank = nc_ps[4 + u % 4][:, :].rearrange("p (j k) -> p j k", j=2)
                    src = bank
                    if u < 8:
                        h, qt = u // 2, u % 2
                        if u >= 2:
                            dve.wait_ge(s("exp_ready"), u - 1)
                        link(nc.vector.scalar_tensor_tensor(scores[:, u % 2], dist[:, qt].unsqueeze(1).broadcast_to([P, 2, T]),
                                                            -lam_slopes(h) / scale, bank, ALU.mult, ALU.add))
                        src = scores[:, u % 2]
                    if u >= 4:
                        dve.wait_ge(s("exp_ready"), u - 3)
                    m = small[:, 112 + 2 * (u % 4):114 + 2 * (u % 4)]
                    link(nc.vector.tensor_reduce(m, src, AX_X, ALU.max))
                    if u < 8:
                        nc.vector.tensor_scalar(m, m, -scale, None, ALU.mult).then_inc(s("max_ready"), 1)
                        dve.sem_inc(s("scores_used"), 1)
                    else:
                        nc.vector.tensor_scalar(m, m, -scale, None, ALU.mult).then_inc(s("max_ready"), 1)

                def combine(u):
                    dve.wait_ge(s("exp_ready"), u + 1)
                    z = small[:, 128 + 2 * u:130 + 2 * u]
                    link(nc.vector.reciprocal(z, z))
                    if u < 8:
                        if u >= 2:
                            dve.wait_ge(s("turned"), u - 1)
                        link(nc.vector.tensor_tensor(z[:, 1:2], z[:, 1:2], small[:, 104:105], ALU.mult))
                        link(nc.vector.tensor_scalar(mix[:, u % 2], probs[:, u % 2, 1], z[:, 1:2], None, ALU.mult))
                        nc.vector.scalar_tensor_tensor(mix[:, u % 2], probs[:, u % 2, 0], z[:, 0:1], mix[:, u % 2],
                                                       ALU.mult, ALU.add).then_inc(s("probs_ready"), 1)
                    else:
                        for j in range(2):
                            last = nc.vector.tensor_scalar(probs[:, 2, j], probs[:, 2, j], z[:, j:j + 1], None, ALU.mult)
                        last.then_inc(s("probs_ready"), 1)

                for u in range(12):
                    maxima(u)
                    if u >= 1:
                        combine(u - 1)
                combine(11)
                dve.wait_ge(s("root_sub"), 1)
                link(nc.vector.reciprocal(small[:, 8:16], small[:, 8:16]))
                for tt in range(NT):
                    last = nc.vector.tensor_copy(rexp[:, tt, 0:2].rearrange("p k (h c) -> p (k h) c", h=2),
                                                 small[:, 8 + 4 * tt:12 + 4 * tt].unsqueeze(2).broadcast_to([P, 4, MH]))
                last.then_inc(s("rstd_sub"), 1)
                link(nc.vector.tensor_tensor(small[:, 105:106], par[:, C_SUBLN:C_SUBLN + 1], par[:, C_LINIT + 1:C_LINIT + 2], ALU.mult))
                dve.wait_ge(s("spread_sub"), 1)
                for i in range(GT):
                    last = nc.vector.scalar_tensor_tensor(cat[:, 2 * GT + i], cat[:, 2 * GT + i], small[:, 105:106],
                                                          nc_ps[7][:, i * T:(i + 1) * T], ALU.mult, ALU.mult)
                last.then_inc(s("diff_scaled"), 1)
                dve.wait_ge(s("root_late"), 1)
                nc.vector.reciprocal(rms_g[1], rms_g[1])
                link(nc.vector.reciprocal(rms_g[4], rms_g[4]))
                grouped((1, 4), "cat_ready")
                dve.wait_ge(s("root_diff"), 1)
                link(nc.vector.reciprocal(rms_g[2], rms_g[2]))
                grouped((2,), "cat_ready")
                for m in range(KD):
                    dve.wait_ge(s("w_used"), N_OUT + m + 1)
                    nc.vector.tensor_tensor(xT[:, m], xT[:, m], nc_ps[4 + m % 4][:, 0:T], ALU.add).then_inc(s("out_added"), 1)

                recip(rms[:, 0], "root_ffn", "rstd_ffn")
                normed(xn, xT, par[:, C_NFFN:C_NFFN + KD], rms[:, 0], "rstd_ffn", "ffn_ready")
                dve.wait_ge(s("ffn_ready"), KD)
                link(nc.vector.tensor_copy(xr[:, 0], xn))
                link(nc.vector.tensor_tensor(xr[:, 1], xn, xr[:, 0].bitcast(F32), ALU.subtract))

                for h in range(PH + 1):
                    rows = []
                    if h < PH:
                        dve.wait_ge(s("score_kept"), h + 1)
                        rows += [(top[:, i // 2, h, i % 2], topi[:, i // 2, h, i % 2], score[:, h % 4, i], spare[:, i]) for i in range(2 * NT)]
                    if h >= 1:
                        dve.wait_ge(s("cand_ready"), h)
                        rows += [(best[:, tt, h - 1], besti[:, tt, h - 1], cand[:, (h - 1) % 2, tt], cand2[:, tt]) for tt in range(NT)]
                    for v, at_, x, y in rows:
                        last = nc.vector.max(v[:, 0:8], x)
                    link(last)
                    for v, at_, x, y in rows:
                        nc.vector.max_index(at_[:, 0:8], v[:, 0:8], x)
                        last = nc.vector.match_replace(y, v[:, 0:8], x, NEG)
                    link(last)
                    if h < PH:
                        dve.sem_inc(s("score_used"), 1)
                    if h >= 1:
                        dve.sem_inc(s("cand_used"), 1)
                    for v, at_, x, y in rows:
                        last = nc.vector.max(v[:, 8:16], y)
                    link(last)
                    if h < PH:
                        dve.sem_inc(s("halves_done"), 1)
                    for v, at_, x, y in rows:
                        last = nc.vector.max_index(at_[:, 8:16], v[:, 8:16], y)
                link(last)
                bi = besti.rearrange("p t h a -> p (t h a)")
                nc.vector.tensor_scalar(pick[:, 0], bi, 4, None, ALU.logical_shift_right)
                link(nc.vector.tensor_scalar(pick[:, 1], bi, TOPK - 1, None, ALU.bitwise_and))
                nc.vector.tensor_copy(topf.rearrange("p t h j a -> p (t h j a)"), topi.rearrange("p t h j a -> p (t h j a)"))
                link(nc.vector.tensor_copy(pickf.rearrange("p j t h a -> p j (t h a)"), pick))
                for i in range(2 * NT):
                    nc.vector.tensor_tensor(hit[i], pickf[:, i % 2, i // 2].unsqueeze(3).broadcast_to([P, PH, TOPK, TOPK]),
                                            iota[:, 0:TOPK].unsqueeze(1).unsqueeze(1).broadcast_to([P, PH, TOPK, TOPK]),
                                            ALU.is_equal).then_inc(s("hit_ready"), 1)
                    if i == 0:
                        bt = best.rearrange("p t h a -> p (t h) a")
                        nc.vector.tensor_tensor(ex, bt, bt[:, :, 0:1].broadcast_to([P, NT * PH, TOPK]), ALU.subtract).then_inc(s("best_shifted"), 1)
                dve.wait_ge(s("best_exp"), 1)
                link(nc.vector.reduce_sum(gsum, ex, AX_X))
                link(nc.vector.reciprocal(gsum, gsum))
                link(nc.vector.tensor_tensor(slot_t[:, :, 2].rearrange("p t (h a) -> p t h a", h=PH), ex.rearrange("p (t h) a -> p t h a", t=NT),
                                             gsum.rearrange("p (t h) -> p t h", t=NT).unsqueeze(3).broadcast_to([P, NT, PH, TOPK]), ALU.mult))
                link(nc.vector.tensor_tensor(hit[3], hit[3], topf[:, 1, :, 1].unsqueeze(2).broadcast_to([P, PH, TOPK, TOPK]), ALU.mult))
                for i in (0, 1, 3, 2):
                    if i < 2 * NT - 1:
                        dve.wait_ge(s("hit_keyed"), i + 1)
                    last = nc.vector.tensor_reduce(slot_t[:, i // 2, i % 2].rearrange("p (h a) -> p h a", h=PH), hit[i], AX_X, ALU.add)
                    if i in (1, 2):
                        last.then_inc(s("slots_ready"), 1)
                dve.wait_ge(s("slots_ready"), NT)
                dve.wait_ge(s("slots_kept"), 1)
                dve.wait_ge(s("w_used"), N_ALL)

                def one_hot(out, half, position, ready):
                    nc.vector.tensor_tensor(out, iota.unsqueeze(1).broadcast_to([P, 4, P]),
                                            slot[:, half, bass.ds(position, 4)].unsqueeze(2).broadcast_to([P, 4, P]),
                                            ALU.is_equal).then_inc(s(ready), 1)

                dve.sem_inc(s("g_ready"), 4)
                one_hot(ha[:, 0], 0, 0, "first_hot")
                with dve.Fori(0, GROUPS // ROUND - 1) as i:
                    for g in range(ROUND):
                        dve.wait_ge(s("g_ready"), i * ROUND + (g + 2))
                        one_hot(ha[:, (g + 1) % 4], 0, i * (4 * ROUND) + 4 * (g + 1), "first_hot")
                        dve.wait_ge(s("g_ready"), i * ROUND + (g + 3))
                        one_hot(hb[:, g % 2], 1, i * (4 * ROUND) + 4 * g, "second_hot")
                for g in range(GROUPS - ROUND, GROUPS):
                    if g + 1 < GROUPS:
                        dve.wait_ge(s("g_ready"), g + 2)
                        one_hot(ha[:, (g + 1) % 4], 0, 4 * (g + 1), "first_hot")
                    dve.wait_ge(s("g_ready"), g + 3)
                    one_hot(hb[:, g % 2], 1, 4 * g, "second_hot")
                dve.wait_ge(s("g_kept"), 2 + T // 4)


                def gated(n, tile, ready, links):
                    dve.wait_ge(s("act_used"), ready)
                    nc.vector.tensor_tensor(wgt[:, n % 2], act_e[:, n % 2], G[:, :, bass.ds(tile, 1)].squeeze(2), ALU.mult).then_inc(s("w_full"), 1)
                    dve.wait_ge(s("w_full"), links)
                    nc.vector.tensor_copy(wr[:, 0, n % 2], wgt[:, n % 2]).then_inc(s("w_high"), 1)
                    dve.wait_ge(s("w_high"), links)
                    nc.vector.tensor_tensor(wr[:, 1, n % 2], wgt[:, n % 2], wr[:, 0, n % 2].bitcast(F32), ALU.subtract).then_inc(s("wgt_ready"), 1)

                def low(k, ready):
                    dve.wait_ge(s("hi_done"), ready)
                    nc.vector.tensor_tensor(split[:, k % SPLITS, 1], wring[:, (N_ALL + k) % WSLOTS, 0:D],
                                            split[:, k % SPLITS, 0].bitcast(F32), ALU.subtract).then_inc(s("lo_done"), 1)

                low(0, 1)
                low(1, 2)
                gated(0, 0, 3, 1)
                low(2, 3)
                low(3, 4)
                with dve.Fori(0, NK // 6) as i:
                    for e in range(6):
                        gated(e + 1, i * 6 + (e + 1), i * 6 + (e + 4), i * 6 + (e + 2))
                        for k in (2 * e + 4, 2 * e + 5):
                            low(k, i * 12 + (k + 1))
                gated(NK - 1, NK - 1, NK + 2, NK)
                for tt in range(NT):
                    for c in range(2):
                        dve.wait_ge(s("peer_turned"), 2 * tt + c + 1)
                        at = xT[:, 4 * c:4 * c + 4, tt * P:(tt + 1) * P]
                        link(nc.vector.tensor_tensor(at, at, nc_ps[c][:, :].rearrange("p (a t) -> p a t", a=4), ALU.add))
                        dve.sem_inc(s("peer_added"), 1)

        nc.all_engine_barrier(sems_to_clear=s.range())


LH = 8
CTAPS = 4
RG_C = 8.0
R2 = 5
NPAIR = LH * NT
GRP = 4
LEVELS = (1, 2, 4, 8, 16, 32, 64)

Q_NORM = 0
Q_FINAL = Q_NORM + 2 * KD
Q_ADAB = Q_FINAL + KD
Q_LCW = Q_ADAB + 2 * 3 * KD
Q_LCB = Q_LCW + LH * CTAPS
Q_LGB = Q_LCB + LH
Q_LAM = Q_LGB + 2 * LH
Q_GCW = Q_LAM + LH
Q_ONORM = Q_GCW + 3 * LH * CTAPS
Q_ALOG = Q_ONORM + 1
Q_DT = Q_ALOG + LH
NPAR2 = Q_DT + LH
M_TRI, M_LEVEL = 0, P
NMASK = P + len(LEVELS) * P


def softplus(nc, dve, link, s, out, z, w):
    link(nc.vector.tensor_scalar(w[0], z, -1.0, None, ALU.mult))
    link(nc.vector.tensor_tensor(w[0], w[0], z, ALU.min))
    dve.sem_inc(s("sp_in"), 1)
    dve.wait_ge(s("sp_exp"), 1)
    link(nc.vector.tensor_scalar(w[1], w[0], 2.0, None, ALU.add))
    link(nc.vector.reciprocal(w[1], w[1]))
    link(nc.vector.tensor_tensor(w[1], w[1], w[0], ALU.mult))
    link(nc.vector.tensor_tensor(w[2], w[1], w[1], ALU.mult))
    link(nc.vector.tensor_scalar(w[3], w[2], 1.0 / 19, 1.0 / 17, ALU.mult, ALU.add))
    for n in (15, 13, 11, 9, 7, 5, 3, 1):
        link(nc.vector.tensor_tensor(w[3], w[3], w[2], ALU.mult))
        link(nc.vector.tensor_scalar(w[3], w[3], 1.0 / n, None, ALU.add))
    link(nc.vector.tensor_tensor(w[3], w[3], w[1], ALU.mult))
    link(nc.vector.tensor_scalar(w[1], z, 0.0, None, ALU.max))
    link(nc.vector.scalar_tensor_tensor(out, w[3], 2.0, w[1], ALU.mult, ALU.add))


def lru_layer(nc, ctx, m, d_in, d_gate, d_out, d_par):
    ps, xT, big, const, par, cond, ring, split, xr = (m[k] for k in ("ps", "xT", "big", "const", "par2", "cond", "ring2", "split", "xr"))
    s = Sems(nc, ctx, "r_")
    ones, ident, eps = const[:, K_ONES:K_ONES + P], const[:, K_IDENT:K_IDENT + P], const[:, K_EPS:K_EPS + 1]
    b = Region(big, NK * T)
    sq = b(KD, T)
    xn = b(KD, T)
    xpad = b(LH, T + CTAPS - 1)
    xc = b(LH, T)
    zs = b(LH, T)
    rt = b(LH, T)
    it = b(LH, T)
    at = b(LH, T)
    th = b(LH, T)
    hs = b(LH, T)
    rms = b(T)
    small = b(128)
    sp = small[:, 8:16]
    w4 = [small[:, 32 + 8 * j:40 + 8 * j] for j in range(4)]
    gain = small[:, 64:72]
    NIN2 = 2 * LH
    N_G, N_O = NIN2, NIN2 + 2
    N_END = N_O + KD
    cd = cond[:, 0]

    with nc.Block() as block:
        @block.sync
        def _(sy):
            sy.dma_start(par, d_par).then_inc(s("par_loaded"), 16)
            for n in range(N_END):
                if n >= R2:
                    sy.wait_ge(s("lo_done" if n - R2 < NIN2 else "used"), n - R2 + 1)
                src = d_in[n] if n < N_G else d_gate[n - N_G] if n < N_O else d_out[n - N_O]
                sy.dma_start(ring[n % R2], src).then_inc(s(f"loaded{n % R2}"), 16)

        @block.tensor
        def _(pe):
            def tile_of(n):
                pe.wait_ge(s(f"loaded{n % R2}"), 16 * (n // R2 + 1))
                return ring[n % R2].rearrange("p (k c) -> p k c", k=KD)

            def gates(n):
                pe.wait_ge(s("convolved"), n + 1)
                for g in range(2):
                    i = 2 * n + g
                    wt = tile_of(N_G + g)
                    if i >= 4:
                        pe.wait_ge(s("gates_kept"), i - 3)
                    nc.tensor.matmul(ps[4 + i % 4][:, 0:T], wt[:, n], xc[:, n], start=True, stop=True).then_inc(s("gates"), 1)

            norm_pe(nc, pe, s, ps[4][:, 0:T], sq, ones)
            for n in range(NIN2):
                if n >= 4:
                    pe.wait_ge(s("kept"), n - 3)
                chunk_product(nc, pe, s, ps[n % 4][:, 0:T], split, xr, n).then_inc(s("used"), 1)
                if n >= LH + 1:
                    gates(n - LH - 1)
            gates(LH - 1)
            pe.wait_ge(s("kept"), NIN2)
            pe.wait_ge(s("gates"), 2 * LH)
            pe.sem_inc(s("used"), 2)
            for mm in range(KD):
                wt = tile_of(N_O + mm)
                if mm >= 4:
                    pe.wait_ge(s("x_added"), mm - 3)
                for k in range(KD):
                    if mm == 0 and k % (LH // 2) == 0:
                        pe.wait_ge(s("y_ready"), k // (LH // 2) + 1)
                    last = nc.tensor.matmul(ps[mm % 4][:, 0:T], wt[:, k], hs[:, k], start=(k == 0), stop=(k == KD - 1))
                last.then_inc(s("used"), 1)

        @block.scalar
        def _(act):
            norm_act(nc, act, s, ps[4][:, 0:T], sq, xT, rms, eps)
            modulate_act(nc, act, s, xn, cd)
            for n in range(SPLITS):
                chunk_high(nc, act, s, split, ring, n)
            act.wait_ge(s("sp_in"), 1)
            nc.scalar.activation(w4[0], w4[0], ACT.Exp).then_inc(s("sp_exp"), 1)
            act.wait_ge(s("pads"), 1)

            def gates_keep(n):
                for g in range(2):
                    i = 2 * n + g
                    act.wait_ge(s("gates"), i + 1)
                    nc.scalar.activation((rt, it)[g][:, n], ps[4 + i % 4][:, 0:T], ACT.Sigmoid,
                                         bias=par[:, Q_LGB + g * LH + n:Q_LGB + g * LH + n + 1]).then_inc(s("gates_kept"), 1)

            for n in range(NIN2):
                act.wait_ge(s("used"), n + 1)
                out = xpad[:, n, CTAPS - 1:] if n < LH else zs[:, n - LH]
                nc.scalar.copy(out, ps[n % 4][:, 0:T]).then_inc(s("kept"), 1)
                if n + SPLITS < NIN2:
                    chunk_high(nc, act, s, split, ring, n + SPLITS)
                if n >= LH + 1:
                    gates_keep(n - LH - 1)
            gates_keep(LH - 1)
            act.wait_ge(s("sp_ready"), 1)
            act.wait_ge(s("gates_kept"), 2 * LH)
            for n in range(LH):
                nc.scalar.activation(at[:, n], rt[:, n], ACT.Exp, scale=small[:, 8 + n:9 + n])
                nc.scalar.activation(th[:, n], rt[:, n], ACT.Tanh, scale=small[:, 16 + n:17 + n]).then_inc(s("a_ready"), 1)
            for i in range(2):
                v = slice(i * (LH // 2), (i + 1) * (LH // 2))
                act.wait_ge(s("m2_ready"), (i + 1) * (LH // 4))
                nc.scalar.activation(th[:, v], th[:, v], ACT.Sqrt).then_inc(s("mult_ready"), 1)
            for i in range(2):
                v = slice(i * (LH // 2), (i + 1) * (LH // 2))
                nc.scalar.activation(zs[:, v], zs[:, v], ACT.Silu).then_inc(s("z_ready"), 1)

        @block.gpsimd
        def _(pool):
            nc.gpsimd.memset(xpad[:, :, 0:CTAPS - 1], 0.0).then_inc(s("pads"), 1)
            for n in range(NIN2):
                chunk_low(nc, pool, s, split, ring, n)
            for i in range(2):
                v = slice(i * (LH // 2), (i + 1) * (LH // 2))
                pool.wait_ge(s("gates_kept"), (i + 1) * LH)
                nc.gpsimd.tensor_tensor(it[:, v], it[:, v], xc[:, v], ALU.mult).then_inc(s("ix_ready"), 1)

        @block.vector
        def _(dve):
            link = Link(dve, s("dve_link"))
            dve.wait_ge(s("par_loaded"), 16)
            link(nc.vector.tensor_tensor(cond[:, :, :], cond[:, :, :], par[:, Q_ADAB:Q_ADAB + 6 * KD].rearrange("p (l c) -> p l c", l=2), ALU.add))
            dve.sem_inc(s("cond_ready"), 1)
            norm_dve(nc, dve, link, s, rms, xT, xn, gain, par[:, Q_NORM:Q_NORM + KD], cd)
            x_parts(nc, dve, s, xr, xn)
            link(nc.vector.tensor_scalar(small[:, 24:32], par[:, Q_LAM:Q_LAM + LH], -1.0, None, ALU.mult))
            softplus(nc, dve, link, s, sp, small[:, 24:32], w4)
            link(nc.vector.tensor_scalar(small[:, 16:24], sp, RG_C, None, ALU.mult))
            link(nc.vector.tensor_scalar(sp, sp, -RG_C, None, ALU.mult))
            dve.sem_inc(s("sp_ready"), 1)
            causal_conv(nc, dve, s, "kept", "convolved", LH, xpad, xc, par, Q_LCW, par[:, Q_LCB:Q_LCB + LH])
            HL = LH // 2
            halves = [slice(i * HL, (i + 1) * HL) for i in range(2)]
            for n in range(0, LH, 2):
                dve.wait_ge(s("a_ready"), n + 2)
                v = slice(n, n + 2)
                link(nc.vector.tensor_tensor(hs[:, v], at[:, v], at[:, v], ALU.mult))
                nc.vector.scalar_tensor_tensor(flat(th[:, v]), flat(hs[:, v]), 1.0, flat(th[:, v]), ALU.add, ALU.mult).then_inc(s("m2_ready"), 1)
            for i, v in enumerate(halves):
                dve.wait_ge(s("mult_ready"), i + 1)
                dve.wait_ge(s("ix_ready"), i + 1)
                link(nc.vector.tensor_tensor(th[:, v], th[:, v], it[:, v], ALU.mult))
                for n in range(i * HL, (i + 1) * HL):
                    last = nc.vector.tensor_tensor_scan(hs[:, n], at[:, n], th[:, n], 0.0, ALU.mult, ALU.add)
                link(last)
                dve.wait_ge(s("z_ready"), i + 1)
                nc.vector.tensor_tensor(hs[:, v], hs[:, v], zs[:, v], ALU.mult).then_inc(s("y_ready"), 1)
            for mm in range(KD):
                dve.wait_ge(s("used"), N_O + mm + 1)
                nc.vector.scalar_tensor_tensor(xT[:, mm], ps[mm % 4][:, 0:T], cd[:, 2 * KD + mm:2 * KD + mm + 1], xT[:, mm],
                                               ALU.mult, ALU.add).then_inc(s("x_added"), 1)
    nc.all_engine_barrier(sems_to_clear=s.range())


def flat(v):
    return v.rearrange("p a b -> p (a b)")


def causal_conv(nc, dve, s, ready, done, tiles, src, dst, par, at, bias):
    for n0 in range(0, tiles, 2):
        dve.wait_ge(s(ready), n0 + 2)
        for j in range(CTAPS):
            for n in (n0, n0 + 1):
                tap = par[:, at + n * CTAPS + j:at + n * CTAPS + j + 1]
                x = src[:, n, j:j + T]
                count = (n0 * CTAPS) + 2 * j + (n - n0) + 1
                if j == 0:
                    ins = nc.vector.tensor_scalar(dst[:, n], x, tap, 0.0 if bias is None else bias[:, n:n + 1], ALU.mult, ALU.add)
                else:
                    dve.wait_ge(s(done + "_tap"), count - 2)
                    ins = nc.vector.scalar_tensor_tensor(dst[:, n], x, tap, dst[:, n], ALU.mult, ALU.add)
                ins.then_inc(s(done + "_tap"), 1)
        for i in range(2):
            dve.wait_ge(s(done + "_tap"), (n0 + 2) * CTAPS - 1 + i)
            dve.sem_inc(s(done), 1)


def chunk_high(nc, act, s, split, ring, n):
    act.wait_ge(s(f"loaded{n % R2}"), 16 * (n // R2 + 1))
    if n >= SPLITS:
        act.wait_ge(s("used"), n - SPLITS + 1)
    nc.scalar.copy(split[:, n % SPLITS, 0], ring[n % R2]).then_inc(s("hi_done"), 1)


def chunk_low(nc, pool, s, split, ring, n):
    pool.wait_ge(s("hi_done"), n + 1)
    nc.gpsimd.tensor_tensor(split[:, n % SPLITS, 1], ring[n % R2], split[:, n % SPLITS, 0].bitcast(F32), ALU.subtract).then_inc(s("lo_done"), 1)


def chunk_product(nc, pe, s, out, split, xr, n):
    pe.wait_ge(s("lo_done"), n + 1)
    for k in range(KD):
        if n == 0:
            pe.wait_ge(s("x_parts"), k + 1)
        for a, x in ((0, 0), (0, 1), (1, 0)):
            last = nc.tensor.matmul(out, split[:, n % SPLITS, a, k * P:(k + 1) * P], xr[:, x, k],
                                    start=(k == 0 and a == 0 and x == 0), stop=(k == KD - 1 and a == 1))
    return last


def x_parts(nc, dve, s, xr, xn):
    for k in range(KD):
        dve.wait_ge(s("xn_ready"), k + 1)
        nc.vector.tensor_copy(xr[:, 0, k], xn[:, k]).then_inc(s("x_high"), 1)
    for k in range(KD):
        dve.wait_ge(s("x_high"), k + 1)
        nc.vector.tensor_tensor(xr[:, 1, k], xn[:, k], xr[:, 0, k].bitcast(F32), ALU.subtract).then_inc(s("x_parts"), 1)


def norm_pe(nc, pe, s, out, sq, ones):
    for k in range(KD):
        pe.wait_ge(s("sq_x"), k + 1)
        last = nc.tensor.matmul(out, ones, sq[:, k], start=(k == 0), stop=(k == KD - 1))
    last.then_inc(s("sum_x"), 1)


def norm_act(nc, act, s, total, sq, xT, rms, eps):
    for k in range(KD):
        nc.scalar.activation(sq[:, k], xT[:, k], ACT.Square).then_inc(s("sq_x"), 1)
    act.wait_ge(s("sum_x"), 1)
    nc.scalar.activation(rms, total, ACT.Sqrt, scale=1.0 / D, bias=eps).then_inc(s("root_x"), 1)


def modulate_act(nc, act, s, xn, cd):
    act.wait_ge(s("cond_ready"), 1)
    for k in range(KD):
        act.wait_ge(s("scaled"), k + 1)
        nc.scalar.activation(xn[:, k], xn[:, k], ACT.Identity, bias=cd[:, k:k + 1]).then_inc(s("xn_ready"), 1)


def norm_dve(nc, dve, link, s, rms, xT, dst, gain, g, cd):
    link(nc.vector.scalar_tensor_tensor(gain, cd[:, KD:2 * KD], 1.0, g, ALU.add, ALU.mult))
    dve.wait_ge(s("root_x"), 1)
    link(nc.vector.reciprocal(rms, rms))
    for k in range(KD):
        nc.vector.scalar_tensor_tensor(dst[:, k], xT[:, k], gain[:, k:k + 1], rms, ALU.mult, ALU.mult).then_inc(s("scaled"), 1)


def gdn_layer(nc, ctx, m, d_in, d_ab, d_out, d_mask, out):
    ps, xT, big, const, par, cond, ring, split, xr = (m[k] for k in ("ps", "xT", "big", "const", "par2", "cond", "ring2", "split", "xr"))
    s = Sems(nc, ctx, "g_")
    ones, ident, eps = const[:, K_ONES:K_ONES + P], const[:, K_IDENT:K_IDENT + P], const[:, K_EPS:K_EPS + 1]
    b = Region(big, NK * T)
    qkv = b(3 * LH, T)
    zs = b(LH, T)
    at_pad = b.at
    pad = b(3 * LH, T + CTAPS - 1)
    end_pad = b.at
    mask = b(NMASK)
    sq = b(2 * LH, T)
    b2 = Region(big, end_pad)
    b2.at = at_pad
    kbg = b2(LH, P)
    kdec = b2(LH, P)
    eg = b2(LH, P)
    qdec = b2(LH, P)
    vb = b2(LH, NT, P)
    dec = b(LH, NT, P)
    aT = b(LH, NT, P)
    attn = b(LH, NT, P)
    xn = attn.rearrange("p h t c -> p h (t c)")
    Tm = b(LH, NT, P)
    Um = b(LH, NT, P)
    X = sq.rearrange("p (a h) t -> p a h t", a=2)[:, 0].rearrange("p h (t c) -> p h t c", t=NT)
    BT = sq.rearrange("p (a h) t -> p a h t", a=2)[:, 1].rearrange("p h (t c) -> p h t c", t=NT)
    rms = b(T)
    u_ = b(LH, NT, P)
    small = m["small2"]
    wT = dec[:, :, 0]
    state = aT[:, :, 1]
    oT = Tm.rearrange("p h t c -> p h (t c)")
    osq = X.rearrange("p h t c -> p h (t c)")

    def cols(i):
        return small[:, 16 * i:16 * (i + 1)].rearrange("p (t h) -> p t h", t=NT)

    ab, bb, gg, gc, rk, rq, rb, gl, kb_s, kd_s = (cols(i) for i in range(1, 11))
    w4 = [small[:, 176 + 16 * j:192 + 16 * j].rearrange("p (t h) -> p t h", t=NT) for j in range(4)]
    gain = small[:, 240:248]
    ms = cols(16)
    beta = bb
    cd = cond[:, 1]
    tri = mask[:, M_TRI:M_TRI + P]
    wab = m["wab"]
    NQ = 4 * LH
    N_END = NQ + KD
    NG = NPAIR // GRP

    def grp(v, q):
        return v[:, 2 * q:2 * q + 2].rearrange("p h t c -> p (h t) c")

    with nc.Block() as block:
        @block.sync
        def _(sy):
            sy.dma_start(wab, d_ab.rearrange("p (k c) -> p k c", k=KD)).then_inc(s("ab_loaded"), 16)
            for n in range(N_END):
                if n >= R2:
                    sy.wait_ge(s("lo_done" if n - R2 < NQ else "used"), n - R2 + 1)
                src = d_in[n] if n < NQ else d_out[n - NQ]
                sy.dma_start(ring[n % R2], src).then_inc(s(f"loaded{n % R2}"), 16)
                if n == R2 - 1:
                    sy.dma_start(mask, d_mask).then_inc(s("mask_loaded"), 16)
            for k in range(KD):
                sy.wait_ge(s("scaled"), KD + k + 1)
                sy.dma_start(out[:, k], xn[:, k]).then_inc(s("stored"), 16)
            sy.wait_ge(s("stored"), 16 * KD)

        @block.tensor
        def _(pe):
            def tile_of(n):
                pe.wait_ge(s(f"loaded{n % R2}"), 16 * (n // R2 + 1))
                return ring[n % R2].rearrange("p (k c) -> p k c", k=KD)

            def final_sum(k):
                pe.wait_ge(s("sq_f"), k + 1)
                return nc.tensor.matmul(ps[0][:, 0:T], ones, sq[:, k], start=(k == 0), stop=(k == KD - 1))

            norm_pe(nc, pe, s, ps[4][:, 0:T], sq, ones)
            pe.wait_ge(s("xn_ready"), KD)
            pe.wait_ge(s("ab_loaded"), 16)
            for tt in range(NT):
                for k in range(KD):
                    last = nc.tensor.matmul(ps[5][:, 16 * tt:16 * (tt + 1)], xn[:, k, tt * P:(tt + 1) * P], wab[:, k],
                                            start=(k == 0), stop=(k == KD - 1))
            last.then_inc(s("ab_done"), 1)
            for n in range(NQ):
                if n >= 4:
                    pe.wait_ge(s("kept"), n - 3)
                chunk_product(nc, pe, s, ps[n % 4][:, 0:T], split, xr, n).then_inc(s("used"), 1)
                if n == LH:
                    pe.wait_ge(s("g_ready"), 1)
                    pe.wait_ge(s("mask_loaded"), 16)
                    for tt in range(NT):
                        last = nc.tensor.matmul(ps[6][:, 8 * tt:8 * (tt + 1)], tri, gg[:, tt], start=True, stop=True)
                    last.then_inc(s("gc_done"), 1)
            pe.wait_ge(s("sq_qk"), 1)
            for tt in range(NT):
                for i in range(2 * LH):
                    last = nc.tensor.matmul(ps[5][:, 32 + 16 * tt + i:33 + 16 * tt + i], sq[:, i, tt * P:(tt + 1) * P], ones[:, 0:1],
                                            start=True, stop=True)
            last.then_inc(s("sum_qk"), 1)
            pe.wait_ge(s("gc_kept"), 1)
            pe.wait_ge(s("kept"), NQ)
            for q in range(NG):
                for j in range(GRP):
                    h, tt = 2 * q + j // 2, j % 2
                    last = nc.tensor.matmul(ps[q][:, j * P:(j + 1) * P], gc[:, tt, h:h + 1].broadcast_to([P, P]), ident, start=True, stop=True)
                last.then_inc(s("g_spread"), 1)
            pe.wait_ge(s("rb_ready"), 1)
            for q in range(NG):
                if q >= 1:
                    pe.wait_ge(s("kk_used"), q)
                    pe.wait_ge(s("kq_used"), q)
                for j in range(GRP):
                    h, tt = 2 * q + j // 2, j % 2
                    kT = qkv[:, LH + h, tt * P:(tt + 1) * P]
                    nc.tensor.matmul(ps[4][:, j * P:(j + 1) * P], kT, kT, start=True, stop=True)
                    last = nc.tensor.matmul(ps[5][:, j * P:(j + 1) * P], rb[:, tt, h:h + 1].broadcast_to([P, P]), ident, start=True, stop=True)
                last.then_inc(s("kk_done"), 1)
                for j in range(GRP):
                    h, tt = 2 * q + j // 2, j % 2
                    last = nc.tensor.matmul(ps[6][:, j * P:(j + 1) * P], qkv[:, LH + h, tt * P:(tt + 1) * P],
                                            qkv[:, h, tt * P:(tt + 1) * P], start=True, stop=True)
                last.then_inc(s("kq_done"), 1)
            for q in range(NG):
                pe.wait_ge(s("g_used"), q + 1)
                if q >= 2:
                    pe.wait_ge(s("kv_kept"), q - 1)
                for c in range(2):
                    bank = ps[2 * (q % 2) + c]
                    if q == 0:
                        pe.wait_ge(s("g_used"), NG)
                    for j in range(GRP):
                        h, tt = 2 * q + j // 2, j % 2
                        last = nc.tensor.transpose(bank[:, j * P:(j + 1) * P], qkv[:, (1 + c) * LH + h, tt * P:(tt + 1) * P], ident)
                last.then_inc(s("kv_turned"), 1)
            pe.wait_ge(s("kv_kept"), NG)
            pe.wait_ge(s("kq_used"), NG)
            for v, lv in enumerate(LEVELS):
                for q in range(NG):
                    pe.wait_ge(s("bt_ready"), v * NG + q + 1)
                    if v > 0:
                        pe.wait_ge(s("inv_ready"), v * NG - NG + q + 1)
                    for j in range(GRP):
                        rhs = ident if v == 0 else grp(Tm, q)[:, j]
                        last = nc.tensor.matmul(ps[q][:, j * P:(j + 1) * P], grp(BT, q)[:, j], rhs, start=True, stop=True)
                    last.then_inc(s("x_done"), 1)
                if v == 0:
                    continue
                for q in range(NG):
                    pe.wait_ge(s("x_kept"), (v - 1) * NG + q + 1)
                    i = (v - 1) * NG + q
                    if i >= 2:
                        pe.wait_ge(s("inv_ready"), NG + i - 1)
                    for j in range(GRP):
                        last = nc.tensor.matmul(ps[4 + 2 * (q % 2)][:, j * P:(j + 1) * P], grp(X, q)[:, j], grp(Um, q)[:, j], start=True, stop=True)
                    if v < len(LEVELS) - 1:
                        for j in range(GRP):
                            last = nc.tensor.matmul(ps[5 + 2 * (q % 2)][:, j * P:(j + 1) * P], grp(Um, q)[:, j], grp(X, q)[:, j], start=True, stop=True)
                    last.then_inc(s("y_done"), 1)
            for q in range(NG):
                pe.wait_ge(s("inv_ready"), NG * len(LEVELS) - NG + q + 1)
                for j in range(GRP):
                    h, tt = 2 * q + j // 2, j % 2
                    last = nc.tensor.matmul(ps[q][:, j * P:(j + 1) * P], Um[:, h, tt], vb[:, h, tt], start=True, stop=True)
                last.then_inc(s("u_done"), 1)
            for hh in range(2):
                pe.wait_ge(s("inv_ready"), NG * len(LEVELS))
                for j in range(4):
                    h = 4 * hh + j
                    last = nc.tensor.matmul(ps[4 + hh][:, j * P:(j + 1) * P], kbg[:, h], Um[:, h, 1], start=True, stop=True)
                last.then_inc(s("wT_done"), 1)
            for hh in range(2):
                pe.wait_ge(s("u_kept"), 2 * hh + 2)
                for j in range(4):
                    h = 4 * hh + j
                    last = nc.tensor.matmul(ps[6 + hh][:, j * P:(j + 1) * P], kdec[:, h], u_[:, h, 0], start=True, stop=True)
                last.then_inc(s("state_done"), 1)
            for hh in range(2):
                pe.wait_ge(s("state_kept"), hh + 1)
                pe.wait_ge(s("wT_kept"), hh + 1)
                for j in range(4):
                    h = 4 * hh + j
                    last = nc.tensor.matmul(ps[4 + hh][:, j * P:(j + 1) * P], wT[:, h], state[:, h], start=True, stop=True)
                last.then_inc(s("wS_done"), 1)
            pe.wait_ge(s("qdec_ready"), 1)
            for q in range(NG):
                pe.wait_ge(s("vnew"), q // 2 + 1)
                for j in range(GRP):
                    h, tt = 2 * q + j // 2, j % 2
                    o = ps[q][:, j * P:(j + 1) * P]
                    if tt == 1:
                        nc.tensor.matmul(o, state[:, h], qdec[:, h], start=True, stop=False)
                    last = nc.tensor.matmul(o, u_[:, h, tt], attn[:, h, tt], start=(tt == 0), stop=True)
                last.then_inc(s("o_done"), 1)
            pe.wait_ge(s("o_sq"), 1)
            for tt in range(NT):
                for h in range(LH):
                    last = nc.tensor.matmul(ps[4][:, 8 * tt + h:8 * tt + h + 1], osq[:, h, tt * P:(tt + 1) * P], ones[:, 0:1], start=True, stop=True)
            last.then_inc(s("sum_o"), 1)
            pe.wait_ge(s("o_rstd"), 1)
            for q in range(NG):
                for j in range(GRP):
                    h, tt = 2 * q + j // 2, j % 2
                    last = nc.tensor.matmul(ps[q][:, j * P:(j + 1) * P], ms[:, tt, h:h + 1].broadcast_to([P, P]), ident, start=True, stop=True)
                last.then_inc(s("o_spread"), 1)
            pe.wait_ge(s("y_ready"), 1)
            for mm in range(KD):
                wt = tile_of(NQ + mm)
                if mm >= 4:
                    pe.wait_ge(s("x_added"), mm - 3)
                for k in range(KD):
                    last = nc.tensor.matmul(ps[4 + mm % 4][:, 0:T], wt[:, k], oT[:, k], start=(k == 0), stop=(k == KD - 1))
                last.then_inc(s("used"), 1)
                if mm >= 1:
                    final_sum(mm - 1)
            final_sum(KD - 1).then_inc(s("sum_f"), 1)

        @block.scalar
        def _(act):
            norm_act(nc, act, s, ps[4][:, 0:T], sq, xT, rms, eps)
            modulate_act(nc, act, s, xn, cd)
            for n in range(SPLITS):
                chunk_high(nc, act, s, split, ring, n)
            act.wait_ge(s("sp_in"), 1)
            nc.scalar.activation(w4[0], w4[0], ACT.Exp).then_inc(s("sp_exp"), 1)
            nc.scalar.activation(small[:, 248:256], par[:, Q_ALOG:Q_ALOG + LH], ACT.Exp).then_inc(s("alog_exp"), 1)
            act.wait_ge(s("ab_kept"), 1)
            nc.scalar.activation(beta, bb, ACT.Sigmoid).then_inc(s("beta_ready"), 1)
            act.wait_ge(s("pads"), 1)
            done = 0
            for n in range(NQ):
                act.wait_ge(s("used"), n + 1)
                if n < 3 * LH:
                    nc.scalar.copy(pad[:, n, CTAPS - 1:], ps[n % 4][:, 0:T]).then_inc(s("kept"), 1)
                else:
                    nc.scalar.activation(zs[:, n - 3 * LH], ps[n % 4][:, 0:T], ACT.Silu).then_inc(s("kept"), 1)
                if n + SPLITS < NQ:
                    chunk_high(nc, act, s, split, ring, n + SPLITS)
                if n >= 4 and n % 2 == 1 and done < 3 * LH:
                    act.wait_ge(s("convolved"), done + 2)
                    nc.scalar.activation(qkv[:, done:done + 2], qkv[:, done:done + 2], ACT.Silu).then_inc(s("silu"), 2)
                    done += 2
                    if done == 2 * LH:
                        act.wait_ge(s("silu"), 2 * LH)
                        nc.scalar.activation(sq, qkv[:, 0:2 * LH], ACT.Square).then_inc(s("sq_qk"), 1)
            assert done == 3 * LH
            act.wait_ge(s("sum_qk"), 1)
            for tt in range(NT):
                nc.scalar.activation(rq[:, tt], ps[5][:, 32 + 16 * tt:40 + 16 * tt], ACT.Sqrt, bias=eps)
                last = nc.scalar.activation(rk[:, tt], ps[5][:, 40 + 16 * tt:48 + 16 * tt], ACT.Sqrt, bias=eps)
            last.then_inc(s("rqk_root"), 1)
            act.wait_ge(s("gl_in"), 1)
            nc.scalar.activation(gl, gl, ACT.Exp)
            nc.scalar.activation(kb_s, gc, ACT.Exp).then_inc(s("gl_exp"), 1)
            for q in range(NG):
                act.wait_ge(s("dec_in"), q + 1)
                nc.scalar.activation(grp(dec, q), grp(dec, q), ACT.Exp)
                for j in range(2):
                    h = 2 * q + j
                    last = nc.scalar.activation(eg[:, h], ps[q][:, (2 * j + 1) * P:(2 * j + 2) * P], ACT.Exp)
                last.then_inc(s("dec_ready"), 1)
            for q in range(NG):
                act.wait_ge(s("kv_turned"), q + 1)
                for j in range(GRP):
                    h, tt = 2 * q + j // 2, j % 2
                    if q == 0 and j == 0:
                        act.wait_ge(s("kb_ready"), 1)
                        act.wait_ge(s("beta_ready"), 1)
                    kk, scale = (kdec, kd_s) if tt == 0 else (kbg, kb_s)
                    nc.scalar.activation(kk[:, h], ps[2 * (q % 2)][:, j * P:(j + 1) * P], ACT.Copy, scale=scale[:, tt, h:h + 1])
                    last = nc.scalar.activation(vb[:, h, tt], ps[2 * (q % 2) + 1][:, j * P:(j + 1) * P], ACT.Copy, scale=beta[:, tt, h:h + 1])
                last.then_inc(s("kv_kept"), 1)
            for v in range(1, len(LEVELS)):
                for q in range(NG):
                    act.wait_ge(s("x_done"), v * NG + q + 1)
                    nc.scalar.copy(grp(X, q), ps[q][:, :].rearrange("p (a c) -> p a c", a=GRP)).then_inc(s("x_kept"), 1)
            for q in range(NG):
                act.wait_ge(s("u_done"), q + 1)
                nc.scalar.copy(grp(u_, q), ps[q][:, :].rearrange("p (a c) -> p a c", a=GRP)).then_inc(s("u_kept"), 1)
                if q >= 2:
                    hh = q - 2
                    act.wait_ge(s("wT_done"), hh + 1)
                    nc.scalar.copy(wT[:, 4 * hh:4 * hh + 4], ps[4 + hh][:, :].rearrange("p (a c) -> p a c", a=4)).then_inc(s("wT_kept"), 1)
            for hh in range(2):
                act.wait_ge(s("state_done"), hh + 1)
                nc.scalar.copy(state[:, 4 * hh:4 * hh + 4], ps[6 + hh][:, :].rearrange("p (a c) -> p a c", a=4)).then_inc(s("state_kept"), 1)
            for q in range(NG):
                act.wait_ge(s("o_done"), q + 1)
                src = ps[q][:, :].rearrange("p (h t) -> p h t", h=2)
                nc.scalar.copy(oT[:, 2 * q:2 * q + 2], src)
                last = nc.scalar.activation(osq[:, 2 * q:2 * q + 2], src, ACT.Square)
            last.then_inc(s("o_sq"), 1)
            act.wait_ge(s("ms_in"), 1)
            nc.scalar.activation(ms, ms, ACT.Sqrt, bias=eps).then_inc(s("o_root"), 1)
            for k in range(KD):
                act.wait_ge(s("x_added"), k + 1)
                nc.scalar.activation(sq[:, k], xT[:, k], ACT.Square).then_inc(s("sq_f"), 1)
            act.wait_ge(s("sum_f"), 1)
            nc.scalar.activation(rms, ps[0][:, 0:T], ACT.Sqrt, scale=1.0 / D, bias=eps).then_inc(s("root_f"), 1)

        @block.gpsimd
        def _(pool):
            nc.gpsimd.memset(pad[:, :, 0:CTAPS - 1], 0.0).then_inc(s("pads"), 1)
            for n in range(NQ):
                chunk_low(nc, pool, s, split, ring, n)
            pool.wait_ge(s("mask_loaded"), 16)
            for v in range(len(LEVELS)):
                mk = mask[:, M_LEVEL + v * P:M_LEVEL + (v + 1) * P]
                for q in range(NG):
                    if v == 0:
                        pool.wait_ge(s("aT_ready"), q + 1)
                    else:
                        pool.wait_ge(s("x_done"), (v - 1) * NG + q + 1)
                        if v == 1:
                            pool.wait_ge(s("inv_ready"), q + 1)
                    nc.gpsimd.tensor_tensor(grp(BT, q), grp(aT, q), mk.unsqueeze(1).broadcast_to([P, GRP, P]), ALU.mult).then_inc(s("bt_ready"), 1)

        @block.vector
        def _(dve):
            link = Link(dve, s("dve_link"))
            dve.sem_inc(s("cond_ready"), 1)
            norm_dve(nc, dve, link, s, rms, xT, xn, gain, par[:, Q_NORM + KD:Q_NORM + 2 * KD], cd)
            x_parts(nc, dve, s, xr, xn)
            dve.wait_ge(s("ab_done"), 1)
            for tt in range(NT):
                nc.vector.tensor_tensor(ab[:, tt], ps[5][:, 16 * tt:16 * tt + 8], par[:, Q_DT:Q_DT + LH], ALU.add)
                last = nc.vector.tensor_copy(bb[:, tt], ps[5][:, 16 * tt + 8:16 * tt + 16])
            link(last)
            dve.sem_inc(s("ab_kept"), 1)
            softplus(nc, dve, link, s, gg, ab, w4)
            dve.wait_ge(s("alog_exp"), 1)
            for tt in range(NT):
                last = nc.vector.scalar_tensor_tensor(gg[:, tt], gg[:, tt], -1.0, small[:, 248:256], ALU.mult, ALU.mult)
            last.then_inc(s("g_ready"), 1)
            causal_conv(nc, dve, s, "kept", "convolved", 3 * LH, pad, qkv, par, Q_GCW, None)
            dve.wait_ge(s("gc_done"), 1)
            nc.vector.tensor_copy(gc, ps[6][:, 0:16].rearrange("p (t h) -> p t h", t=NT)).then_inc(s("gc_kept"), 1)
            dve.wait_ge(s("rqk_root"), 1)
            nc.vector.reciprocal(rq, rq)
            link(nc.vector.reciprocal(rk, rk))
            dve.wait_ge(s("beta_ready"), 1)
            link(nc.vector.tensor_scalar(rq, rq, float(P) ** -0.5, None, ALU.mult))
            nc.vector.tensor_tensor(rb, rk, beta, ALU.mult).then_inc(s("rb_ready"), 1)
            dve.wait_ge(s("rb_ready"), 1)
            dve.wait_ge(s("g_spread"), NG)
            for q in range(NG):
                for j in range(GRP):
                    h, tt = 2 * q + j // 2, j % 2
                    last = nc.vector.tensor_tensor(gl[:, tt, h:h + 1], ps[q][:, (j + 1) * P - 1:(j + 1) * P], gc[:, tt, h:h + 1], ALU.subtract)
            link(last)
            dve.sem_inc(s("gl_in"), 1)
            for q in range(NG):
                for j in range(GRP):
                    h, tt = 2 * q + j // 2, j % 2
                    last = nc.vector.tensor_scalar(dec[:, h, tt], ps[q][:, j * P:(j + 1) * P], gc[:, tt, h:h + 1], 0.0, ALU.subtract, ALU.min)
                last.then_inc(s("dec_in"), 1)
            dve.wait_ge(s("gl_exp"), 1)
            nc.vector.tensor_tensor(kb_s, kb_s, rb, ALU.mult)
            link(nc.vector.tensor_tensor(kd_s, gl, rk, ALU.mult))
            dve.sem_inc(s("kb_ready"), 1)
            for q in range(NG):
                dve.wait_ge(s("dec_ready"), q + 1)
                dve.sem_inc(s("g_used"), 1)
                dve.wait_ge(s("kk_done"), q + 1)
                for j in range(GRP):
                    h, tt = 2 * q + j // 2, j % 2
                    last = nc.vector.scalar_tensor_tensor(aT[:, h, tt], ps[4][:, j * P:(j + 1) * P], rk[:, tt, h:h + 1], dec[:, h, tt], ALU.mult, ALU.mult)
                link(last)
                link(nc.vector.tensor_tensor(grp(aT, q), grp(aT, q), ps[5][:, :].rearrange("p (a c) -> p a c", a=GRP), ALU.mult))
                dve.sem_inc(s("aT_ready"), 1)
                dve.sem_inc(s("kk_used"), 1)
                dve.wait_ge(s("kq_done"), q + 1)
                for j in range(GRP):
                    h, tt = 2 * q + j // 2, j % 2
                    last = nc.vector.scalar_tensor_tensor(attn[:, h, tt], ps[6][:, j * P:(j + 1) * P], rk[:, tt, h:h + 1], dec[:, h, tt], ALU.mult, ALU.mult)
                link(last)
                dve.sem_inc(s("kq_used"), 1)
                last = nc.vector.tensor_tensor(grp(attn, q), grp(attn, q), tri.unsqueeze(1).broadcast_to([P, GRP, P]), ALU.mult)
            link(last)
            for v in range(len(LEVELS)):
                for q in range(NG):
                    idb = ident.unsqueeze(1).broadcast_to([P, GRP, P])
                    if v == 0:
                        dve.wait_ge(s("x_done"), q + 1)
                        nc.vector.tensor_tensor(grp(Um, q), idb, grp(BT, q), ALU.subtract)
                        nc.vector.tensor_tensor(grp(Tm, q), idb, ps[q][:, :].rearrange("p (a c) -> p a c", a=GRP), ALU.subtract).then_inc(s("inv_ready"), 1)
                    else:
                        dve.wait_ge(s("y_done"), (v - 1) * NG + q + 1)
                        if v < len(LEVELS) - 1:
                            nc.vector.tensor_tensor(grp(Tm, q), grp(Tm, q), ps[5 + 2 * (q % 2)][:, :].rearrange("p (a c) -> p a c", a=GRP), ALU.subtract)
                        nc.vector.tensor_tensor(grp(Um, q), grp(Um, q), ps[4 + 2 * (q % 2)][:, :].rearrange("p (a c) -> p a c", a=GRP), ALU.subtract).then_inc(s("inv_ready"), 1)
                if v == 0:
                    nc.vector.tensor_tensor(qdec, qkv[:, 0:LH, P:2 * P], eg, ALU.mult).then_inc(s("qdec_ready"), 1)
            dve.wait_ge(s("u_kept"), NG)
            for hh in range(2):
                dve.wait_ge(s("wS_done"), hh + 1)
                sl = u_[:, 4 * hh:4 * hh + 4, 1]
                nc.vector.tensor_tensor(sl, sl, ps[4 + hh][:, :].rearrange("p (a c) -> p a c", a=4), ALU.subtract).then_inc(s("vnew"), 1)
            dve.wait_ge(s("sum_o"), 1)
            link(nc.vector.tensor_tensor(ms, ps[4][:, 0:16].rearrange("p (t h) -> p t h", t=NT), rq, ALU.mult))
            link(nc.vector.scalar_tensor_tensor(ms, ms, 1.0 / P, rq, ALU.mult, ALU.mult))
            dve.sem_inc(s("ms_in"), 1)
            dve.wait_ge(s("o_root"), 1)
            link(nc.vector.reciprocal(ms, ms))
            nc.vector.tensor_tensor(ms, ms, rq, ALU.mult).then_inc(s("o_rstd"), 1)
            link(nc.vector.tensor_tensor(zs, zs, oT, ALU.mult))
            for q in range(NG):
                dve.wait_ge(s("o_spread"), q + 1)
                last = nc.vector.scalar_tensor_tensor(flat(oT[:, 2 * q:2 * q + 2]), flat(zs[:, 2 * q:2 * q + 2]), par[:, Q_ONORM:Q_ONORM + 1],
                                                      ps[q][:, :], ALU.mult, ALU.mult)
            last.then_inc(s("y_ready"), 1)
            for mm in range(KD):
                dve.wait_ge(s("used"), NQ + mm + 1)
                nc.vector.scalar_tensor_tensor(xT[:, mm], ps[4 + mm % 4][:, 0:T], cd[:, 2 * KD + mm:2 * KD + mm + 1], xT[:, mm],
                                               ALU.mult, ALU.add).then_inc(s("x_added"), 1)
            dve.wait_ge(s("root_f"), 1)
            link(nc.vector.reciprocal(rms, rms))
            for k in range(KD):
                nc.vector.scalar_tensor_tensor(xn[:, k], xT[:, k], par[:, Q_FINAL + k:Q_FINAL + k + 1], rms,
                                               ALU.mult, ALU.mult).then_inc(s("scaled"), 1)


def build(nc, a, out):
    ctx = ExitStack()
    with ctx:
        def sb(name, size, dt=F32):
            return ctx.enter_context(nc.sbuf_tensor(name, [P, size], dt))

        m = {"big": sb("big", NK * T), "wring_": sb("weight_ring", WSLOTS * WSIZE + P * 2), "const": sb("constants", NKEEP),
             "work": sb("work", 4 * T), "xT_": sb("x_t", KD * T), "zeros": sb("zeros", P, BF16)}
        m["wring"] = m["wring_"][:, 0:WSLOTS * WSIZE].rearrange("p (s c) -> p s c", s=WSLOTS)
        m["xr"] = sb("x_parts", 2 * KD * T, F32R)[:, :].rearrange("p (a k t) -> p a k t", a=2, k=KD)
        m["wr"] = sb("weight_parts", 2 * 2 * T, F32R)[:, :].rearrange("p (a n t) -> p a n t", a=2, n=2)
        m["split"] = sb("chunk_parts", SPLITS * 2 * D, F32R)[:, :].rearrange("p (s a c) -> p s a c", s=SPLITS, a=2)
        m["xT"] = m["xT_"][:, :].rearrange("p (k t) -> p k t", k=KD)
        m["cond"] = m["const"][:, K_COND:K_COND + 2 * NCOND].rearrange("p (l c) -> p l c", l=2)
        m["ring2"] = [m["wring_"][:, i * D:(i + 1) * D] for i in range(R2)]
        m["par2"] = m["work"][:, 0:NPAR2]
        m["small2"] = m["work"][:, 256:256 + 272]
        m["wab"] = m["work"][:, 640:640 + KD * 2 * LH].rearrange("p (k c) -> p k c", k=KD)
        m["ps"] = [ctx.enter_context(nc.psum_tensor(f"bank{i}", [P, 512], F32)) for i in range(8)]
        loaded = ctx.enter_context(nc.semaphore("start_loaded"))
        with nc.Block() as block:
            @block.sync
            def _(sp):
                sp.dma_start(m["xT"], a["x"]).then_inc(loaded, 16)
                sp.dma_start(m["const"][:, 0:NCONST], a["const"]).then_inc(loaded, 16)
                sp.wait_ge(loaded, 32)
        with ExitStack() as part:
            first_block(nc, part, m, [a[k] for k in ("w_in", "w_kv", "w_out", "wq", "sub", "par", "xc", "mem", "experts", "ada", "c")])
        with ExitStack() as part:
            lru_layer(nc, part, m, a["lru_in"], a["lru_gate"], a["lru_out"], a["par2"])
        with ExitStack() as part:
            gdn_layer(nc, part, m, a["gdn_in"], a["gdn_ab"], a["gdn_out"], a["mask"], out)


def columns(w):
    *lead, k, n = w.shape
    v = w.reshape(*lead, k // P, P, n // P, P)
    v = np.moveaxis(v, -2, -4)
    v = np.swapaxes(v, -3, -2)
    return np.ascontiguousarray(v).reshape(*lead, n // P, P, k // P * P)


def per_channel(v):
    return np.swapaxes(v.reshape(v.shape[0], -1, P), 1, 2)


def constants():
    c = np.zeros((P, NCONST), np.float32)
    c[:, K_ONES:K_ONES + P] = 1.0
    c[:, K_IDENT:K_IDENT + P] = np.eye(P)
    c[:, K_IOTA:K_IOTA + P] = np.arange(P)
    c[np.arange(P), K_BD32 + np.arange(P) // DH] = 1.0
    c[np.arange(P), K_BD64 + np.arange(P) // MH] = 1.0
    c[:, K_EPS] = EPS
    x = np.zeros((P, NXC), np.float32)
    t = np.arange(T)
    for g, w in enumerate(POOL_WINDOWS):
        n = np.clip(t + w // 2, 0, T) - np.clip(t - w // 2, 0, T)
        rows = slice(64 * (g % 2), 64 * (g % 2 + 1))
        x[rows, X_INV + (g // 2) * T:X_INV + (g // 2 + 1) * T] = 1.0 / n
    for q in range(NT):
        x[:, X_DIST + q * T:X_DIST + (q + 1) * T] = np.abs((q * P + np.arange(P))[:, None] - t[None])
    return c, x


def layout(i):
    L = LAYERS
    f = {k: np.asarray(v) for k, v in i.items()}
    a = {}
    a["x"] = np.ascontiguousarray(f["x"][0].T.reshape(KD, P, T).transpose(1, 0, 2))
    a["mem"] = np.ascontiguousarray(f["mem"][0].T.reshape(KD, P, T).transpose(1, 0, 2))
    a["const"], a["xc"] = constants()
    a["w_in"] = columns(f["w_in"])
    a["w_kv"] = columns(f["w_mem_kv"])
    a["w_out"] = columns(f["w_out"])
    a["wq"] = columns(f["peer_wq"])
    sub = f["peer_subkeys"].reshape(L, 2, 8, NK, P).transpose(0, 1, 4, 2, 3)
    a["sub"] = np.ascontiguousarray(sub).reshape(L, 2, P, 8 * NK)
    u = f["peer_u"].reshape(L, NK, NK, KD, P).transpose(0, 2, 4, 3, 1).reshape(L, NK, P, D)
    v = f["peer_v"].reshape(L, NK, NK, D).transpose(0, 2, 1, 3)
    e = np.empty((L, NE, P, D), np.float32)
    e[:, 0], e[:, 1:NE - 1:2] = u[:, 0], u[:, 1:]
    e[:, 2:NE:2], e[:, NE - 1] = v[:, 0:NK - 1], v[:, NK - 1]
    a["experts"] = e
    p = np.zeros((L, P, NPAR), np.float32)
    p[:, :, C_NMIX:C_NMIX + KD] = per_channel(f["norm_mix"])
    p[:, :, C_NMEM:C_NMEM + KD] = per_channel(f["mem_norm"])
    p[:, :, C_NFFN:C_NFFN + KD] = per_channel(f["norm_ffn"])
    p[:, :, C_GROUP:C_GROUP + KMIX] = per_channel(f["group_norm"])
    for name, at, taps in (("conv_dw", C_CONV, TAPS), ("sconv_w", C_SCONV, SHORT)):
        w = f[name].transpose(0, 2, 1).reshape(L, GT, P, taps).transpose(0, 2, 1, 3)
        p[:, :, at:at + GT * taps] = w.reshape(L, P, GT * taps)
    p[:, :, C_LNG:C_LNG + GT] = per_channel(f["conv_ln_g"])
    p[:, :, C_LNB:C_LNB + GT] = per_channel(f["conv_ln_b"])
    for j in range(2):
        p[:, :, C_QG + j] = np.tile(f["diff_qk_norm"][:, j], (1, P // DH))
        p[:, :, C_QG + 2 + j] = np.tile(f["mem_qk_norm"][:, j], (1, P // MH))
    p[:, :, C_PSCALE:C_PSCALE + GT] = per_channel(f["pool_scale"])
    p[:, :, C_SUBLN] = np.tile(f["diff_subln"], (1, P // MH))
    for l in range(L):
        start = 0.8 - 0.6 * np.exp(-0.3 * l)
        p[l, :, C_LINIT] = start
        p[l, :, C_LINIT + 1] = 1.0 - start
    p[:, :, C_LAM:C_LAM + 4 * DH] = f["diff_lambda"].reshape(L, 1, 4 * DH)
    for g in range(4):
        rows = slice(64 * (g % 2), 64 * (g % 2 + 1))
        at = C_POOLW + (g // 2) * P + 64 * (g % 2)
        p[:, rows, at:at + 64] = f["pool_w"][:, g]
    p[:, :, C_PW:C_PW + GT * GW] = f["conv_pw"].reshape(L, GT, P, GW).transpose(0, 2, 1, 3).reshape(L, P, GT * GW)
    a["par"] = p
    a["c"] = np.tile(f["c_2"].reshape(1, D), (P, 1))
    a["ada"] = np.ascontiguousarray(f["ada_w_2"].swapaxes(1, 2)).reshape(2, NCOND, P, D)
    a["lru_in"] = columns(f["lru_in_w_2"][0])
    a["lru_out"] = columns(f["lru_out_w_2"][0])
    a["lru_gate"] = np.ascontiguousarray(f["lru_gate_w_2"][0].transpose(0, 2, 1, 3)).reshape(2, P, LH * P)
    gin = f["gdn_in_w_2"][0]
    a["gdn_in"] = columns(np.ascontiguousarray(gin[:, 0:4 * D]))
    a["gdn_ab"] = np.ascontiguousarray(gin[:, 4 * D:].reshape(KD, P, 2 * LH).transpose(1, 0, 2)).reshape(P, KD * 2 * LH)
    a["gdn_out"] = columns(f["gdn_out_w_2"][0])
    q = np.zeros((P, NPAR2), np.float32)
    for l in range(2):
        q[:, Q_NORM + l * KD:Q_NORM + (l + 1) * KD] = f["norm_g_2"][l].reshape(KD, P).T
        q[:, Q_ADAB + l * 3 * KD:Q_ADAB + (l + 1) * 3 * KD] = f["ada_b_2"][l].reshape(3 * KD, P).T
    q[:, Q_FINAL:Q_FINAL + KD] = f["final_g_2"].reshape(KD, P).T
    q[:, Q_LCW:Q_LCW + LH * CTAPS] = f["lru_conv_w_2"][0].reshape(CTAPS, LH, P).transpose(2, 1, 0).reshape(P, LH * CTAPS)
    q[:, Q_LCB:Q_LCB + LH] = f["lru_conv_b_2"][0].reshape(LH, P).T
    q[:, Q_LGB:Q_LGB + 2 * LH] = f["lru_gate_b_2"][0].reshape(2 * LH, P).T
    q[:, Q_LAM:Q_LAM + LH] = f["lru_lambda_2"][0].reshape(LH, P).T
    q[:, Q_GCW:Q_GCW + 3 * LH * CTAPS] = f["gdn_conv_w_2"][0].reshape(CTAPS, 3 * LH, P).transpose(2, 1, 0).reshape(P, 3 * LH * CTAPS)
    q[:, Q_ONORM] = f["gdn_onorm_g_2"][0]
    q[:, Q_ALOG:Q_ALOG + LH] = f["gdn_a_log_2"][0]
    q[:, Q_DT:Q_DT + LH] = f["gdn_dt_bias_2"][0]
    a["par2"] = q
    mask = np.zeros((P, NMASK), np.float32)
    j, i = np.arange(P)[:, None], np.arange(P)[None]
    mask[:, M_TRI:M_TRI + P] = j <= i
    for v, lv in enumerate(LEVELS):
        block = (i // (2 * lv) == j // (2 * lv)) & ((i // lv) % 2 == 1) & ((j // lv) % 2 == 0)
        mask[:, M_LEVEL + v * P:M_LEVEL + (v + 1) * P] = block
    a["mask"] = mask
    return a


def kernel(**inputs):
    import concourse.bacc as bacc
    from concourse.bass_utils import run_bass_kernel_spmd

    arrays = layout(inputs)
    nc = bacc.Bacc("TRN2", target_bir_lowering=False, num_devices=1)
    dram = {k: nc.dram_tensor(f"in_{k}", v.shape, mybir.dt.from_np(v.dtype), kind="ExternalInput").ap() for k, v in arrays.items()}
    out = nc.dram_tensor("out", (P, KD, T), F32, kind="ExternalOutput").ap()
    build(nc, dram, out)
    r = run_bass_kernel_spmd(nc, [{f"in_{k}": v for k, v in arrays.items()}], core_ids=[0])
    y = np.asarray(r.results[0]["out"])
    return np.ascontiguousarray(y.transpose(2, 1, 0)).reshape(1, T, D)
```
